# Optimizing a Trainium2 kernel written in Bass

```python
import math
import jax, jax.numpy as jnp
from jax import lax
import numpy as np

D_MODEL = 1024
BATCH = 1
SEQ = 256
DEPTH = 1

HEAD_DIM = 128
N_HEADS_MOBA = 8
N_HEADS_GDN = 8
MOBA_WIDTH = N_HEADS_MOBA * HEAD_DIM
GDN_WIDTH = N_HEADS_GDN * HEAD_DIM
MOBA_BLOCK = 256
MOBA_TOPK = 3
MOBA_Q_CHUNK = 32
GDN_CHUNK = 64
CONV_WIDTH = 4
ROPE_THETA = 10000.0
D_FF = -(-8 * D_MODEL // (3 * 256)) * 256
PLE_DIM = 256
EPS = 1e-6

IN_SIZES = (MOBA_WIDTH, MOBA_WIDTH, MOBA_WIDTH, 3 * GDN_WIDTH, GDN_WIDTH,
            N_HEADS_GDN, N_HEADS_GDN, D_MODEL, D_MODEL)
IN_SPLITS = tuple(int(s) for s in np.cumsum(IN_SIZES)[:-1])
IN_WIDTH = int(sum(IN_SIZES))


def rms_norm(x, w):
    xf = x.astype(jnp.float32)
    y = xf * lax.rsqrt(jnp.mean(xf * xf, axis=-1, keepdims=True) + EPS)
    return (y * w.astype(jnp.float32)).astype(x.dtype)

def l2_norm(x):
    xf = x.astype(jnp.float32)
    return xf * lax.rsqrt(jnp.sum(xf * xf, axis=-1, keepdims=True) + EPS)

def rope_tables(seq):
    inv = 1.0 / (ROPE_THETA ** (jnp.arange(0, HEAD_DIM, 2, dtype=jnp.float32) / HEAD_DIM))
    ang = jnp.arange(seq, dtype=jnp.float32)[:, None] * inv[None, :]
    return jnp.cos(ang), jnp.sin(ang)

def apply_rope(x, cos, sin):
    x1, x2 = jnp.split(x.astype(jnp.float32), 2, axis=-1)
    out = jnp.concatenate([x1 * cos - x2 * sin, x2 * cos + x1 * sin], axis=-1)
    return out.astype(x.dtype)

def causal_depthwise_conv(x, w):
    c = x.shape[-1]
    return lax.conv_general_dilated(
        x, w[:, None, :].astype(x.dtype), window_strides=(1,),
        padding=[(CONV_WIDTH - 1, 0)], dimension_numbers=("NWC", "WIO", "NWC"),
        feature_group_count=c)

def moba_attention(q, k, v):
    b, h, s, hd = q.shape
    nb = -(-s // MOBA_BLOCK)
    pad = nb * MOBA_BLOCK - s
    n_sel = min(MOBA_TOPK, nb)
    scale = hd ** -0.5
    k_blocks = jnp.pad(k, ((0, 0), (0, 0), (0, pad), (0, 0))).reshape(b, h, nb, MOBA_BLOCK, hd)
    v_blocks = jnp.pad(v, ((0, 0), (0, 0), (0, pad), (0, 0))).reshape(b, h, nb, MOBA_BLOCK, hd)
    k_mean = jnp.mean(k_blocks.astype(jnp.float32), axis=3)
    blk_ids = jnp.arange(nb)
    n_chunks = s // MOBA_Q_CHUNK

    def one_chunk(c):
        start = c * MOBA_Q_CHUNK
        q_c = lax.dynamic_slice_in_dim(q, start, MOBA_Q_CHUNK, axis=2)
        q_blk = start // MOBA_BLOCK
        gate = jnp.einsum("bhcd,bhnd->bhcn", q_c.astype(jnp.float32), k_mean)
        gate = jnp.where(blk_ids < q_blk, gate, -jnp.inf)
        _, sel = lax.top_k(gate, n_sel)
        sel_valid = sel < q_blk
        idx = sel.reshape(b, h, MOBA_Q_CHUNK * n_sel, 1, 1)
        k_sel = jnp.take_along_axis(k_blocks, idx, axis=2).reshape(
            b, h, MOBA_Q_CHUNK, n_sel, MOBA_BLOCK, hd)
        v_sel = jnp.take_along_axis(v_blocks, idx, axis=2).reshape(
            b, h, MOBA_Q_CHUNK, n_sel, MOBA_BLOCK, hd)
        s_past = jnp.einsum("bhcd,bhcknd->bhckn", q_c, k_sel).astype(jnp.float32) * scale
        s_past = jnp.where(sel_valid[..., None], s_past, -jnp.inf)
        s_past = s_past.reshape(b, h, MOBA_Q_CHUNK, n_sel * MOBA_BLOCK)
        k_own = lax.dynamic_index_in_dim(k_blocks, q_blk, axis=2, keepdims=False)
        v_own = lax.dynamic_index_in_dim(v_blocks, q_blk, axis=2, keepdims=False)
        s_own = jnp.einsum("bhcd,bhnd->bhcn", q_c, k_own).astype(jnp.float32) * scale
        q_pos = start + jnp.arange(MOBA_Q_CHUNK)
        k_pos = q_blk * MOBA_BLOCK + jnp.arange(MOBA_BLOCK)
        s_own = jnp.where(k_pos[None, :] <= q_pos[:, None], s_own, -jnp.inf)
        probs = jax.nn.softmax(jnp.concatenate([s_past, s_own], axis=-1), axis=-1)
        p_past = probs[..., : n_sel * MOBA_BLOCK].reshape(
            b, h, MOBA_Q_CHUNK, n_sel, MOBA_BLOCK).astype(v.dtype)
        p_own = probs[..., n_sel * MOBA_BLOCK:].astype(v.dtype)
        return (jnp.einsum("bhckn,bhcknd->bhcd", p_past, v_sel)
                + jnp.einsum("bhcn,bhnd->bhcd", p_own, v_own))

    out = lax.map(one_chunk, jnp.arange(n_chunks))
    return out.transpose(1, 2, 0, 3, 4).reshape(b, h, s, hd)

def gated_delta_rule(q, k, v, g, beta):
    b, h, s, dk = q.shape
    dv = v.shape[-1]
    L = GDN_CHUNK
    nc = s // L
    f32 = jnp.float32
    q = q.astype(f32) * (dk ** -0.5)
    k = k.astype(f32)
    v = v.astype(f32)
    q = q.reshape(b, h, nc, L, dk)
    k = k.reshape(b, h, nc, L, dk)
    v = v.reshape(b, h, nc, L, dv)
    g = g.astype(f32).reshape(b, h, nc, L)
    beta = beta.astype(f32).reshape(b, h, nc, L)
    gc = jnp.cumsum(g, axis=-1)
    causal = jnp.tril(jnp.ones((L, L), dtype=bool))
    strict = jnp.tril(jnp.ones((L, L), dtype=bool), k=-1)
    decay = jnp.exp(jnp.where(causal, gc[..., :, None] - gc[..., None, :], -jnp.inf))
    k_beta = k * beta[..., None]
    a_low = jnp.where(strict, jnp.einsum("bhnid,bhnjd->bhnij", k_beta, k) * decay, 0.0)
    t_mat = a_low + jnp.eye(L, dtype=f32)
    rhs = jnp.concatenate([v * beta[..., None], k_beta * jnp.exp(gc)[..., None]], axis=-1)
    sol = lax.linalg.triangular_solve(t_mat, rhs, left_side=True, lower=True, unit_diagonal=True)
    u = sol[..., :dv]
    w = sol[..., dv:]
    attn = jnp.where(causal, jnp.einsum("bhnid,bhnjd->bhnij", q, k) * decay, 0.0)

    def step(state, inp):
        q_i, k_i, u_i, w_i, g_i, a_i = inp
        v_new = u_i - jnp.einsum("bhld,bhde->bhle", w_i, state)
        o = (jnp.einsum("bhld,bhde->bhle", q_i * jnp.exp(g_i)[..., None], state)
             + jnp.einsum("bhlm,bhme->bhle", a_i, v_new))
        g_last = g_i[..., -1]
        state = (state * jnp.exp(g_last)[..., None, None]
                 + jnp.einsum("bhld,bhle->bhde", k_i * jnp.exp(g_last[..., None] - g_i)[..., None], v_new))
        return state, o

    xs = tuple(jnp.moveaxis(t, 2, 0) for t in (q, k, u, w, gc, attn))
    state0 = jnp.zeros((b, h, dk, dv), dtype=f32)
    _, o = lax.scan(step, state0, xs)
    return jnp.moveaxis(o, 0, 2).reshape(b, h, s, dv)

def first_inputs(seed: int = 0) -> dict:
    key = jax.random.key(seed)
    ks = jax.random.split(key, 24)
    f32 = jnp.float32

    def nrm(k, shape, scale):
        return jax.random.normal(k, shape, f32) * scale

    def gain(k, n):
        return 1.0 + 0.1 * jax.random.normal(k, (DEPTH, n), f32)

    dt = jnp.exp(jax.random.uniform(ks[7], (DEPTH, N_HEADS_GDN), f32,
                                    math.log(1e-3), math.log(1e-1)))
    return {
        "x": nrm(ks[0], (BATCH, SEQ, D_MODEL), 1.0),
        "p": nrm(ks[1], (DEPTH, BATCH, SEQ, PLE_DIM), 1.0),
        "ln_pre_mix": gain(ks[2], D_MODEL),
        "w_in": nrm(ks[3], (DEPTH, D_MODEL, IN_WIDTH), D_MODEL ** -0.5),
        "conv_w": nrm(ks[4], (DEPTH, CONV_WIDTH, 3 * GDN_WIDTH), CONV_WIDTH ** -0.5),
        "a_log": jnp.log(jax.random.uniform(ks[5], (DEPTH, N_HEADS_GDN), f32, 1.0, 16.0)),
        "dt_bias": jnp.log(jnp.expm1(dt)),
        "gdn_norm": gain(ks[6], HEAD_DIM),
        "w_proj_a": nrm(ks[8], (DEPTH, MOBA_WIDTH, D_MODEL), MOBA_WIDTH ** -0.5),
        "w_proj_b": nrm(ks[9], (DEPTH, GDN_WIDTH, D_MODEL), GDN_WIDTH ** -0.5),
        "w_out": nrm(ks[10], (DEPTH, D_MODEL, D_MODEL), D_MODEL ** -0.5),
        "ln_post_mix": gain(ks[11], D_MODEL),
        "ln_pre_ffn": gain(ks[12], D_MODEL),
        "w_ffn_gate": nrm(ks[13], (DEPTH, D_MODEL, D_FF), D_MODEL ** -0.5),
        "w_ffn_up": nrm(ks[14], (DEPTH, D_MODEL, D_FF), D_MODEL ** -0.5),
        "w_ffn_down": nrm(ks[15], (DEPTH, D_FF, D_MODEL), D_FF ** -0.5),
        "ln_post_ffn": gain(ks[16], D_MODEL),
        "w_ple": nrm(ks[17], (DEPTH, PLE_DIM, D_MODEL), PLE_DIM ** -0.5),
        "ln_ple": gain(ks[18], D_MODEL),
        "w_ple_gate": nrm(ks[19], (DEPTH, D_MODEL, D_MODEL), D_MODEL ** -0.5),
    }

def first_block(x, p, ln_pre_mix, w_in, conv_w, a_log, dt_bias, gdn_norm, w_proj_a, w_proj_b,
              w_out, ln_post_mix, ln_pre_ffn, w_ffn_gate, w_ffn_up, w_ffn_down, ln_post_ffn,
              w_ple, ln_ple, w_ple_gate):
    b, s, _ = x.shape
    cos, sin = rope_tables(s)

    def to_heads(t, n):
        return t.reshape(b, s, n, HEAD_DIM).transpose(0, 2, 1, 3)

    def from_heads(t):
        return t.transpose(0, 2, 1, 3).reshape(b, s, -1)

    h = x
    for i in range(DEPTH):
        u = rms_norm(h, ln_pre_mix[i])
        proj = u @ w_in[i]
        q_a, k_a, v_a, qkv_b, z_b, b_b, a_b, gate_a, gate_b = jnp.split(proj, IN_SPLITS, axis=-1)

        qa = apply_rope(to_heads(q_a, N_HEADS_MOBA), cos, sin)
        ka = apply_rope(to_heads(k_a, N_HEADS_MOBA), cos, sin)
        va = to_heads(v_a, N_HEADS_MOBA)
        y_a = from_heads(moba_attention(qa, ka, va))

        qkv_b = jax.nn.silu(causal_depthwise_conv(qkv_b, conv_w[i]))
        q_b, k_b, v_b = jnp.split(qkv_b, 3, axis=-1)
        qb = l2_norm(to_heads(q_b, N_HEADS_GDN))
        kb = l2_norm(to_heads(k_b, N_HEADS_GDN))
        vb = to_heads(v_b, N_HEADS_GDN)
        g_log = -jnp.exp(a_log[i].astype(jnp.float32)) * jax.nn.softplus(
            a_b.astype(jnp.float32) + dt_bias[i].astype(jnp.float32))
        beta = jax.nn.sigmoid(b_b.astype(jnp.float32))
        o_b = gated_delta_rule(qb, kb, vb, g_log.transpose(0, 2, 1), beta.transpose(0, 2, 1))
        o_b = o_b.transpose(0, 2, 1, 3).astype(h.dtype)
        z = z_b.reshape(b, s, N_HEADS_GDN, HEAD_DIM)
        y_b = (rms_norm(o_b, gdn_norm[i]) * jax.nn.silu(z)).reshape(b, s, GDN_WIDTH)

        merged = (jax.nn.sigmoid(gate_a) * (y_a @ w_proj_a[i])
                  + jax.nn.sigmoid(gate_b) * (y_b @ w_proj_b[i]))
        h = h + rms_norm(merged @ w_out[i], ln_post_mix[i])

        f = rms_norm(h, ln_pre_ffn[i])
        f = (jax.nn.silu(f @ w_ffn_gate[i]) * (f @ w_ffn_up[i])) @ w_ffn_down[i]
        h = h + rms_norm(f, ln_post_ffn[i])

        e = rms_norm(p[i].astype(h.dtype) @ w_ple[i], ln_ple[i])
        h = h + jax.nn.sigmoid(h @ w_ple_gate[i]) * e
    return h


MEM_LEN = 256
DA_HEADS = 4
DA_QK_DIM = 64
DA_V_DIM = 2 * DA_QK_DIM
DA_WIDTH = DA_HEADS * DA_V_DIM
QK_WIDTH = DA_HEADS * 2 * DA_QK_DIM
POOL_WINDOWS = (2, 4, 8, 16)
POOL_GROUPS = len(POOL_WINDOWS)
POOL_WIDTH = D_MODEL - DA_WIDTH
POOL_GROUP_DIM = POOL_WIDTH // POOL_GROUPS
MIX_WIDTH = DA_WIDTH + POOL_WIDTH
IN_WIDTH_2 = 2 * QK_WIDTH + DA_WIDTH + POOL_WIDTH
ROPE_THETA_2 = 500000.0
ROPE_DIM = DA_QK_DIM // 4
BLOCK_Q = 128
X_HEADS = 4
X_HEAD_DIM = D_MODEL // X_HEADS
D_FF_2 = -(-(8 * D_MODEL) // (3 * 256)) * 256
def _lambda_init(layer_idx):
    return 0.8 - 0.6 * math.exp(-0.3 * (layer_idx - 1))


def rmsnorm(x, g):
    xf = x.astype(jnp.float32)
    y = xf * lax.rsqrt(jnp.mean(xf * xf, axis=-1, keepdims=True) + EPS)
    return (y * g.astype(jnp.float32)).astype(x.dtype)

def rope_tables_2(positions, dtype):
    inv_freq = ROPE_THETA_2 ** (-jnp.arange(0, ROPE_DIM, 2, dtype=jnp.float32) / ROPE_DIM)
    ang = positions.astype(jnp.float32)[..., None] * inv_freq
    return jnp.cos(ang).astype(dtype), jnp.sin(ang).astype(dtype)

def apply_partial_rope(t, cos, sin):
    cos = cos[:, :, None, None, :]
    sin = sin[:, :, None, None, :]
    half = ROPE_DIM // 2
    t1 = t[..., :half]
    t2 = t[..., half:ROPE_DIM]
    rest = t[..., ROPE_DIM:]
    return jnp.concatenate([t1 * cos - t2 * sin, t2 * cos + t1 * sin, rest], axis=-1)

def diff_attention(q, k, v, lam):
    seq = q.shape[3]
    scale = DA_QK_DIM ** -0.5
    outs = []
    for i in range(seq // BLOCK_Q):
        q0 = i * BLOCK_Q
        kend = q0 + BLOCK_Q
        qb = q[:, :, :, q0:kend]
        kb = k[:, :, :, :kend]
        vb = v[:, :, :kend]
        s = jnp.einsum('bhmqd,bhmkd->bhmqk', qb, kb).astype(jnp.float32) * scale
        mask = (q0 + jnp.arange(BLOCK_Q))[:, None] >= jnp.arange(kend)[None, :]
        s = jnp.where(mask, s, -jnp.inf)
        p = jax.nn.softmax(s, axis=-1)
        a = p[:, :, 0] - lam * p[:, :, 1]
        outs.append(jnp.einsum('bhqk,bhkd->bhqd', a.astype(v.dtype), vb))
    return jnp.concatenate(outs, axis=2)

def causal_multiscale_pool(u):
    b, s, _ = u.shape
    uf = u.astype(jnp.float32).reshape(b, s, POOL_GROUPS, POOL_GROUP_DIM)
    c = jnp.cumsum(uf, axis=1)
    t1 = jnp.arange(1, s + 1, dtype=jnp.float32)
    groups = []
    for g, w in enumerate(POOL_WINDOWS):
        cg = c[:, :, g]
        shifted = jnp.pad(cg, ((0, 0), (w, 0), (0, 0)))[:, :s]
        count = jnp.minimum(t1, float(w))[None, :, None]
        groups.append((cg - shifted) / count - uf[:, :, g])
    return jnp.stack(groups, axis=2).astype(u.dtype)

def second_inputs(seed: int = 0) -> dict:
    key = jax.random.key(seed)
    ks = jax.random.split(key, 32)
    f32 = jnp.float32

    def w(k, shape, fan_in):
        return jax.random.normal(k, shape, f32) * (fan_in ** -0.5)

    def gain(k, n):
        return 1.0 + 0.02 * jax.random.normal(k, (n,), f32)

    return {
        "x": jax.random.normal(ks[0], (BATCH, SEQ, D_MODEL), f32),
        "mem": jax.random.normal(ks[1], (BATCH, MEM_LEN, D_MODEL), f32),
        "positions": jnp.broadcast_to(jnp.arange(SEQ, dtype=jnp.int32), (BATCH, SEQ)),
        "g_mix_pre": gain(ks[2], D_MODEL),
        "w_in": w(ks[3], (D_MODEL, IN_WIDTH_2), D_MODEL),
        "lambda_q1": 0.1 * jax.random.normal(ks[4], (DA_QK_DIM,), f32),
        "lambda_k1": 0.1 * jax.random.normal(ks[5], (DA_QK_DIM,), f32),
        "lambda_q2": 0.1 * jax.random.normal(ks[6], (DA_QK_DIM,), f32),
        "lambda_k2": 0.1 * jax.random.normal(ks[7], (DA_QK_DIM,), f32),
        "g_subln": gain(ks[8], DA_V_DIM),
        "w_pool": w(ks[9], (POOL_GROUPS, POOL_GROUP_DIM, POOL_GROUP_DIM), POOL_GROUP_DIM),
        "pool_scale": 1.0 + 0.1 * jax.random.normal(ks[10], (POOL_WIDTH,), f32),
        "w_out": w(ks[11], (MIX_WIDTH, D_MODEL), MIX_WIDTH),
        "g_mix_post": gain(ks[12], D_MODEL),
        "g_x_pre": gain(ks[13], D_MODEL),
        "g_mem": gain(ks[14], D_MODEL),
        "w_xq": w(ks[15], (D_MODEL, X_HEADS * X_HEAD_DIM), D_MODEL),
        "w_xkv": w(ks[16], (D_MODEL, 2 * X_HEADS * X_HEAD_DIM), D_MODEL),
        "w_xo": w(ks[17], (X_HEADS * X_HEAD_DIM, D_MODEL), X_HEADS * X_HEAD_DIM),
        "g_x_post": gain(ks[18], D_MODEL),
        "g_ffn_pre": gain(ks[19], D_MODEL),
        "w_gate": w(ks[20], (D_MODEL, D_FF_2), D_MODEL),
        "w_up": w(ks[21], (D_MODEL, D_FF_2), D_MODEL),
        "w_down": w(ks[22], (D_FF_2, D_MODEL), D_FF_2),
        "g_ffn_post": gain(ks[23], D_MODEL),
    }

def second_block(x, mem, positions, g_mix_pre, w_in, lambda_q1, lambda_k1, lambda_q2,
              lambda_k2, g_subln, w_pool, pool_scale, w_out, g_mix_post, g_x_pre,
              g_mem, w_xq, w_xkv, w_xo, g_x_post, g_ffn_pre, w_gate, w_up, w_down,
              g_ffn_post):
    b, s, _ = x.shape
    cos, sin = rope_tables_2(positions, x.dtype)
    mem_n = rmsnorm(mem, g_mem)

    for layer in range(DEPTH):
        lam_init = _lambda_init(layer + 1)

        h = rmsnorm(x, g_mix_pre)
        proj = h @ w_in
        q = proj[..., :QK_WIDTH].reshape(b, s, DA_HEADS, 2, DA_QK_DIM)
        k = proj[..., QK_WIDTH:2 * QK_WIDTH].reshape(b, s, DA_HEADS, 2, DA_QK_DIM)
        v = proj[..., 2 * QK_WIDTH:2 * QK_WIDTH + DA_WIDTH].reshape(b, s, DA_HEADS, DA_V_DIM)
        u = proj[..., 2 * QK_WIDTH + DA_WIDTH:]

        q = apply_partial_rope(q, cos, sin).transpose(0, 2, 3, 1, 4)
        k = apply_partial_rope(k, cos, sin).transpose(0, 2, 3, 1, 4)
        v = v.transpose(0, 2, 1, 3)
        lam = (jnp.exp(jnp.sum(lambda_q1.astype(jnp.float32) * lambda_k1.astype(jnp.float32)))
               - jnp.exp(jnp.sum(lambda_q2.astype(jnp.float32) * lambda_k2.astype(jnp.float32)))
               + lam_init)
        da = diff_attention(q, k, v, lam)
        da = rmsnorm(da, g_subln) * (1.0 - lam_init)
        da = da.transpose(0, 2, 1, 3).reshape(b, s, DA_WIDTH)

        pooled = causal_multiscale_pool(u)
        po = jnp.einsum('bsgc,gcd->bsgd', pooled, w_pool).reshape(b, s, POOL_WIDTH)
        po = po * pool_scale

        mix = jnp.concatenate([da, po], axis=-1) @ w_out
        x = x + rmsnorm(mix, g_mix_post)

        hq = rmsnorm(x, g_x_pre)
        xq = (hq @ w_xq).reshape(b, s, X_HEADS, X_HEAD_DIM)
        kv = (mem_n @ w_xkv).reshape(b, MEM_LEN, 2, X_HEADS, X_HEAD_DIM)
        sc = jnp.einsum('bshd,bmhd->bhsm', xq, kv[:, :, 0]).astype(jnp.float32) * (X_HEAD_DIM ** -0.5)
        pm = jax.nn.softmax(sc, axis=-1).astype(x.dtype)
        xo = jnp.einsum('bhsm,bmhd->bshd', pm, kv[:, :, 1]).reshape(b, s, X_HEADS * X_HEAD_DIM)
        x = x + rmsnorm(xo @ w_xo, g_x_post)

        hf = rmsnorm(x, g_ffn_pre)
        ff = (jax.nn.silu(hf @ w_gate) * (hf @ w_up)) @ w_down
        x = x + rmsnorm(ff, g_ffn_post)

    return x


def setup_inputs(seed=0):
    out = dict(first_inputs(seed))
    for name, value in second_inputs(seed + 1).items():
        if name != "x":
            out[name + "_2"] = value
    return out


def reference(
    x, p, ln_pre_mix, w_in, conv_w, a_log, dt_bias, gdn_norm, w_proj_a, w_proj_b, w_out,
    ln_post_mix, ln_pre_ffn, w_ffn_gate, w_ffn_up, w_ffn_down, ln_post_ffn, w_ple, ln_ple,
    w_ple_gate, mem_2, positions_2, g_mix_pre_2, w_in_2, lambda_q1_2, lambda_k1_2, lambda_q2_2,
    lambda_k2_2, g_subln_2, w_pool_2, pool_scale_2, w_out_2, g_mix_post_2, g_x_pre_2, g_mem_2,
    w_xq_2, w_xkv_2, w_xo_2, g_x_post_2, g_ffn_pre_2, w_gate_2, w_up_2, w_down_2, g_ffn_post_2,
):
    x = first_block(
        x, p, ln_pre_mix, w_in, conv_w, a_log, dt_bias, gdn_norm, w_proj_a, w_proj_b, w_out,
        ln_post_mix, ln_pre_ffn, w_ffn_gate, w_ffn_up, w_ffn_down, ln_post_ffn, w_ple, ln_ple,
        w_ple_gate,
    )
    return second_block(
        x, mem_2, positions_2, g_mix_pre_2, w_in_2, lambda_q1_2, lambda_k1_2, lambda_q2_2,
        lambda_k2_2, g_subln_2, w_pool_2, pool_scale_2, w_out_2, g_mix_post_2, g_x_pre_2,
        g_mem_2, w_xq_2, w_xkv_2, w_xo_2, g_x_post_2, g_ffn_pre_2, w_gate_2, w_up_2, w_down_2,
        g_ffn_post_2,
    )


_drawn_inputs = setup_inputs


def setup_inputs(seed=0):
    import zlib

    import numpy as np

    out = dict(_drawn_inputs(seed))
    spreads = {}
    factors = {'g_mix_pre_2': 4.329,
     'lambda_q1_2': 8.0,
     'lambda_k1_2': 4.389,
     'lambda_q2_2': 3.741,
     'lambda_k2_2': 2.784,
     'g_subln_2': 8.0,
     'g_mix_post_2': 5.521,
     'g_x_pre_2': 6.352,
     'g_mem_2': 4.304,
     'g_x_post_2': 19.439,
     'g_ffn_pre_2': 12.866,
     'g_ffn_post_2': 31.523}
    for name, (base, spread) in spreads.items():
        noise = np.random.default_rng([zlib.crc32(name.encode()), seed]).standard_normal(out[name].shape)
        drawn = base * np.exp(spread * noise) if base else spread * noise
        out[name] = __import__('jax').numpy.asarray(drawn.astype(out[name].dtype))
    for name, factor in factors.items():
        out[name] = (out[name] * factor).astype(out[name].dtype)
    return out
```

```python
from contextlib import ExitStack

import numpy as np

import concourse.bass as bass
from concourse import mybir

F32 = mybir.dt.float32
F32R = mybir.dt.float32r
I32 = mybir.dt.int32
ALU = mybir.AluOpType
ACT = mybir.ActivationFunctionType
AX = mybir.AxisListType

P = 128
SEQ = 256
NT = SEQ // P
D = 1024
KD = D // P
HD = 128
NG = 2
GH = 4
FF = 2816
KF = FF // P
CONV = 4
PLE = 256
EPS = 1e-6
NEG = -3.0e38
LEVELS = 7
LAM_INIT = 0.2
WINDOWS = (2, 4, 8, 16)
RAW, SPLIT = 4, 6
UNIT = 1024
KB = 1024
MAGIC = 1.5 * 2.0 ** 23
TWO_PI = (6.28125, 2029 / 2 ** 20, 2 * np.pi - 6.28125 - 2029 / 2 ** 20)
ROPE2 = 8

COL = {"mq": 0, "mk": D, "mv": 2 * D, "cq": 3 * D, "ck": 4 * D, "cv": 5 * D, "z": 6 * D,
       "ba": 7 * D, "ga": 7 * D + 16, "gb": 8 * D + 16}


def constant_tables():
    i = np.arange(P)
    row, col = i[:, None], i[None, :]
    level = [((row >> l) % 2 == 0) & ((col >> l) == (row >> l) + 1) for l in range(LEVELS)]
    masks = [row == col, row <= col] + level + [np.ones((P, P), bool)]
    square = [m.astype(np.float32) for m in masks]
    square.append(np.where(row <= col, 0, NEG).astype(np.float32))
    square.append(np.where(col <= row, 0, NEG).astype(np.float32))
    inv = (1.0 / (10000.0 ** (np.arange(0, HD, 2, dtype=np.float32) / HD))).astype(np.float32)
    angle = (np.arange(SEQ, dtype=np.float32)[:, None] * inv[None, :]).astype(np.float32)
    cos, sin = np.cos(angle), np.sin(angle)
    cos2 = np.concatenate([cos, cos], 1).reshape(NT, P, HD).transpose(1, 0, 2).reshape(P, -1)
    sin2 = np.concatenate([-sin, sin], 1).reshape(NT, P, HD).transpose(1, 0, 2).reshape(P, -1)
    inv2 = 500000.0 ** (-np.arange(0, 2 * ROPE2, 2, dtype=np.float32) / (2 * ROPE2))
    inv2 = np.broadcast_to(inv2.astype(np.float32), (P, ROPE2))
    table = np.concatenate(square + [cos2, sin2, inv2], 1).astype(np.float32)
    t = np.arange(SEQ)
    pool = []
    for w in WINDOWS:
        seen = (t[:, None] <= t[None, :]) & (t[:, None] > t[None, :] - w)
        mean = seen / np.minimum(t + 1, w)[None, :] - np.eye(SEQ)
        pool.append(mean.reshape(NT, P, SEQ).transpose(1, 0, 2))
    pool = np.stack(pool, 1).reshape(P, -1).astype(np.float32)
    return np.ascontiguousarray(table), np.ascontiguousarray(pool)


class Done:

    def __init__(self, sem, known):
        self.sem, self.known, self.n, self.names = sem, known, 0, {}

    def mark(self, *name):
        self.n += 1
        if name:
            self.names[name] = self.n
        return self.sem, 1

    def __call__(self, *name):
        return self.sem, (self.known[name] if self.known else 1)


def schedule():
    s = [("u",), ("ba",)]
    for gr in range(2):
        s += [("conv", gr, 0), ("conv", gr, 1), ("conv", gr, 2), ("moba", gr, 0), ("tok", gr), ("moba", gr, 1), ("feat", gr),
              ("moba", gr, 2), ("att", gr)]
        s += [("z", 0), ("inv", 0), ("z", 1), ("ga", 0), ("scan", 0)] if gr == 0 else [("ga", 1), ("inv", 1), ("proj_a",), ("scan", 1)]
    s += [("gb", 0), ("yb",), ("gb", 1), ("mem",), ("proj_b",), ("xkv", 0), ("p",), ("merge",), ("w_out",)]
    s += [("norm", "mix"), ("ple",), ("next", "mix")]
    s += [("ffn", 1, c) for c in range(6)] + [("down", 1), ("norm", "ffn1"), ("xkv", 1), ("next", "ffn1")]
    s += [("ple_gate",), ("norm", "ple"), ("xkv", 2), ("next", "ple")]
    s += [("in2", c) for c in range(4)] + [("diff",), ("pool",), ("dnorm",), ("out2",), ("norm", "mix2"), ("xkv", 3), ("next", "mix2")]
    s += [("xq",), ("cross",), ("xo",), ("norm", "x"), ("next", "x")]
    s += [("ffn", 2, c) for c in range(6)] + [("down", 2), ("norm", "ffn2")]
    return s


FILLING = {("feat", 0): [("moba", 0, 2)], ("feat", 1): [("moba", 1, 2)],
           ("att", 0): [("z", 0)], ("inv", 0): [("z", 1), ("ga", 0)],
           ("att", 1): [("ga", 1)], ("inv", 1): [("proj_a",)]}
INSIDE = {f for fs in FILLING.values() for f in fs}


SCHEDULE = schedule()


def weight_units(w):
    units = []

    def columns(step, m, c0, n=512):
        per = UNIT // n
        for j in range(m.shape[0] // P // per):
            units.append((step, m[j * per * P:(j + 1) * per * P, c0:c0 + n].rearrange("(k p) n -> p k n", p=P)))

    def rows(step, m):
        for k in range(m.shape[0] // P):
            units.append((step, m[k * P:(k + 1) * P, :].rearrange("(k p) n -> p k n", p=P)))

    wide = {"proj_a": w["w_proj_a"], "proj_b": w["w_proj_b"], "w_out": w["w_out"], "ple_gate": w["w_ple_gate"],
            "ple": w["w_ple"], "out2": w["w_out_2"], "xq": w["w_xq_2"], "xo": w["w_xo_2"]}
    order = []
    for step in SCHEDULE:
        order += FILLING.get(step, [] if step in INSIDE else [step])
    for step in order:
        kind = step[0]
        if kind == "conv":
            columns(step, w["w_in"], COL["cq"] + step[2] * D + step[1] * 512)
        elif kind == "moba":
            columns(step, w["w_in"], COL["mq"] + step[2] * D + step[1] * 512)
        elif kind in ("z", "ga", "gb"):
            columns(step, w["w_in"], COL[kind] + step[1] * 512)
        elif kind == "xkv":
            columns(step, w["w_xkv_2"], step[1] * 512)
        elif kind == "in2":
            columns(step, w["w_in_2"], step[1] * 512)
        elif kind == "ffn":
            n = 512 if step[2] < FF // 512 else FF % 512
            for m in (("w_ffn_gate", "w_ffn_up") if step[1] == 1 else ("w_gate_2", "w_up_2")):
                columns(step, w[m], step[2] * 512, n)
        elif kind == "down":
            rows(step, w["w_ffn_down"] if step[1] == 1 else w["w_down_2"])
        elif kind in wide:
            rows(step, wide[kind])
    return units


def build(nc, a, out, known):
    w = {n: (a[n][0] if len(a[n].shape) == 3 else a[n]) for n in
         ("w_in", "w_proj_a", "w_proj_b", "w_out", "w_ffn_gate", "w_ffn_up", "w_ffn_down", "w_ple", "w_ple_gate",
          "w_in_2", "w_out_2", "w_xq_2", "w_xkv_2", "w_xo_2", "w_gate_2", "w_up_2", "w_down_2")}
    UNITS = weight_units(w)
    FIRST, LAST = {}, {}
    for n, (step, _) in enumerate(UNITS):
        FIRST.setdefault(step, n)
        LAST[step] = n
    ctx = ExitStack()
    with ctx:
        def sem(name):
            return ctx.enter_context(nc.semaphore(name))

        base = -(-nc.sbuf_base // 32) * 32
        at = [base]

        def place(name, shape, dt=F32, offset=None):
            size = 4 * int(np.prod(shape[1:]))
            if offset is None:
                offset = at[0]
                at[0] += -(-size // 32) * 32
            return nc.alloc_sbuf_tensor_at(name, list(shape), dt, offset=offset)

        raw = place("raw", [P, RAW, UNIT])
        w_hi = place("w_hi", [P, SPLIT, UNIT], F32R)
        w_lo = place("w_lo", [P, SPLIT, UNIT], F32R)
        uH = place("uH", [P, KD, SEQ], F32R)
        uL = place("uL", [P, KD, SEQ], F32R)
        table = place("table", [P, 12 * P + 2 * NT * HD + ROPE2])
        small = place("small", [P, 960])
        Y = at[0]
        yH = place("yH", [P, KD, SEQ], F32R)
        yL = place("yL", [P, KD, SEQ], F32R)
        B = at[0]
        hH = place("hH", [P, KF, SEQ], F32R, Y)
        hL = place("hL", [P, KF, SEQ], F32R, Y + KF * SEQ * 4)

        def big(name, kb, shape, dt=F32):
            return place(name, shape, dt, B + int(kb * KB))

        HALF = [P, NT, GH, HD]
        x0 = big("x0", 0, [P, NT, D])
        z = big("z", 0, [P, NT, D])
        gs = big("gs", 8, [P, NT, D])
        o = big("o", 16, [P, NT, D])
        ln0 = big("ln0", 24, [P, D])
        C = big("C", 24, [P, 3 * GH, SEQ])
        kT = big("kT", 24, HALF)
        kbqT = big("kbqT", 28, [P, NT, GH, 2, HD])
        gsb = big("gsb", 24, [P, NT, D])
        tok = big("tok", 36, [P, NT, 3, GH, HD])
        mtok = big("mtok", 48, [P, 3, NT, GH, HD])
        T = big("T", 60, HALF)
        TT = big("TT", 64, HALF)
        X = big("X", 68, HALF)
        M = big("M", 72, HALF)
        kb = big("kb", 72, HALF)
        vn = big("vn", 76, HALF)
        xn0 = big("xn0", 60, [P, NT, D])
        qTa = big("qTa", 60, [P, GH, SEQ])
        kTa = big("kTa", 64, [P, GH, SEQ])
        pr = big("pr", 68, [P, GH, 3 * P])
        prT = big("prT", 74, [P, GH, 3 * P])
        qeT = big("qeT", 80, [P, GH, HD])
        Dm = big("Dm", 82, HALF)
        AT = big("AT", 86, HALF)
        aT = big("aT", 90, HALF)
        kbe = big("kbe", 94, [P, GH, HD])
        kdec = big("kdec", 96, [P, GH, HD])
        qe = big("qe", 98, [P, GH, HD])
        S = big("S", 72, [P, GH, HD])
        wT = big("wT", 74, [P, GH, HD])
        sq = big("sq", 98, [P, GH, HD])
        sqr = big("sqr", 98, [P, GH, HD])
        h = big("h", 28, [P, NT, D])
        tmp = big("tmp", 36, [P, NT, D])
        sil = big("sil", 36, [P, NT, 512])
        hm = big("hm", 40, [P, NT, 512])
        gA = big("gA", 44, [P, D])
        gB = big("gB", 48, [P, D])
        hg = big("hg", 52, [P, NT, D])
        e = big("e", 60, [P, NT, D])
        mem = big("mem", 60, [P, NT, D])
        xkT = big("xkT", 68, [P, KD, SEQ])
        lnm = big("lnm", 68, [P, D])
        xv = big("xv", 76, [P, NT, D])
        mH = big("mH", 84, [P, KD, SEQ], F32R)
        mL = big("mL", 92, [P, KD, SEQ], F32R)
        pt = big("pt", 16, [P, NT, PLE])
        lnp = big("lnp", 20, [P, D])
        pH = big("pH", 0, [P, PLE // P, SEQ], F32R)
        pL = big("pL", 2, [P, PLE // P, SEQ], F32R)
        xk = [big("xk0", 52, [P, NT, 512]), big("xk1", 20, [P, NT, 512])]
        poolm = big("poolm", 0, [P, 4, NT, SEQ])
        qk2 = big("qk2", 8, [P, NT, 2, 2 * GH, 64])
        v2 = big("v2", 16, [P, NT, GH, HD])
        u2 = big("u2", 20, [P, NT, 512])
        da = big("da", 24, [P, NT, GH, HD])
        dqT = big("dqT", 36, [P, GH, SEQ])
        dkT = big("dkT", 40, [P, GH, SEQ])
        pd = [big("pd0", 52, [P, GH, 3 * P]), big("pd1", 60, [P, GH, 3 * P])]
        pdT = big("pdT", 36, [P, GH, 3 * P])
        poolT = place("poolT", [P, 4, SEQ], F32, Y)
        wpool = place("wpool", [P, 4, P], F32, Y + 4 * KB)
        dsq = place("dsq", [P, GH, HD], F32, Y + 6 * KB)
        gsub = place("gsub", [P, HD], F32, Y + 8 * KB)
        lamv = place("lamv", [P, 4, 64], F32, Y + 9 * KB)
        cq = big("cq", 0, [P, NT, D])
        cqT = big("cqT", 8, [P, KD, SEQ])
        cp = big("cp", 16, [P, NT, GH, SEQ])
        cpT = place("cpT", [P, NT, GH, SEQ], F32, Y)
        used = B + 100 * KB
        assert used <= nc.sbuf_usable_end, (used, nc.sbuf_usable_end)

        def square(n):
            return table[:, n * P:(n + 1) * P]

        ident, tri, ones = square(0), square(1), square(2 + LEVELS)
        neg_kq, neg_qk = square(3 + LEVELS), square(4 + LEVELS)
        base_t = (5 + LEVELS) * P
        cos1 = table[:, base_t:base_t + NT * HD].rearrange("p (t d) -> p t d", t=NT)
        sin1 = table[:, base_t + NT * HD:base_t + 2 * NT * HD].rearrange("p (t d) -> p t d", t=NT)
        inv2 = table[:, base_t + 2 * NT * HD:base_t + 2 * NT * HD + ROPE2]

        free = [0]

        def tiny(n):
            free[0] += n
            assert free[0] <= 960
            return small[:, free[0] - n:free[0]]

        def over(ap, n):
            return ap.unsqueeze(2).to_broadcast([P, ap.shape[1], n])

        def each(ap, n):
            return ap.unsqueeze(1).to_broadcast([P, n, ap.shape[1]])

        ss = tiny(8)
        rv = tiny(16)
        rt = tiny(16)
        rstd0 = tiny(2)
        rstd_m = tiny(2)
        rstd_p = tiny(2)
        rstd_h = tiny(2)
        rstd_o = tiny(2)
        cw = tiny(CONV * 24)
        cwr = tiny(P)
        gnorm = tiny(HD)
        ba_raw = tiny(KD * 16)
        ba = tiny(32)
        dtb, alog = tiny(8), tiny(8)
        beta, g = tiny(16), tiny(16)
        tA, tB = tiny(16), tiny(16)
        ss_p = tA[:, 0:4]
        gc, eg = tiny(8), tiny(8)
        glast, edec = tiny(4), tiny(4)
        s2 = tiny(16)
        rq = tiny(16)
        mx, nm, rs, ri = tiny(16), tiny(16), tiny(16), tiny(16)
        lam = tiny(4)
        posf = tiny(2)
        ang, kk, sn, cs = tiny(16), tiny(16), tiny(16), tiny(16)
        psc = tiny(4)
        r1, so = tiny(8), tiny(16)
        baH = big("baH", 36, [P, KD, 16], F32R)
        baL = big("baL", 37, [P, KD, 16], F32R)
        trg = big("trg", 68, HALF)
        pos_i = place("pos_i", [P, NT], I32, Y + 12 * KB)
        psr = place("psr", [4, P], F32, Y + 12 * KB + 512)
        r2t = [place(f"r2t{n}", [P, 4 * GH * ROPE2], F32, Y + 10 * KB + 512 * n) for n in range(4)]

        L = [ctx.enter_context(nc.psum_tensor(f"L{n}", [P, 512], F32)) for n in range(4)]
        Q = [ctx.enter_context(nc.psum_tensor(f"Q{n}", [P, 512], F32)) for n in range(4)]

        tensor_done, scalar_done, vector_done = sem("tensor_done"), sem("scalar_done"), sem("vector_done")
        w_landed = [sem(f"w_landed{n}") for n in range(RAW)]
        w_hi_there, w_lo_there, w_used = sem("w_hi_there"), sem("w_lo_there"), sem("w_used")
        loads = {}

        def load_sem(name):
            if name not in loads:
                loads[name] = sem(f"{name}_landed")
            return loads[name]

        PE = Done(tensor_done, known.get("pe"))
        AC = Done(scalar_done, known.get("act"))
        VE = Done(vector_done, known.get("dve"))
        load_names = ["x", "table", "ln0", "cwr", "ba", "dtb", "alog", "gnorm", "mem", "lnm", "p", "lnp", "xres",
                      "gA_mix", "gA_ffn1", "gA_mix2", "gA_x", "gA_ffn2", "gB_mix", "gB_ple", "gB_mix2", "gB_x",
                      "poolm", "wpool", "gsub", "lamv", "pos", "psc"]
        landed = {n: sem(f"{n}_landed") for n in load_names}
        stored = sem("stored")

        def fed(step, units=None):
            return w_used, (LAST[step] + 1 if units is None else FIRST[step] + units)

        block = ctx.enter_context(nc.Block())

        def tokens(ap):
            return ap.rearrange("(t p) d -> p t d", p=P)

        def row(ap, n):
            return ap.rearrange("(o d) -> o d", o=1).to_broadcast([P, n])

        RES = {"mix": ("ln_post_mix", "ln_pre_ffn"), "ffn1": ("ln_post_ffn", None), "ple": (None, "g_mix_pre_2"),
               "mix2": ("g_mix_post_2", "g_x_pre_2"), "x": ("g_x_post_2", "g_ffn_pre_2"), "ffn2": ("g_ffn_post_2", None)}

        @block.sync
        def _(sp):
            sp.dma_start(x0[:], tokens(a["x"][0])).then_inc(landed["x"], 16)
            sp.dma_start(ln0[:], row(a["ln_pre_mix"][0], D)).then_inc(landed["ln0"], 16)
            for n, (step, src) in enumerate(UNITS):
                if n >= RAW:
                    sp.wait_ge(w_lo_there, n - RAW + 1)
                dst = raw[:, n % RAW, :].rearrange("p (k n) -> p k n", k=src.shape[1])
                sp.dma_start(dst, src).then_inc(w_landed[n % RAW], 16)
            sp.wait_ge(*VE("out", 3))
            sp.dma_start(tokens(out[0]), h[:]).then_inc(stored, 16)
            sp.wait_ge(stored, 16)

        @block.gpsimd
        def _(pool):
            for n in range(len(UNITS)):
                pool.wait_ge(w_hi_there, n + 1)
                nc.gpsimd.tensor_tensor(w_lo[:, n % SPLIT, :], raw[:, n % RAW, :], w_hi[:, n % SPLIT, :].bitcast(F32),
                                        ALU.subtract).then_inc(w_lo_there, 1)

        @block.tensor
        def _(pe):
            mm, turn = nc.tensor.matmul, nc.tensor.transpose

            def split_mm(dst, sH, sL, wH, wL, start, stop):
                mm(dst, sH, wH, start=start, stop=False)
                mm(dst, sH, wL, start=False, stop=False)
                return mm(dst, sL, wH, start=False, stop=stop)

            def unit(n, k):
                slot = n % SPLIT
                return (w_hi[:, slot, :].rearrange("p (k n) -> p k n", k=k),
                        w_lo[:, slot, :].rearrange("p (k n) -> p k n", k=k))

            def column_unit(step, j, banks, n0=None, n=512, sH=uH, sL=uL):
                n0 = FIRST[step] if n0 is None else n0
                per = UNIT // n
                pe.wait_ge(w_lo_there, n0 + j + 1)
                wH, wL = unit(n0 + j, per)
                for i in range(per):
                    k = j * per + i
                    for t in range(NT):
                        last = split_mm(banks[t][:, 0:n], sH[:, k, t * P:(t + 1) * P], sL[:, k, t * P:(t + 1) * P],
                                        wH[:, i, :], wL[:, i, :], k == 0, k == KD - 1)
                last.then_inc(w_used, 1)

            def columns(step, banks, n0=None, n=512, sH=uH, sL=uL):
                for j in range(KD * n // UNIT):
                    column_unit(step, j, banks, n0, n, sH, sL)

            def row_unit(step, k, sH, sL, k_tiles):
                n0 = FIRST[step]
                pe.wait_ge(w_lo_there, n0 + k + 1)
                wH, wL = unit(n0 + k, 2)
                for t in range(NT):
                    s_h, s_l = sH[:, k, t * P:(t + 1) * P], sL[:, k, t * P:(t + 1) * P]
                    for c in range(2):
                        last = split_mm(L[2 * t + c][:], s_h, s_l, wH[:, c, :], wL[:, c, :], k == 0, k == k_tiles - 1)
                        if k == k_tiles - 1 and 2 * t + c < 3:
                            last.then_inc(*PE.mark(step, "bank", 2 * t + c))
                last.then_inc(w_used, 1)

            def rows(step, sH, sL, k_tiles):
                for k in range(k_tiles):
                    row_unit(step, k, sH, sL, k_tiles)

            inside = {("moba", 0, 2): ([L[0], L[1]], [VE(("moba", 0, 0), "rope", 1)]),
                      ("moba", 1, 2): ([L[0], L[1]], [VE(("moba", 1, 0), "rope", 1)]),
                      ("z", 0): ([L[2], L[3]], [VE(("moba", 0, 1), "rope", 1)]),
                      ("z", 1): ([L[0], L[1]], [AC(("moba", 0, 2), "v", 1)]),
                      ("ga", 0): ([L[2], L[3]], [AC(("z", 0))]),
                      ("ga", 1): ([L[2], L[3]], [VE(("moba", 1, 1), "rope", 1)]),
                      ("proj_a",): (L, [AC(("moba", 1, 2), "v", 1), AC(("ga", 1)), VE(("att", 1), "lo", 1)])}

            def fill(step, i):
                n = FIRST[FILLING[step][0]] + i
                f, j = next((f, n - FIRST[f]) for f in FILLING[step] if FIRST[f] <= n <= LAST[f])
                banks, free_ = inside[f]
                if j == 0:
                    for wt in free_:
                        pe.wait_ge(*wt)
                if f == ("proj_a",):
                    row_unit(f, j, yH, yL, KD)
                else:
                    column_unit(f, j, banks)

            def turn_wide(step, src, k_tiles, ready):
                for j in range(k_tiles // 2):
                    for t in range(NT):
                        pe.wait_ge(*ready(j, t))
                        if t == 0 and j >= 4:
                            pe.wait_ge(*VE(step, "lo", j - 4))
                        for i in range(2):
                            last = turn(Q[j % 4][:, i * SEQ + t * P:i * SEQ + (t + 1) * P],
                                        src[:, t, (2 * j + i) * P:(2 * j + i + 1) * P], ident)
                    last.then_inc(*PE.mark(step, "turned", j))

            for step in SCHEDULE:
                kind = step[0]
                if kind == "u":
                    pe.wait_ge(landed["table"], 16)
                    turn_wide(step, xn0, KD, lambda j, t: VE(("u",), "scaled", t))
                elif step in INSIDE:
                    continue
                elif kind == "ba":
                    pe.wait_ge(landed["cwr"], 16)
                    pe.wait_ge(*VE(("u",), "lo", 3))
                    turn(Q[1][:, 0:CONV * 24], cwr[0:CONV * 24, :], ident[0:CONV * 24, 0:CONV * 24]).then_inc(*PE.mark(step, "taps"))
                    pe.wait_ge(*VE(step, "split"))
                    for t in range(NT):
                        for k in range(KD):
                            last = split_mm(Q[0][:, t * 16:t * 16 + 16], uH[:, k, t * P:(t + 1) * P], uL[:, k, t * P:(t + 1) * P],
                                            baH[:, k, :], baL[:, k, :], k == 0, k == KD - 1)
                    last.then_inc(*PE.mark(step))
                elif kind == "conv":
                    _, gr, part = step
                    n0 = FIRST[step]
                    b0 = 2 * (part % 2)
                    if part == 2:
                        pe.wait_ge(*VE(("conv", gr, 0), "taps done"))
                    elif gr == 1:
                        pe.wait_ge(*AC(("z", 1) if part == 0 else ("ga", 0)))
                    for ct in range(4):
                        for k in range(KD):
                            if ct == 0 and k % 2 == 0:
                                pe.wait_ge(w_lo_there, n0 + k // 2 + 1)
                            wH, wL = unit(n0 + k // 2, 2)
                            bank = L[b0 + ct // 2][:, (ct % 2) * SEQ:(ct % 2 + 1) * SEQ]
                            sH, sL = wH[:, k % 2, ct * P:(ct + 1) * P], wL[:, k % 2, ct * P:(ct + 1) * P]
                            mm(bank, sH, uH[:, k, :], start=k == 0, stop=False)
                            mm(bank, sH, uL[:, k, :], start=False, stop=False)
                            last = mm(bank, sL, uH[:, k, :], start=False, stop=k == KD - 1)
                            if ct == 3 and k % 2 == 1:
                                last.then_inc(w_used, 1)
                        if ct == 1:
                            last.then_inc(*PE.mark(step, "half"))
                elif kind == "tok":
                    gr = step[1]
                    for part in range(3):
                        for t in range(NT):
                            b = part * NT + t
                            pe.wait_ge(*AC(("conv", gr, part), "silu"))
                            if b >= 4:
                                pe.wait_ge(*AC(step, "out", (b - 4) // NT, (b - 4) % NT))
                            elif b == 0:
                                if gr == 0:
                                    pe.wait_ge(*VE(("ba",), "g"))
                                else:
                                    pe.wait_ge(*AC(("scan", 0), "o", 1))
                            for i in range(GH):
                                last = turn(Q[b % 4][:, i * P:(i + 1) * P], C[:, part * GH + i, t * P:(t + 1) * P], ident)
                            last.then_inc(*PE.mark(step, "turned", part, t))
                elif kind == "moba":
                    _, gr, part = step
                    pe.wait_ge(*VE(("conv", gr, 2 - part), "taps done"))
                    columns(step, [L[2 * part], L[2 * part + 1]])
                elif kind == "feat":
                    gr = step[1]
                    pe.wait_ge(*AC(("tok", gr), "out", 2, 1))
                    for t in range(NT):
                        last = mm(Q[3][:, t * 8:t * 8 + GH], tri, g[:, t * 8 + gr * GH:t * 8 + gr * GH + GH], start=True, stop=True)
                    last.then_inc(*PE.mark(step, "gc"))
                    fill(step, 0)
                    for t in range(NT):
                        pe.wait_ge(*VE(step, "tri g", t))
                        mm(Q[t][:], ones, trg[:, t, :, :].rearrange("p h d -> p (h d)"), start=True, stop=True).then_inc(*PE.mark(step, "rows", t))
                    lots = [("kn", 0), ("kb", 0), ("qn", 0), ("kn", 1), ("kb", 1), ("qn", 1), ("qe", 1)]
                    src = {"kn": lambda t, i: tok[:, t, 1, i, :], "kb": lambda t, i: kb[:, t, i, :],
                           "qn": lambda t, i: tok[:, t, 0, i, :], "qe": lambda t, i: qe[:, i, :]}
                    fill(step, 1)
                    for b, (what, t) in enumerate(lots):
                        if b == 4:
                            fill(step, 2)
                        pe.wait_ge(*VE(step, what, t))
                        if b >= 4:
                            pe.wait_ge(*AC(step, "out", b - 4))
                        for i in range(GH):
                            last = turn(Q[b % 4][:, i * P:(i + 1) * P], src[what](t, i), ident)
                        last.then_inc(*PE.mark(step, "turned", b))
                    fill(step, 3)
                    pe.wait_ge(*AC(step, "out", 6))
                    for t in range(NT):
                        for i in range(GH):
                            last = mm(Q[2 * t + i // 2][:, (i % 2) * 256:(i % 2 + 1) * 256], kT[:, t, i, :],
                                      kbqT[:, t, i, :, :].rearrange("p a b -> p (a b)"), start=True, stop=True)
                            if i % 2:
                                last.then_inc(*PE.mark(step, "kk", t, i // 2))
                elif kind == "att":
                    gr = step[1]
                    for b in range(4):
                        part, pair = b // 2, b % 2
                        pe.wait_ge(*VE(("moba", gr, part), "rope", 1))
                        pe.wait_ge(*VE(("feat", gr), "attn", 1, 1))
                        for i in range(2):
                            for t in range(NT):
                                last = turn(Q[b][:, i * SEQ + t * P:i * SEQ + (t + 1) * P], mtok[:, part, t, 2 * pair + i, :], ident)
                        last.then_inc(*PE.mark(step, "turned", b))
                    fill(step, 0)
                    pe.wait_ge(*AC(step, "heads", 3))
                    for i in range(GH):
                        last = mm(Q[0][:, i * P:(i + 1) * P], qTa[:, i, 0:P], kTa[:, i, 0:P], start=True, stop=True)
                    last.then_inc(*PE.mark(step, "scores", 0))
                    for i in range(GH):
                        last = mm(Q[1 + i // 2][:, (i % 2) * SEQ:(i % 2 + 1) * SEQ], qTa[:, i, P:SEQ], kTa[:, i, :], start=True, stop=True)
                        if i % 2:
                            last.then_inc(*PE.mark(step, "scores", 1 + i // 2))
                    fill(step, 1)
                    fill(step, 2)
                    for b, j in enumerate((0, 1, 2)):
                        pe.wait_ge(*VE(step, "probs"))
                        for i in range(GH):
                            last = turn(Q[b][:, i * P:(i + 1) * P], pr[:, i, j * P:(j + 1) * P], ident)
                        last.then_inc(*PE.mark(step, "probs turned", b))
                    fill(step, 3)
                    pe.wait_ge(*AC(("moba", gr, 2), "v", 1))
                    pe.wait_ge(*AC(step, "probs", 2))
                    for i in range(GH):
                        bank = Q[3 if i < 2 else 0]
                        c0 = (i % 2) * SEQ
                        mm(bank[:, c0:c0 + SEQ], mtok[:, 2, 0, i, :], prT[:, i, 0:SEQ], start=True, stop=False)
                        last = mm(bank[:, c0 + P:c0 + SEQ], mtok[:, 2, 1, i, :], prT[:, i, SEQ:3 * P], start=False, stop=True)
                        if i % 2:
                            last.then_inc(*PE.mark(step, "out", i // 2))
                elif kind == "gb":
                    c = step[1]
                    pe.wait_ge(*VE(("proj_a",), "mul", 2 + c))
                    columns(step, [L[c], L[2 + c]])
                elif kind == "proj_b":
                    pe.wait_ge(*AC(("gb", 1)))
                    pe.wait_ge(*VE(("yb",), "lo", 3))
                    rows(step, yH, yL, KD)
                elif kind == "inv":
                    gr = step[1]
                    pe.wait_ge(*VE(step, "mask", 0))
                    pe.wait_ge(*VE(("att", gr), "lo", 1))
                    for t in range(NT):
                        for i in range(GH):
                            last = turn(Q[t][:, i * P:(i + 1) * P], M[:, t, i, :], ident)
                        last.then_inc(*PE.mark(step, "M0", t))
                    fill(step, 0)
                    for l in range(1, LEVELS):
                        pe.wait_ge(*VE(step, "mask", l))
                        A = [Q[2], Q[3], Q[0], Q[1]] if l % 2 else Q
                        for t in range(NT):
                            pe.wait_ge(*VE(step, "TT", l - 1, t))
                            for i in range(GH):
                                last = mm(A[t][:, i * P:(i + 1) * P], M[:, t, i, :], T[:, t, i, :], start=True, stop=True)
                            last.then_inc(*PE.mark(step, "X", l, t))
                        fill(step, l)
                        for t in range(NT):
                            pe.wait_ge(*AC(step, "X", l, t))
                            by, bt = (A[2], A[3]) if t == 0 else (A[0], A[1])
                            if l < LEVELS - 1:
                                for i in range(GH):
                                    last = mm(by[:, i * P:(i + 1) * P], TT[:, t, i, :], X[:, t, i, :], start=True, stop=True)
                                last.then_inc(*PE.mark(step, "Y", l, t))
                            for i in range(GH):
                                last = mm(bt[:, i * P:(i + 1) * P], X[:, t, i, :], TT[:, t, i, :], start=True, stop=True)
                            last.then_inc(*PE.mark(step, "YT", l, t))
                    fill(step, LEVELS)
                elif kind == "scan":
                    gr = step[1]
                    iv = ("inv", gr)
                    pe.wait_ge(*VE(iv, "TT", LEVELS - 1, 1))
                    for t in range(NT):
                        for i in range(GH):
                            last = mm(Q[t][:, i * P:(i + 1) * P], TT[:, t, i, :], tok[:, t, 2, i, :], start=True, stop=True)
                        last.then_inc(*PE.mark(step, "u", t))
                    for i in range(GH):
                        last = mm(Q[2][:, i * P:(i + 1) * P], kbe[:, i, :], TT[:, 1, i, :], start=True, stop=True)
                    last.then_inc(*PE.mark(step, "wT"))
                    pe.wait_ge(*AC(step, "u", 0))
                    for i in range(GH):
                        last = mm(Q[3][:, i * P:(i + 1) * P], kdec[:, i, :], vn[:, 0, i, :], start=True, stop=True)
                    last.then_inc(*PE.mark(step, "S"))
                    for i in range(GH):
                        last = mm(Q[0][:, i * P:(i + 1) * P], aT[:, 0, i, :], vn[:, 0, i, :], start=True, stop=True)
                    last.then_inc(*PE.mark(step, "o", 0))
                    pe.wait_ge(*AC(step, "S"))
                    for i in range(GH):
                        last = mm(Q[2][:, i * P:(i + 1) * P], wT[:, i, :], S[:, i, :], start=True, stop=True)
                    last.then_inc(*PE.mark(step, "wS"))
                    pe.wait_ge(*VE(step, "vn"))
                    for i in range(GH):
                        mm(Q[1][:, i * P:(i + 1) * P], qeT[:, i, :], S[:, i, :], start=True, stop=False)
                        last = mm(Q[1][:, i * P:(i + 1) * P], aT[:, 1, i, :], vn[:, 1, i, :], start=False, stop=True)
                    last.then_inc(*PE.mark(step, "o", 1))
                elif kind == "mem":
                    pe.wait_ge(*VE(("yb",), "lo", 3))
                    turn_wide(step, mem, KD, lambda j, t: VE(("mem",), "scaled"))
                elif kind == "yb":
                    pe.wait_ge(*AC(("scan", 1), "o", 1))
                    turn_wide(step, o, KD, lambda j, t: VE(("yb",), "y", t))
                elif kind == "p":
                    pe.wait_ge(landed["p"], 16)
                    pe.wait_ge(*AC(("xkv", 0), 1))
                    turn_wide(step, pt, 2, lambda j, t: VE(("yb",), "lo", 3))
                elif kind == "merge":
                    pe.wait_ge(*VE(("p",), "lo", 0))
                    pe.wait_ge(*AC(("xkv", 0), "turned", 1))
                    turn_wide(step, gs, KD, lambda j, t: VE(("proj_b",), "sum", t))
                elif kind == "w_out":
                    pe.wait_ge(*VE(("merge",), "lo", 3))
                    rows(step, uH, uL, KD)
                elif kind == "ple":
                    pe.wait_ge(*VE(("merge",), "lo", 3))
                    for k in range(2):
                        n = FIRST[step] + k
                        pe.wait_ge(w_lo_there, n + 1)
                        wH, wL = unit(n, 2)
                        for t in range(NT):
                            for c in range(2):
                                last = split_mm(Q[2 * t + c][:], pH[:, k, t * P:(t + 1) * P], pL[:, k, t * P:(t + 1) * P],
                                                wH[:, c, :], wL[:, c, :], k == 0, k == 1)
                        last.then_inc(w_used, 1)
                elif kind == "xkv":
                    c = step[1]
                    before = {0: VE(("mem",), "lo", 3), 1: VE(("ffn", 1, 5), "lo", 0), 2: VE(("next", "ffn1"), "lo", 3),
                              3: VE(("dnorm",), "lo", 1)}
                    pe.wait_ge(*before[c])
                    columns(step, [Q[0], Q[1]], sH=mH, sL=mL)
                    if c < 2:
                        pe.wait_ge(*AC(step, 1))
                        for j in range(2):
                            for i in range(2):
                                for t in range(NT):
                                    last = turn(Q[2 + j][:, i * SEQ + t * P:i * SEQ + (t + 1) * P],
                                                xk[c][:, t, (2 * j + i) * P:(2 * j + i + 1) * P], ident)
                            last.then_inc(*PE.mark(step, "turned", j))
                elif kind == "next":
                    what = step[1]
                    through = {"mix": VE(("ple",), "e", 3), "ffn1": AC(("xkv", 1), "turned", 1), "ple": AC(("xkv", 2), 1),
                               "mix2": AC(("xkv", 3), 1)}
                    if what in through:
                        pe.wait_ge(*through[what])
                    src = h if what == "ffn1" else hg
                    turn_wide(step, src, KD, lambda j, t: VE(("norm", what), "next", t, j // 2))
                elif kind == "ffn":
                    _, blk, c = step
                    n = 512 if c < 5 else 256
                    half = (LAST[step] + 1 - FIRST[step]) // 2
                    if c == 0:
                        pe.wait_ge(*VE(("next", "mix" if blk == 1 else "x"), "lo", 3))
                    else:
                        pe.wait_ge(*AC(("ffn", blk, c - 1), "silu", 1))
                    columns(step, [L[0], L[1]], n=n)
                    if c > 0:
                        prev = ("ffn", blk, c - 1)
                        pe.wait_ge(*VE(prev, "hidden", 1))
                        for j in range(2):
                            for i in range(2):
                                for t in range(NT):
                                    last = turn(Q[2 * (c % 2) + j][:, i * SEQ + t * P:i * SEQ + (t + 1) * P],
                                                hm[:, t, (2 * j + i) * P:(2 * j + i + 1) * P], ident)
                            last.then_inc(*PE.mark(prev, "turned", j))
                    columns(step, [L[2], L[3]], FIRST[step] + half, n)
                    if c == 5:
                        pe.wait_ge(*VE(step, "hidden", 1))
                        for i in range(2):
                            for t in range(NT):
                                last = turn(Q[0][:, i * SEQ + t * P:i * SEQ + (t + 1) * P], hm[:, t, i * P:(i + 1) * P], ident)
                        last.then_inc(*PE.mark(step, "turned", 0))
                elif kind == "down":
                    blk = step[1]
                    pe.wait_ge(*VE(("ffn", blk, 5), "lo", 0))
                    rows(step, hH, hL, KF)
                elif kind == "ple_gate":
                    pe.wait_ge(*VE(("next", "ffn1"), "lo", 3))
                    rows(step, uH, uL, KD)
                elif kind == "in2":
                    c = step[1]
                    if c == 0:
                        pe.wait_ge(*VE(("next", "ple"), "lo", 3))
                    elif c >= 2:
                        pe.wait_ge(*AC(("in2", c - 2), 1))
                    b0 = 2 * (c % 2)
                    columns(step, [L[b0], L[b0 + 1]])
                elif kind == "diff":
                    pe.wait_ge(*VE(("diff",), "rope"))
                    pe.wait_ge(*VE(("next", "ple"), "lo", 3))
                    for b in range(4):
                        part, pair = b // 2, b % 2
                        for i in range(2):
                            for t in range(NT):
                                hh = 2 * pair + i
                                last = turn(Q[b][:, i * SEQ + t * P:i * SEQ + (t + 1) * P],
                                            qk2[:, t, part, 2 * hh:2 * hh + 2, :].rearrange("p m d -> p (m d)"), ident)
                        last.then_inc(*PE.mark(step, "turned", b))
                    pe.wait_ge(*AC(step, "heads", 3))
                    pe.wait_ge(*AC(("in2", 3), 1))
                    banks = [[Q[0], Q[1], Q[2]], [Q[3], L[0], L[1]]]
                    for m in range(2):
                        lo, hi = 64 * m, 64 * m + 64
                        for i in range(GH):
                            last = mm(banks[m][0][:, i * P:(i + 1) * P], dqT[lo:hi, i, 0:P], dkT[lo:hi, i, 0:P], start=True, stop=True)
                        last.then_inc(*PE.mark(step, "scores", m, 0))
                        for i in range(GH):
                            last = mm(banks[m][1 + i // 2][:, (i % 2) * SEQ:(i % 2 + 1) * SEQ], dqT[lo:hi, i, P:SEQ], dkT[lo:hi, i, :],
                                      start=True, stop=True)
                            if i % 2:
                                last.then_inc(*PE.mark(step, "scores", m, 1 + i // 2))
                    pe.wait_ge(landed["poolm"], 16)
                    for b in range(2):
                        for i in range(2):
                            gi = 2 * b + i
                            for t in range(NT):
                                last = mm(L[2 + b][:, i * SEQ:(i + 1) * SEQ], u2[:, t, gi * P:(gi + 1) * P], poolm[:, gi, t, :],
                                          start=t == 0, stop=t == 1)
                        last.then_inc(*PE.mark(("pool",), "pooled", b))
                    pe.wait_ge(*VE(step, "probs"))
                    for j in range(3):
                        for i in range(GH):
                            last = turn(Q[j][:, i * P:(i + 1) * P], pd[0][:, i, j * P:(j + 1) * P], ident)
                        last.then_inc(*PE.mark(step, "probs turned", j))
                    pe.wait_ge(*AC(step, "probs", 2))
                    for t in range(NT):
                        bank = Q[3] if t == 0 else L[0]
                        for i in range(GH):
                            o_ = bank[:, i * P:(i + 1) * P]
                            last = mm(o_, pdT[:, i, t * P:(t + 1) * P], v2[:, 0, i, :], start=True, stop=t == 0)
                            if t == 1:
                                last = mm(o_, pdT[:, i, 2 * P:3 * P], v2[:, 1, i, :], start=False, stop=True)
                        last.then_inc(*PE.mark(step, "out", t))
                elif kind == "pool":
                    pe.wait_ge(landed["wpool"], 16)
                    pe.wait_ge(landed["psc"], 16)
                    pe.wait_ge(*AC(("in2", 3), 1))
                    turn(Q[2][:, 0:4], psr[:, :], ident[0:4, 0:4]).then_inc(*PE.mark(step, "scale"))
                    for b in range(2):
                        pe.wait_ge(*AC(step, "pooled", 1))
                        for i in range(2):
                            gi = 2 * b + i
                            last = mm(Q[b][:, i * SEQ:(i + 1) * SEQ], wpool[:, gi, :], poolT[:, gi, :], start=True, stop=True)
                        last.then_inc(*PE.mark(step, "out", b))
                elif kind == "dnorm":
                    pe.wait_ge(*VE(("pool",), "scale"))
                    for j in range(2):
                        pe.wait_ge(*VE(step, "da"))
                        for i in range(2):
                            for t in range(NT):
                                last = turn(Q[2 + j][:, i * SEQ + t * P:i * SEQ + (t + 1) * P], da[:, t, 2 * j + i, :], ident)
                        last.then_inc(*PE.mark(step, "turned", j))
                elif kind == "out2":
                    pe.wait_ge(*VE(("pool",), "lo", 3))
                    pe.wait_ge(*VE(("dnorm",), "lo", 1))
                    rows(step, uH, uL, KD)
                elif kind == "xq":
                    pe.wait_ge(*VE(("next", "mix2"), "lo", 3))
                    rows(step, uH, uL, KD)
                elif kind == "cross":
                    for j in range(4):
                        for t in range(NT):
                            pe.wait_ge(*AC(("xq",), t, j // 2))
                            for i in range(2):
                                last = turn(Q[j][:, i * SEQ + t * P:i * SEQ + (t + 1) * P],
                                            cq[:, t, (2 * j + i) * P:(2 * j + i + 1) * P], ident)
                        last.then_inc(*PE.mark(step, "turned", j))
                    pe.wait_ge(*AC(step, "heads", 3))
                    pe.wait_ge(*VE(step, "heads", 2))
                    for t in range(NT):
                        for i in range(GH):
                            bank = L[2 * t + i // 2][:, (i % 2) * SEQ:(i % 2 + 1) * SEQ]
                            for k in range(2):
                                last = mm(bank, cqT[:, 2 * i + k, t * P:(t + 1) * P], xkT[:, 2 * i + k, :], start=k == 0, stop=k == 1)
                            if i % 2:
                                last.then_inc(*PE.mark(step, "scores", t, i // 2))
                    for t in range(NT):
                        pe.wait_ge(*VE(step, "probs", t))
                        for j in range(2):
                            for i in range(GH):
                                last = turn(Q[2 * t + j][:, i * P:(i + 1) * P], cp[:, t, i, j * P:(j + 1) * P], ident)
                            last.then_inc(*PE.mark(step, "probs turned", t, j))
                    pe.wait_ge(*AC(step, "probs", 1, 1))
                    for j in range(4):
                        for i in range(2):
                            for k in range(NT):
                                last = mm(L[j][:, i * SEQ:(i + 1) * SEQ], xv[:, k, (2 * j + i) * P:(2 * j + i + 1) * P], cpT[:, k, j, :],
                                          start=k == 0, stop=k == 1)
                        last.then_inc(*PE.mark(step, "out", j))
                elif kind == "xo":
                    pe.wait_ge(*VE(("cross",), "lo", 3))
                    rows(step, uH, uL, KD)

        @block.scalar
        def _(act):
            made = [0]
            copy, actf = nc.scalar.copy, nc.scalar.activation

            def split_up_to(n):
                while made[0] < min(n, len(UNITS)):
                    u = made[0]
                    act.wait_ge(w_landed[u % RAW], 16 * (u // RAW + 1))
                    if u >= SPLIT:
                        act.wait_ge(w_used, u - SPLIT + 1)
                    copy(w_hi[:, u % SPLIT, :], raw[:, u % RAW, :]).then_inc(w_hi_there, 1)
                    made[0] += 1

            def hi_wide(step, dst, k_tiles):
                for j in range(k_tiles // 2):
                    act.wait_ge(*PE(step, "turned", j))
                    copy(dst[:, 2 * j:2 * j + 2, :], Q[j % 4][:].rearrange("p (k n) -> p k n", k=2)).then_inc(*AC.mark(step, "hi", j))

            def load(name, dst, src, *waits, **how):
                for wt in waits:
                    act.wait_ge(*wt)
                act.dma_start(dst, src, **how).then_inc(landed[name], 16)

            def fill(step, i):
                split_up_to(FIRST[FILLING[step][0]] + i + SPLIT)

            load("table", table[:], a["table"])
            load("cwr", cwr[0:CONV * 24, :], a["conv_w"][0].rearrange("j (t c) -> (j t) c", c=P))
            load("ba", ba_raw.rearrange("p (k n) -> p k n", k=KD),
                 w["w_in"][:, COL["ba"]:COL["ba"] + 16].rearrange("(k p) n -> p k n", p=P))
            load("dtb", dtb, row(a["dt_bias"][0], 8))
            load("alog", alog, row(a["a_log"][0], 8))
            load("gnorm", gnorm, row(a["gdn_norm"][0], HD))
            consumed = 0
            for step in SCHEDULE:
                kind = step[0]
                if step in LAST:
                    consumed = max(consumed, LAST[step] + 1)
                if kind != "u":
                    split_up_to(consumed + SPLIT - 1)
                if kind == "u":
                    act.wait_ge(landed["x"], 16)
                    for t in range(NT):
                        actf(xn0[:, t, :], x0[:, t, :], ACT.Square, accum_out=ss[:, t:t + 1]).then_inc(*AC.mark(step, "ss", t))
                    hi_wide(step, uH, KD)
                elif kind == "ba":
                    act.wait_ge(*VE(step, "ba"))
                    bav = ba.rearrange("p (t n) -> p t n", t=NT)
                    actf(beta.rearrange("p (t n) -> p t n", t=NT), bav[:, :, 0:8], ACT.Sigmoid).then_inc(*AC.mark(step, "beta"))
                    act.wait_ge(landed["alog"], 16)
                    actf(alog, alog, ACT.Exp).then_inc(*AC.mark(step, "alog"))
                    act.wait_ge(*VE(step, "abs"))
                    actf(tB, tB, ACT.Exp, scale=-1.0).then_inc(*AC.mark(step, "exp"))
                    act.wait_ge(*VE(step, "1+exp"))
                    actf(tB, tB, ACT.Ln).then_inc(*AC.mark(step, "ln"))
                elif kind == "conv":
                    _, gr, part = step
                    act.wait_ge(*VE(step, "taps done"))
                    cv = C[:, part * GH:(part + 1) * GH, :]
                    actf(cv, cv, ACT.Silu).then_inc(*AC.mark(step, "silu"))
                elif kind == "tok":
                    for part in range(3):
                        for t in range(NT):
                            act.wait_ge(*PE(step, "turned", part, t))
                            if part == 0 and t == 0 and step[1] == 1:
                                act.wait_ge(*PE(("scan", 0), "o", 1))
                            copy(tok[:, t, part, :, :], Q[(part * NT + t) % 4][:].rearrange("p (h d) -> p h d", h=GH)).then_inc(*AC.mark(step, "out", part, t))
                            if part < 2:
                                act.wait_ge(*AC(step, "out", part, t))
                                if part + t == 0:
                                    act.wait_ge(*VE(("moba", step[1], 0), "rope", 1))
                                if part + t > 0:
                                    pt_, pp_ = (0, part) if t == 1 else (1, part - 1)
                                    act.wait_ge(*VE(step, "sum", pp_, pt_))
                                elif step[1] == 1:
                                    act.wait_ge(*VE(("scan", 0), "sum", 1))
                                actf(sq[:], tok[:, t, part, :, :], ACT.Square).then_inc(*AC.mark(step, "sq", part, t))
                elif kind == "moba":
                    _, gr, part = step
                    if part == 2:
                        act.wait_ge(*fed(step))
                        if gr == 1:
                            act.wait_ge(*PE(("att", 0), "out", 1))
                        for t in range(NT):
                            copy(mtok[:, 2, t, :, :], L[t][:].rearrange("p (h d) -> p h d", h=GH)).then_inc(*AC.mark(step, "v", t))
                elif kind == "feat":
                    gr = step[1]
                    outs = [kT[:, 0], kbqT[:, 0, :, 0, :], kbqT[:, 0, :, 1, :], kT[:, 1], kbqT[:, 1, :, 0, :], kbqT[:, 1, :, 1, :], qeT[:]]
                    act.wait_ge(*VE(step, "gc"))
                    actf(eg, gc, ACT.Exp).then_inc(*AC.mark(step, "eg"))
                    fill(step, 0)
                    act.wait_ge(*VE(step, "glast"))
                    actf(edec, edec, ACT.Exp).then_inc(*AC.mark(step, "edec"))
                    for t in range(NT):
                        act.wait_ge(*VE(step, "decay log", t))
                        actf(Dm[:, t], Dm[:, t], ACT.Exp).then_inc(*AC.mark(step, "decay", t))
                    fill(step, 1)
                    for b in range(7):
                        if b == 4:
                            fill(step, 2)
                        act.wait_ge(*PE(step, "turned", b))
                        copy(outs[b], Q[b % 4][:].rearrange("p (h d) -> p h d", h=GH)).then_inc(*AC.mark(step, "out", b))
                    fill(step, 3)
                elif kind == "att":
                    gr = step[1]
                    outs = [qTa[:, 0:2, :], qTa[:, 2:4, :], kTa[:, 0:2, :], kTa[:, 2:4, :]]
                    for b in range(4):
                        act.wait_ge(*PE(step, "turned", b))
                        copy(outs[b], Q[b][:].rearrange("p (h d) -> p h d", h=2)).then_inc(*AC.mark(step, "heads", b))
                    fill(step, 0)
                    act.wait_ge(*VE(step, "max"))
                    for t in range(NT):
                        for i in range(GH):
                            p_ = pr[:, i, 0:P] if t == 0 else pr[:, i, P:3 * P]
                            n_ = t * GH + i
                            actf(p_, p_, ACT.Exp, bias=nm[:, n_:n_ + 1], accum_out=rs[:, n_:n_ + 1]).then_inc(*AC.mark(step, "exp", t, i))
                    fill(step, 1)
                    fill(step, 2)
                    for b in range(3):
                        act.wait_ge(*PE(step, "probs turned", b))
                        copy(prT[:, :, b * P:(b + 1) * P], Q[b][:].rearrange("p (h d) -> p h d", h=GH)).then_inc(*AC.mark(step, "probs", b))
                    fill(step, 3)
                    for b in range(2):
                        act.wait_ge(*PE(step, "out", b))
                        copy(yH[:, gr * GH + 2 * b:gr * GH + 2 * b + 2, :], Q[3 if b == 0 else 0][:].rearrange("p (h d) -> p h d", h=2)).then_inc(*AC.mark(step, "hi", b))
                elif kind in ("z", "ga", "gb"):
                    c = step[1]
                    act.wait_ge(*fed(step))
                    dst = {"z": z, "ga": gs, "gb": gsb}[kind]
                    fn = ACT.Silu if kind == "z" else ACT.Sigmoid
                    banks = {"z": ((2, 3), (0, 1)), "ga": ((2, 3), (2, 3)), "gb": ((0, 2), (1, 3))}[kind][c]
                    for t in range(NT):
                        last = actf(dst[:, t, c * 512:(c + 1) * 512], L[banks[t]][:], fn)
                    last.then_inc(*AC.mark(step))
                elif kind == "inv":
                    fill(step, 0)
                    for l in range(1, LEVELS):
                        if l > 1:
                            fill(step, l - 1)
                        for t in range(NT):
                            act.wait_ge(*PE(step, "X", l, t))
                            copy(X[:, t], (Q[(t + 2) % 4] if l % 2 else Q[t])[:].rearrange("p (h d) -> p h d", h=GH)).then_inc(*AC.mark(step, "X", l, t))
                    fill(step, LEVELS - 1)
                    fill(step, LEVELS)
                elif kind == "scan":
                    for t in range(NT):
                        act.wait_ge(*PE(step, "u", t))
                        copy(vn[:, t], Q[t][:].rearrange("p (h d) -> p h d", h=GH)).then_inc(*AC.mark(step, "u", t))
                    act.wait_ge(*PE(step, "wT"))
                    copy(wT[:], Q[2][:].rearrange("p (h d) -> p h d", h=GH)).then_inc(*AC.mark(step, "wT"))
                    act.wait_ge(*PE(step, "S"))
                    copy(S[:], Q[3][:].rearrange("p (h d) -> p h d", h=GH)).then_inc(*AC.mark(step, "S"))
                    gr = step[1]
                    for t in range(NT):
                        act.wait_ge(*PE(step, "o", t))
                        ot = o[:, t, gr * 512:(gr + 1) * 512].rearrange("p (h d) -> p h d", h=GH)
                        copy(ot, Q[t][:].rearrange("p (h d) -> p h d", h=GH)).then_inc(*AC.mark(step, "o", t))
                        act.wait_ge(*AC(step, "o", t))
                        if t == 1:
                            act.wait_ge(*VE(step, "sum", 0))
                        actf(sq[:], ot, ACT.Square).then_inc(*AC.mark(step, "sq", t))
                elif kind == "mem":
                    load("mem", mem[:], tokens(a["mem_2"][0]), PE(("scan", 1), "o", 1), AC(("scan", 1), "u", 1))
                    load("lnm", lnm[:], row(a["g_mem_2"], D), VE(("inv", 1), "TT", LEVELS - 1, 1))
                    act.wait_ge(landed["mem"], 16)
                    act.wait_ge(*PE(("scan", 1), "u", 1))
                    for t in range(NT):
                        actf(xv[:, t, :], mem[:, t, :], ACT.Square, accum_out=ss[:, 4 + t:5 + t]).then_inc(*AC.mark(step, "ss", t))
                    hi_wide(step, mH, KD)
                elif kind == "yb":
                    hi_wide(step, yH, KD)
                elif kind == "p":
                    load("p", pt[:], tokens(a["p"][0, 0]), VE(("yb",), "lo", 3))
                    load("lnp", lnp[:], row(a["ln_ple"][0], D))
                    load("xres", h[:], tokens(a["x"][0]), VE(("proj_b",), "sum", 1))
                    load("gA_mix", gA[:], row(a["ln_post_mix"][0], D))
                    load("gB_mix", gB[:], row(a["ln_pre_ffn"][0], D), PE(("att", 1), "out", 1))
                    hi_wide(step, pH, 2)
                elif kind == "merge":
                    hi_wide(step, uH, KD)
                elif kind == "ple":
                    act.wait_ge(*fed(step))
                    for t in range(NT):
                        for c in range(2):
                            actf(e[:, t, c * 512:(c + 1) * 512], Q[2 * t + c][:], ACT.Square, accum_out=ss_p[:, 2 * t + c:2 * t + c + 1]).then_inc(*AC.mark(step, "ss", t, c))
                elif kind == "xkv":
                    c = step[1]
                    act.wait_ge(*fed(step))
                    for t in range(NT):
                        dst = xk[c][:, t, :] if c < 2 else xv[:, t, (c - 2) * 512:(c - 1) * 512]
                        actf(dst, Q[t][:], ACT.Copy, scale=rstd_m[:, t:t + 1]).then_inc(*AC.mark(step, t))
                    if c < 2:
                        for j in range(2):
                            act.wait_ge(*PE(step, "turned", j))
                            copy(xkT[:, 4 * c + 2 * j:4 * c + 2 * j + 2, :], Q[2 + j][:].rearrange("p (k n) -> p k n", k=2)).then_inc(*AC.mark(step, "turned", j))
                elif kind == "norm":
                    what = step[1]
                    src_step = {"mix": ("w_out",), "ffn1": ("down", 1), "ple": ("ple_gate",), "mix2": ("out2",), "x": ("xo",),
                                "ffn2": ("down", 2)}[what]
                    if what in ("ffn1", "ffn2"):
                        act.wait_ge(*PE(("ffn", 1 if what == "ffn1" else 2, 5), "turned", 0))
                    for t in range(NT):
                        for c in range(2):
                            b = 2 * t + c
                            act.wait_ge(*(PE(src_step, "bank", b) if b < 3 else fed(src_step)))
                            out_ = tmp[:, t, c * 512:(c + 1) * 512]
                            if what == "ple":
                                actf(out_, L[b][:], ACT.Sigmoid).then_inc(*AC.mark(step, "gate", t, c))
                            else:
                                actf(out_, L[b][:], ACT.Square, accum_out=ss[:, b:b + 1]).then_inc(*AC.mark(step, "ss", t, c))
                elif kind == "next":
                    what = step[1]
                    hi_wide(step, uH, KD)
                    if what != "ffn1":
                        for t in range(NT):
                            act.wait_ge(*VE(("norm", what), "next", t, 1))
                            actf(tmp[:, t, :], h[:, t, :], ACT.Square, accum_out=ss[:, 4 + t:5 + t]).then_inc(*AC.mark(step, "hss", t))
                    if what == "mix":
                        load("gA_ffn1", gA[:], row(a["ln_post_ffn"][0], D), VE(("norm", what), "next", 1, 1))
                    if what == "ffn1":
                        load("gB_ple", gB[:], row(a["g_mix_pre_2"], D), VE(("norm", what), "next", 1, 1))
                        load("gA_mix2", gA[:], row(a["g_mix_post_2"], D))
                    if what == "ple":
                        load("gB_mix2", gB[:], row(a["g_x_pre_2"], D), VE(("norm", what), "next", 1, 1))
                        load("poolm", poolm[:].rearrange("p a b c -> p (a b c)"), a["pool_table"], fed(("down", 1)))
                        load("wpool", wpool[:], a["w_pool_2"].rearrange("g c d -> c g d"))
                        load("gsub", gsub[:], row(a["g_subln_2"], HD))
                        for n, v_ in enumerate(("lambda_q1_2", "lambda_k1_2", "lambda_q2_2", "lambda_k2_2")):
                            act.dma_start(lamv[:, n, :], row(a[v_], 64)).then_inc(landed["lamv"], 16)
                        load("pos", pos_i[:], a["positions_2"][0].rearrange("(t p) -> p t", p=P), fed(("ple",)), allow_slow_non_contiguous=True)
                        load("psc", psr[:], a["pool_scale_2"].rearrange("(g c) -> g c", c=P))
                    if what == "mix2":
                        load("gA_x", gA[:], row(a["g_x_post_2"], D), VE(("norm", what), "next", 1, 1))
                        load("gB_x", gB[:], row(a["g_ffn_pre_2"], D))
                    if what == "x":
                        load("gA_ffn2", gA[:], row(a["g_ffn_post_2"], D), VE(("norm", what), "next", 1, 1))
                elif kind == "ffn":
                    _, blk, c = step
                    n = 512 if c < 5 else 256
                    act.wait_ge(*fed(step, (LAST[step] + 1 - FIRST[step]) // 2))
                    if c > 0:
                        act.wait_ge(*VE(("ffn", blk, c - 1), "hidden", 1))
                    else:
                        act.wait_ge(*VE(("next", "mix" if blk == 1 else "x"), "rstd"))
                    for t in range(NT):
                        actf(sil[:, t, 0:n], L[t][:, 0:n], ACT.Silu, scale=rstd_h[:, t:t + 1]).then_inc(*AC.mark(step, "silu", t))
                    todo = ([c - 1] if c > 0 else []) + ([5] if c == 5 else [])
                    for c_ in todo:
                        prev = ("ffn", blk, c_)
                        if c_ == 5:
                            pass
                        for j in range(2 if c_ < 5 else 1):
                            act.wait_ge(*PE(prev, "turned", j))
                            bank = Q[2 * ((c_ + 1) % 2) + j]
                            copy(hH[:, 4 * c_ + 2 * j:4 * c_ + 2 * j + 2, :], bank[:].rearrange("p (k n) -> p k n", k=2)).then_inc(*AC.mark(prev, "hi", j))
                elif kind == "in2":
                    c = step[1]
                    act.wait_ge(*fed(step))
                    if c == 0:
                        act.wait_ge(*VE(("next", "ple"), "rstd"))
                    for t in range(NT):
                        src = L[2 * (c % 2) + t][:]
                        if c < 2:
                            dst, src = qk2[:, t, c, :, :], src.rearrange("p (h d) -> p h d", h=2 * GH)
                        elif c == 2:
                            dst, src = v2[:, t, :, :], src.rearrange("p (h d) -> p h d", h=GH)
                        else:
                            dst = u2[:, t, :]
                        actf(dst, src, ACT.Copy, scale=rstd_h[:, t:t + 1]).then_inc(*AC.mark(step, t))
                elif kind == "diff":
                    act.wait_ge(*VE(step, "angles"))
                    actf(sn, sn, ACT.Sin).then_inc(*AC.mark(step, "sin"))
                    actf(cs, cs, ACT.Sin).then_inc(*AC.mark(step, "cos"))
                    act.wait_ge(*VE(step, "lam sums"))
                    actf(lam[:, 0:2], lam[:, 0:2], ACT.Exp).then_inc(*AC.mark(step, "lam"))
                    outs = [dqT[:, 0:2, :], dqT[:, 2:4, :], dkT[:, 0:2, :], dkT[:, 2:4, :]]
                    for b in range(4):
                        act.wait_ge(*PE(step, "turned", b))
                        copy(outs[b], Q[b][:].rearrange("p (h d) -> p h d", h=2)).then_inc(*AC.mark(step, "heads", b))
                    for m in range(2):
                        act.wait_ge(*VE(step, "max", m))
                        for t in range(NT):
                            for i in range(GH):
                                p_ = pd[m][:, i, 0:P] if t == 0 else pd[m][:, i, P:3 * P]
                                n_ = m * 8 + t * GH + i
                                actf(p_, p_, ACT.Exp, bias=nm[:, n_:n_ + 1], accum_out=rs[:, n_:n_ + 1]).then_inc(*AC.mark(step, "exp", m, t, i))
                    for b in range(3):
                        act.wait_ge(*PE(step, "probs turned", b))
                        copy(pdT[:, :, b * P:(b + 1) * P], Q[b][:].rearrange("p (h d) -> p h d", h=GH)).then_inc(*AC.mark(step, "probs", b))
                    for t in range(NT):
                        act.wait_ge(*PE(step, "out", t))
                        bank = Q[3] if t == 0 else L[0]
                        copy(da[:, t], bank[:].rearrange("p (h d) -> p h d", h=GH)).then_inc(*AC.mark(step, "out", t))
                        act.wait_ge(*AC(step, "out", t))
                        if t == 1:
                            act.wait_ge(*VE(step, "sum", 0))
                        actf(dsq[:], da[:, t], ACT.Square).then_inc(*AC.mark(step, "sq", t))
                elif kind == "pool":
                    for b in range(2):
                        act.wait_ge(*PE(step, "pooled", b))
                        copy(poolT[:, 2 * b:2 * b + 2, :], L[2 + b][:].rearrange("p (k n) -> p k n", k=2)).then_inc(*AC.mark(step, "pooled", b))
                    act.wait_ge(*VE(step, "scale"))
                    for b in range(2):
                        act.wait_ge(*PE(step, "out", b))
                        for i in range(2):
                            gi = 2 * b + i
                            actf(uH[:, 4 + gi, :], Q[b][:, i * SEQ:(i + 1) * SEQ], ACT.Copy, scale=psc[:, gi:gi + 1]).then_inc(*AC.mark(step, "hi", gi))
                elif kind == "dnorm":
                    for j in range(2):
                        act.wait_ge(*PE(step, "turned", j))
                        copy(uH[:, 2 * j:2 * j + 2, :], Q[2 + j][:].rearrange("p (k n) -> p k n", k=2)).then_inc(*AC.mark(step, "hi", j))
                elif kind == "xq":
                    act.wait_ge(*fed(step))
                    act.wait_ge(*VE(("next", "mix2"), "rstd"))
                    for t in range(NT):
                        for c in range(2):
                            actf(cq[:, t, c * 512:(c + 1) * 512], L[2 * t + c][:], ACT.Copy, scale=rstd_h[:, t:t + 1]).then_inc(*AC.mark(step, t, c))
                elif kind == "cross":
                    for j in (1, 3):
                        act.wait_ge(*PE(step, "turned", j))
                        copy(cqT[:, 2 * j:2 * j + 2, :], Q[j][:].rearrange("p (k n) -> p k n", k=2)).then_inc(*AC.mark(step, "heads", j))
                    for t in range(NT):
                        act.wait_ge(*VE(step, "max", t))
                        for i in range(GH):
                            n_ = t * GH + i
                            actf(cp[:, t, i, :], L[2 * t + i // 2][:, (i % 2) * SEQ:(i % 2 + 1) * SEQ], ACT.Exp, scale=1.0 / 16,
                                 bias=nm[:, n_:n_ + 1], accum_out=rs[:, n_:n_ + 1]).then_inc(*AC.mark(step, "exp", t, i))
                    for t in range(NT):
                        for j in range(2):
                            act.wait_ge(*PE(step, "probs turned", t, j))
                            copy(cpT[:, j, :, t * P:(t + 1) * P], Q[2 * t + j][:].rearrange("p (h d) -> p h d", h=GH)).then_inc(*AC.mark(step, "probs", t, j))
                    for j in range(4):
                        act.wait_ge(*PE(step, "out", j))
                        copy(uH[:, 2 * j:2 * j + 2, :], L[j][:].rearrange("p (k n) -> p k n", k=2)).then_inc(*AC.mark(step, "hi", j))

        @block.vector
        def _(dve):
            V = nc.vector

            def v(ins, *name):
                ins.then_inc(*VE.mark(*name))
                dve.wait_ge(vector_done, VE.n)

            def tt(out_, x_, y_, op, *name):
                v(V.tensor_tensor(out_, x_, y_, op), *name)

            def ts(out_, x_, s1, s2_, op0, op1, *name):
                if op1 is None:
                    v(V.tensor_scalar(out_, x_, s1, None, op0), *name)
                else:
                    v(V.tensor_scalar(out_, x_, s1, s2_, op0, op1), *name)

            def stt(out_, x_, s_, y_, op0, op1, *name):
                v(V.scalar_tensor_tensor(out=out_, in0=x_, scalar=s_, in1=y_, op0=op0, op1=op1), *name)

            def rsqrt(dst, src, *name):
                n = src.shape[1]
                t_ = rt[:, 0:n]
                ts(dst.bitcast(I32), src.bitcast(I32), -0.5, 1597463007.0, ALU.mult, ALU.add)
                for i in range(3):
                    stt(t_, src, -0.5, dst, ALU.mult, ALU.mult)
                    tt(t_, t_, dst, ALU.mult)
                    stt(dst, t_, 1.5, dst, ALU.add, ALU.mult, *(name if i == 2 else ()))

            def lo_wide(step, dH, dL, k_tiles):
                for j in range(k_tiles // 2):
                    dve.wait_ge(*AC(step, "hi", j))
                    tt(dL[:, 2 * j:2 * j + 2, :], Q[j % 4][:].rearrange("p (k n) -> p k n", k=2), dH[:, 2 * j:2 * j + 2, :].bitcast(F32),
                       ALU.subtract, step, "lo", j)

            def heads(bank, n=GH):
                return bank[:].rearrange("p (h d) -> p h d", h=n)

            for step in SCHEDULE:
                kind = step[0]
                if kind == "u":
                    dve.wait_ge(*AC(step, "ss", 1))
                    ts(rv[:, 0:2], ss[:, 0:2], 1.0 / D, EPS, ALU.mult, ALU.add)
                    rsqrt(rstd0, rv[:, 0:2])
                    dve.wait_ge(landed["ln0"], 16)
                    for t in range(NT):
                        stt(xn0[:, t, :], x0[:, t, :], rstd0[:, t:t + 1], ln0[:], ALU.mult, ALU.mult, step, "scaled", t)
                    lo_wide(step, uH, uL, KD)
                elif kind == "ba":
                    dve.wait_ge(landed["ba"], 16)
                    bv = ba_raw.rearrange("p (k n) -> p k n", k=KD)
                    v(V.tensor_copy(baH[:], bv))
                    tt(baL[:], bv, baH[:].bitcast(F32), ALU.subtract, step, "split")
                    dve.wait_ge(*PE(step, "taps"))
                    v(V.tensor_copy(cw, Q[1][:, 0:CONV * 24]))
                    dve.wait_ge(*PE(step))
                    v(V.tensor_copy(ba, Q[0][:, 0:32]), step, "ba")
                    bav = ba.rearrange("p (t n) -> p t n", t=NT)
                    tAv = tA.rearrange("p (t n) -> p t n", t=NT)
                    dve.wait_ge(landed["dtb"], 16)
                    tt(tAv, bav[:, :, 8:16], each(dtb, NT), ALU.add)
                    ts(tB, tA, -1.0, None, ALU.mult, None)
                    tt(tB, tB, tA, ALU.max, step, "abs")
                    dve.wait_ge(*AC(step, "exp"))
                    ts(tB, tB, 1.0, None, ALU.add, None, step, "1+exp")
                    ts(tA, tA, 0.0, None, ALU.max, None)
                    dve.wait_ge(*AC(step, "ln"))
                    tt(tA, tA, tB, ALU.add)
                    gv = g.rearrange("p (t n) -> p t n", t=NT)
                    ts(tA, tA, -1.0, None, ALU.mult, None)
                    tt(gv, tAv, each(alog, NT), ALU.mult, step, "g")
                elif kind == "conv":
                    _, gr, part = step
                    cwv = cw.rearrange("p (j t) -> p j t", j=CONV)
                    if part == 0 and gr == 1:
                        dve.wait_ge(*PE(("feat", 0), "kk", 1, 1))
                    for ct in range(4):
                        if ct % 2 == 0:
                            dve.wait_ge(*(PE(step, "half") if ct == 0 else fed(step)))
                        tile = part * 8 + gr * GH + ct
                        src = L[2 * (part % 2) + ct // 2][:, (ct % 2) * SEQ:(ct % 2 + 1) * SEQ]
                        dst = C[:, part * GH + ct, :]
                        ts(dst, src, cwv[:, 3, tile:tile + 1], None, ALU.mult, None)
                        for back in range(1, CONV):
                            j = CONV - 1 - back
                            name = (step, "taps done") if back == CONV - 1 and ct == 3 else ()
                            stt(dst[:, back:SEQ], src[:, 0:SEQ - back], cwv[:, j, tile:tile + 1], dst[:, back:SEQ], ALU.mult, ALU.add, *name)
                elif kind == "tok":
                    s2v = s2.rearrange("p (t a h) -> p t a h", t=NT, a=2)
                    for part in range(2):
                        for t in range(NT):
                            dve.wait_ge(*AC(step, "sq", part, t))
                            v(V.tensor_reduce(s2v[:, t, part, :], sq[:], AX.X, ALU.add), step, "sum", part, t)
                    ts(s2, s2, EPS, None, ALU.add, None)
                    rsqrt(rq, s2)
                    rqv = rq.rearrange("p (t a h) -> p t a h", t=NT, a=2)
                    ts(rqv[:, :, 0, :], rqv[:, :, 0, :], float(HD) ** -0.5, None, ALU.mult, None, step, "rq")
                elif kind == "moba":
                    _, gr, part = step
                    if part == 2:
                        continue
                    dve.wait_ge(*fed(step))
                    if gr == 1 and part == 0:
                        dve.wait_ge(*PE(("att", 0), "turned", 3))
                    b0 = 2 * (part % 2)
                    for t in range(NT):
                        src = heads(L[b0 + t])
                        dst = mtok[:, part, t]
                        r_ = sqr[:]
                        tt(dst, src, each(cos1[:, t, :], GH), ALU.mult)
                        tt(r_[:, :, 0:64], src[:, :, 64:128], each(sin1[:, t, 0:64], GH), ALU.mult)
                        tt(r_[:, :, 64:128], src[:, :, 0:64], each(sin1[:, t, 64:128], GH), ALU.mult)
                        tt(dst, dst, r_, ALU.add, step, "rope", t)
                elif kind == "feat":
                    gr = step[1]
                    rqv = rq.rearrange("p (t a h) -> p t a h", t=NT, a=2)
                    bet = beta.rearrange("p (t n) -> p t n", t=NT)[:, :, gr * GH:(gr + 1) * GH]
                    gv = g.rearrange("p (t n) -> p t n", t=NT)[:, :, gr * GH:(gr + 1) * GH]
                    gcv = gc.rearrange("p (t h) -> p t h", t=NT)
                    egv = eg.rearrange("p (t h) -> p t h", t=NT)
                    if gr == 1:
                        dve.wait_ge(*PE(("scan", 0), "o", 1))
                    for t in range(NT):
                        tt(trg[:, t], each(tri, GH), over(gv[:, t, :], P), ALU.mult, step, "tri g", t)
                    dve.wait_ge(*PE(step, "gc"))
                    v(V.tensor_copy(gcv, Q[3][:, 0:16].rearrange("p (t h) -> p t h", t=NT)[:, :, 0:GH]), step, "gc")
                    for t in range(NT):
                        dve.wait_ge(*PE(step, "rows", t))
                        if t == 0:
                            tt(edec, heads(Q[0])[:, :, P - 1], gcv[:, 0, :], ALU.subtract, step, "glast")
                        tt(Dm[:, t], heads(Q[t]), over(gcv[:, t, :], P), ALU.subtract)
                        tt(Dm[:, t], Dm[:, t], each(neg_kq, GH), ALU.add, step, "decay log", t)
                    dve.wait_ge(*AC(("tok", gr), "out", 2, 1))
                    dve.wait_ge(*AC(("ba",), "beta"))
                    for t in range(NT):
                        tt(tok[:, t, 1], tok[:, t, 1], over(rqv[:, t, 1, :], HD), ALU.mult, step, "kn", t)
                        tt(kb[:, t], tok[:, t, 1], over(bet[:, t, :], HD), ALU.mult, step, "kb", t)
                        tt(tok[:, t, 0], tok[:, t, 0], over(rqv[:, t, 0, :], HD), ALU.mult, step, "qn", t)
                    dve.wait_ge(*AC(step, "edec"))
                    tt(qe[:], tok[:, 1, 0], over(egv[:, 1, :], HD), ALU.mult, step, "qe", 1)
                    tt(kbe[:], kb[:, 1], over(egv[:, 1, :], HD), ALU.mult)
                    tt(kdec[:], tok[:, 0, 1], over(edec, HD), ALU.mult)
                    for t in range(NT):
                        tt(tok[:, t, 2], tok[:, t, 2], over(bet[:, t, :], HD), ALU.mult)
                    for t in range(NT):
                        dve.wait_ge(*AC(step, "decay", t))
                        for pair in range(2):
                            dve.wait_ge(*PE(step, "kk", t, pair))
                            kk_ = Q[2 * t + pair][:].rearrange("p (i a d) -> p i a d", i=2, a=2)
                            hs = slice(2 * pair, 2 * pair + 2)
                            tt(AT[:, t, hs], kk_[:, :, 0, :], Dm[:, t, hs], ALU.mult)
                            tt(aT[:, t, hs], kk_[:, :, 1, :], Dm[:, t, hs], ALU.mult, step, "attn", t, pair)
                elif kind == "att":
                    gr = step[1]
                    scale = float(HD) ** -0.5
                    dve.wait_ge(*PE(step, "scores", 0))
                    stt(pr[:, :, 0:P], heads(Q[0]), scale, each(neg_qk, GH), ALU.mult, ALU.add)
                    v(V.tensor_reduce(mx[:, 0:GH], pr[:, :, 0:P], AX.X, ALU.max))
                    for pair in range(2):
                        dve.wait_ge(*PE(step, "scores", 1 + pair))
                        src, hs = heads(Q[1 + pair], 2), slice(2 * pair, 2 * pair + 2)
                        ts(pr[:, hs, P:2 * P], src[:, :, 0:P], scale, None, ALU.mult, None)
                        stt(pr[:, hs, 2 * P:3 * P], src[:, :, P:SEQ], scale, each(neg_qk, 2), ALU.mult, ALU.add)
                    v(V.tensor_reduce(mx[:, GH:2 * GH], pr[:, :, P:3 * P], AX.X, ALU.max))
                    ts(nm[:, 0:8], mx[:, 0:8], -1.0, None, ALU.mult, None, step, "max")
                    dve.wait_ge(*AC(step, "exp", 1, 3))
                    v(V.reciprocal(ri[:, 0:8], rs[:, 0:8]))
                    tt(pr[:, :, 0:P], pr[:, :, 0:P], over(ri[:, 0:GH], P), ALU.mult)
                    tt(pr[:, :, P:3 * P], pr[:, :, P:3 * P], over(ri[:, GH:2 * GH], 2 * P), ALU.mult, step, "probs")
                    for b in range(2):
                        dve.wait_ge(*AC(step, "hi", b))
                        k0 = gr * GH + 2 * b
                        tt(yL[:, k0:k0 + 2, :], heads(Q[3 if b == 0 else 0], 2), yH[:, k0:k0 + 2, :].bitcast(F32), ALU.subtract, step, "lo", b)
                elif kind == "inv":
                    gr = step[1]

                    def mask(l):
                        tt(M[:].rearrange("p t h d -> p (t h) d"), AT[:].rearrange("p t h d -> p (t h) d"), each(square(2 + l), NT * GH),
                           ALU.mult, step, "mask", l)

                    dve.wait_ge(*PE(("att", gr), "out", 1))
                    mask(0)
                    for t in range(NT):
                        dve.wait_ge(*PE(step, "M0", t))
                        tt(T[:, t], each(ident, GH), heads(Q[t]), ALU.subtract)
                        tt(TT[:, t], each(ident, GH), M[:, t], ALU.subtract, step, "TT", 0, t)
                    for l in range(1, LEVELS):
                        mask(l)
                        A = [Q[2], Q[3], Q[0], Q[1]] if l % 2 else Q
                        for t in range(NT):
                            if l < LEVELS - 1:
                                dve.wait_ge(*PE(step, "Y", l, t))
                                tt(T[:, t], T[:, t], heads(A[2] if t == 0 else A[0]), ALU.subtract)
                            dve.wait_ge(*PE(step, "YT", l, t))
                            tt(TT[:, t], TT[:, t], heads(A[3] if t == 0 else A[1]), ALU.subtract, step, "TT", l, t)
                elif kind == "scan":
                    gr = step[1]
                    dve.wait_ge(*AC(step, "u", 1))
                    dve.wait_ge(*PE(step, "wS"))
                    tt(vn[:, 1], vn[:, 1], heads(Q[2]), ALU.subtract, step, "vn")
                    for t in range(NT):
                        dve.wait_ge(*AC(step, "sq", t))
                        v(V.tensor_reduce(so[:, t * 8 + gr * GH:t * 8 + (gr + 1) * GH], sq[:], AX.X, ALU.add), step, "sum", t)
                elif kind == "proj_a":
                    dve.wait_ge(*fed(step))
                    dve.wait_ge(*AC(("ga", 1)))
                    for t in range(NT):
                        for c in range(2):
                            gt = gs[:, t, c * 512:(c + 1) * 512]
                            tt(gt, gt, L[2 * t + c][:], ALU.mult, step, "mul", 2 * t + c)
                elif kind == "proj_b":
                    dve.wait_ge(*fed(step))
                    dve.wait_ge(*AC(("gb", 1)))
                    for t in range(NT):
                        for c in range(2):
                            gt, bt = gs[:, t, c * 512:(c + 1) * 512], gsb[:, t, c * 512:(c + 1) * 512]
                            tt(bt, bt, L[2 * t + c][:], ALU.mult)
                            tt(gt, gt, bt, ALU.add, *((step, "sum", t) if c == 1 else ()))
                elif kind == "mem":
                    dve.wait_ge(landed["mem"], 16)
                    dve.wait_ge(landed["lnm"], 16)
                    dve.wait_ge(*AC(step, "ss", 1))
                    ts(rv[:, 0:2], ss[:, 4:6], 1.0 / D, EPS, ALU.mult, ALU.add)
                    rsqrt(rstd_m, rv[:, 0:2], step, "rstd")
                    tt(mem[:], mem[:], each(lnm[:], NT), ALU.mult, step, "scaled")
                    lo_wide(step, mH, mL, KD)
                elif kind == "yb":
                    ts(so, so, 1.0 / HD, EPS, ALU.mult, ALU.add)
                    rsqrt(rq, so)
                    dve.wait_ge(landed["gnorm"], 16)
                    dve.wait_ge(*AC(("z", 1)))
                    for t in range(NT):
                        ot = o[:, t, :].rearrange("p (h d) -> p h d", h=8)
                        tt(ot, ot, over(rq[:, t * 8:(t + 1) * 8], HD), ALU.mult)
                        tt(ot, ot, each(gnorm, 8), ALU.mult)
                        tt(o[:, t, :], o[:, t, :], z[:, t, :], ALU.mult, step, "y", t)
                    lo_wide(step, yH, yL, KD)
                elif kind == "p":
                    lo_wide(step, pH, pL, 2)
                elif kind == "merge":
                    lo_wide(step, uH, uL, KD)
                elif kind == "ple":
                    dve.wait_ge(*AC(step, "ss", 1, 1))
                    tt(rv[:, 0:2], ss_p[:, 0:4:2], ss_p[:, 1:4:2], ALU.add)
                    ts(rv[:, 0:2], rv[:, 0:2], 1.0 / D, EPS, ALU.mult, ALU.add)
                    rsqrt(rstd_p, rv[:, 0:2])
                    dve.wait_ge(landed["lnp"], 16)
                    for t in range(NT):
                        for c in range(2):
                            cc = slice(c * 512, (c + 1) * 512)
                            stt(e[:, t, cc], Q[2 * t + c][:], rstd_p[:, t:t + 1], lnp[:, cc], ALU.mult, ALU.mult, step, "e", 2 * t + c)
                elif kind == "norm":
                    what = step[1]
                    post, pre = RES[what]
                    if post:
                        dve.wait_ge(*AC(step, "ss", 1, 1))
                        tt(rv[:, 0:2], ss[:, 0:4:2], ss[:, 1:4:2], ALU.add)
                        ts(rv[:, 0:2], rv[:, 0:2], 1.0 / D, EPS, ALU.mult, ALU.add)
                        rsqrt(rstd_o, rv[:, 0:2])
                        dve.wait_ge(landed["gA_" + what], 16)
                    if what == "mix":
                        dve.wait_ge(landed["xres"], 16)
                    if pre:
                        dve.wait_ge(landed["gB_" + what], 16)
                    for c in range(2):
                        for t in range(NT):
                            cc = slice(c * 512, (c + 1) * 512)
                            if post:
                                stt(tmp[:, t, cc], L[2 * t + c][:], rstd_o[:, t:t + 1], gA[:, cc], ALU.mult, ALU.mult)
                            else:
                                dve.wait_ge(*AC(step, "gate", t, c))
                                tt(tmp[:, t, cc], tmp[:, t, cc], e[:, t, cc], ALU.mult)
                            name = {"ffn1": (step, "next", t, c), "ffn2": ("out", 2 * c + t)}.get(what, ())
                            tt(h[:, t, cc], h[:, t, cc], tmp[:, t, cc], ALU.add, *name)
                            if pre:
                                tt(hg[:, t, cc], h[:, t, cc], gB[:, cc], ALU.mult, step, "next", t, c)
                elif kind == "next":
                    lo_wide(step, uH, uL, KD)
                    if step[1] != "ffn1":
                        dve.wait_ge(*AC(step, "hss", 1))
                        ts(rv[:, 0:2], ss[:, 4:6], 1.0 / D, EPS, ALU.mult, ALU.add)
                        rsqrt(rstd_h, rv[:, 0:2], step, "rstd")
                elif kind == "ffn":
                    _, blk, c = step
                    n = 512 if c < 5 else 256

                    def low(c_, j):
                        prev = ("ffn", blk, c_)
                        dve.wait_ge(*AC(prev, "hi", j))
                        k0 = 4 * c_ + 2 * j
                        tt(hL[:, k0:k0 + 2, :], heads(Q[2 * ((c_ + 1) % 2) + j], 2), hH[:, k0:k0 + 2, :].bitcast(F32), ALU.subtract, prev, "lo", j)

                    if c > 0:
                        low(c - 1, 0)
                        low(c - 1, 1)
                    dve.wait_ge(*fed(step))
                    for t in range(NT):
                        dve.wait_ge(*AC(step, "silu", t))
                        stt(hm[:, t, 0:n], L[2 + t][:, 0:n], rstd_h[:, t:t + 1], sil[:, t, 0:n], ALU.mult, ALU.mult, step, "hidden", t)
                    if c == 5:
                        low(5, 0)
                elif kind == "diff":
                    dve.wait_ge(landed["pos"], 16)
                    ang3, kk3 = (q_.rearrange("p (t n) -> p t n", t=NT) for q_ in (ang, kk))
                    v(V.tensor_copy(posf, pos_i[:]))
                    tt(ang3, over(posf, ROPE2), each(inv2, NT), ALU.mult)
                    ts(kk, ang, 1.0 / (2 * np.pi), MAGIC, ALU.mult, ALU.add)
                    ts(kk, kk, MAGIC, None, ALU.subtract, None)
                    stt(sn, kk, -TWO_PI[0], ang, ALU.mult, ALU.add)
                    stt(sn, kk, -TWO_PI[1], sn, ALU.mult, ALU.add)
                    stt(sn, kk, -TWO_PI[2], sn, ALU.mult, ALU.add)
                    ts(cs, sn, float(np.pi / 2), None, ALU.add, None)
                    ts(kk, cs, float(np.pi), -2 * float(np.pi), ALU.is_gt, ALU.mult)
                    tt(cs, cs, kk, ALU.add)
                    ts(sn, sn, 3.1415925, -3.1415925, ALU.min, ALU.max)
                    ts(cs, cs, 3.1415925, -3.1415925, ALU.min, ALU.max, step, "angles")
                    dve.wait_ge(landed["lamv"], 64)
                    for n in range(2):
                        tt(lamv[:, 2 * n, :], lamv[:, 2 * n, :], lamv[:, 2 * n + 1, :], ALU.mult)
                        v(V.tensor_reduce(lam[:, n:n + 1], lamv[:, 2 * n, :], AX.X, ALU.add), *((step, "lam sums") if n else ()))
                    dve.wait_ge(*AC(("in2", 1), 1))
                    dve.wait_ge(*AC(step, "cos"))
                    sn3, cs3 = (q_.rearrange("p (t n) -> p t n", t=NT) for q_ in (sn, cs))
                    for t in range(NT):
                        x_ = qk2[:, t].rearrange("p a h d -> p (a h) d")
                        x1, x2 = x_[:, :, 0:ROPE2], x_[:, :, ROPE2:2 * ROPE2]
                        c_, s_ = each(cs3[:, t, :], 4 * GH), each(sn3[:, t, :], 4 * GH)
                        q4 = [r2t[n][:].rearrange("p (h d) -> p h d", d=ROPE2) for n in range(4)]
                        tt(q4[0], x1, c_, ALU.mult)
                        tt(q4[1], x2, s_, ALU.mult)
                        tt(q4[2], x2, c_, ALU.mult)
                        tt(q4[3], x1, s_, ALU.mult)
                        tt(x1, q4[0], q4[1], ALU.subtract)
                        tt(x2, q4[2], q4[3], ALU.add, *((step, "rope") if t else ()))
                    banks = [[Q[0], Q[1], Q[2]], [Q[3], L[0], L[1]]]
                    for m in range(2):
                        p_ = pd[m]
                        dve.wait_ge(*PE(step, "scores", m, 0))
                        stt(p_[:, :, 0:P], heads(banks[m][0]), 0.125, each(neg_qk, GH), ALU.mult, ALU.add)
                        v(V.tensor_reduce(mx[:, 8 * m:8 * m + GH], p_[:, :, 0:P], AX.X, ALU.max))
                        for pair in range(2):
                            dve.wait_ge(*PE(step, "scores", m, 1 + pair))
                            src, hs = heads(banks[m][1 + pair], 2), slice(2 * pair, 2 * pair + 2)
                            ts(p_[:, hs, P:2 * P], src[:, :, 0:P], 0.125, None, ALU.mult, None)
                            stt(p_[:, hs, 2 * P:3 * P], src[:, :, P:SEQ], 0.125, each(neg_qk, 2), ALU.mult, ALU.add)
                        v(V.tensor_reduce(mx[:, 8 * m + GH:8 * m + 8], p_[:, :, P:3 * P], AX.X, ALU.max))
                        ts(nm[:, 8 * m:8 * m + 8], mx[:, 8 * m:8 * m + 8], -1.0, None, ALU.mult, None, step, "max", m)
                    dve.wait_ge(*AC(step, "lam"))
                    tt(lam[:, 2:3], lam[:, 0:1], lam[:, 1:2], ALU.subtract)
                    ts(lam[:, 2:3], lam[:, 2:3], LAM_INIT, None, ALU.add, None)
                    for m in range(2):
                        dve.wait_ge(*AC(step, "exp", m, 1, 3))
                        v(V.reciprocal(ri[:, 8 * m:8 * m + 8], rs[:, 8 * m:8 * m + 8]))
                        if m == 1:
                            ts(ri[:, 8:16], ri[:, 8:16], lam[:, 2:3], None, ALU.mult, None)
                        tt(pd[m][:, :, 0:P], pd[m][:, :, 0:P], over(ri[:, 8 * m:8 * m + GH], P), ALU.mult)
                        tt(pd[m][:, :, P:3 * P], pd[m][:, :, P:3 * P], over(ri[:, 8 * m + GH:8 * m + 8], 2 * P), ALU.mult)
                    tt(pd[0][:], pd[0][:], pd[1][:], ALU.subtract, step, "probs")
                    for t in range(NT):
                        dve.wait_ge(*AC(step, "sq", t))
                        v(V.tensor_reduce(mx[:, t * GH:(t + 1) * GH], dsq[:], AX.X, ALU.add), step, "sum", t)
                elif kind == "pool":
                    dve.wait_ge(*PE(step, "scale"))
                    v(V.tensor_copy(psc, Q[2][:, 0:4]), step, "scale")
                    for gi in range(4):
                        dve.wait_ge(*AC(step, "hi", gi | 1))
                        stt(uL[:, 4 + gi, :], Q[gi // 2][:, (gi % 2) * SEQ:(gi % 2 + 1) * SEQ], psc[:, gi:gi + 1], uH[:, 4 + gi, :].bitcast(F32),
                            ALU.mult, ALU.subtract, step, "lo", gi)
                elif kind == "dnorm":
                    ts(rv[:, 0:8], mx[:, 0:8], 1.0 / HD, EPS, ALU.mult, ALU.add)
                    rsqrt(r1, rv[:, 0:8])
                    dve.wait_ge(landed["gsub"], 16)
                    ts(gsub[:], gsub[:], 1.0 - LAM_INIT, None, ALU.mult, None)
                    dav = da[:].rearrange("p t h d -> p (t h) d")
                    tt(dav, dav, over(r1, HD), ALU.mult)
                    tt(dav, dav, each(gsub[:], NT * GH), ALU.mult, step, "da")
                    for j in range(2):
                        dve.wait_ge(*AC(step, "hi", j))
                        tt(uL[:, 2 * j:2 * j + 2, :], heads(Q[2 + j], 2), uH[:, 2 * j:2 * j + 2, :].bitcast(F32), ALU.subtract, step, "lo", j)
                elif kind == "cross":
                    for j in (0, 2):
                        dve.wait_ge(*PE(step, "turned", j))
                        v(V.tensor_copy(cqT[:, 2 * j:2 * j + 2, :], heads(Q[j], 2)), step, "heads", j)
                    for t in range(NT):
                        for pair in range(2):
                            dve.wait_ge(*PE(step, "scores", t, pair))
                            n_ = t * GH + 2 * pair
                            v(V.tensor_reduce(mx[:, n_:n_ + 2], heads(L[2 * t + pair], 2), AX.X, ALU.max))
                        ts(nm[:, t * GH:(t + 1) * GH], mx[:, t * GH:(t + 1) * GH], -1.0 / 16, None, ALU.mult, None, step, "max", t)
                    for t in range(NT):
                        dve.wait_ge(*AC(step, "exp", t, 3))
                        v(V.reciprocal(ri[:, t * GH:(t + 1) * GH], rs[:, t * GH:(t + 1) * GH]))
                        tt(cp[:, t], cp[:, t], over(ri[:, t * GH:(t + 1) * GH], SEQ), ALU.mult, step, "probs", t)
                    for j in range(4):
                        dve.wait_ge(*AC(step, "hi", j))
                        tt(uL[:, 2 * j:2 * j + 2, :], heads(L[j], 2), uH[:, 2 * j:2 * j + 2, :].bitcast(F32), ALU.subtract, step, "lo", j)

    return {"pe": PE.names, "act": AC.names, "dve": VE.names}


_INS = ["x", "p", "ln_pre_mix", "w_in", "conv_w", "a_log", "dt_bias", "gdn_norm", "w_proj_a", "w_proj_b", "w_out",
        "ln_post_mix", "ln_pre_ffn", "w_ffn_gate", "w_ffn_up", "w_ffn_down", "ln_post_ffn", "w_ple", "ln_ple", "w_ple_gate",
        "mem_2", "positions_2", "g_mix_pre_2", "w_in_2", "lambda_q1_2", "lambda_k1_2", "lambda_q2_2", "lambda_k2_2",
        "g_subln_2", "w_pool_2", "pool_scale_2", "w_out_2", "g_mix_post_2", "g_x_pre_2", "g_mem_2", "w_xq_2", "w_xkv_2",
        "w_xo_2", "g_x_post_2", "g_ffn_pre_2", "w_gate_2", "w_up_2", "w_down_2", "g_ffn_post_2"]


def kernel(**inputs):
    import concourse.bacc as bacc
    from concourse.bass_utils import run_bass_kernel_spmd

    arrays = {f"in_{n}": np.ascontiguousarray(inputs[n]) for n in _INS}
    arrays["in_table"], arrays["in_pool_table"] = constant_tables()

    def program(known):
        nc = bacc.Bacc("TRN2", target_bir_lowering=False, num_devices=1)
        a = {k[3:]: nc.dram_tensor(k, v.shape, mybir.dt.from_np(v.dtype), kind="ExternalInput").ap() for k, v in arrays.items()}
        out = nc.dram_tensor("out", (1, SEQ, D), F32, kind="ExternalOutput").ap()
        return nc, build(nc, a, out, known)

    _, known = program({})
    nc, _ = program(known)
    r = run_bass_kernel_spmd(nc, [arrays], core_ids=[0])
    return r.results[0]["out"]
```

```python
from contextlib import ExitStack

import numpy as np

import concourse.bass as bass
from concourse import mybir

F32 = mybir.dt.float32
F32R = mybir.dt.float32r
I32 = mybir.dt.int32
ALU = mybir.AluOpType
ACT = mybir.ActivationFunctionType
AX = mybir.AxisListType

P = 128
SEQ = 256
NT = SEQ // P
D = 1024
KD = D // P
HD = 128
NG = 2
GH = 4
FF = 2816
KF = FF // P
CONV = 4
PLE = 256
EPS = 1e-6
NEG = -3.0e38
LEVELS = 7
LAM_INIT = 0.2
WINDOWS = (2, 4, 8, 16)
RAW, SPLIT = 4, 6
UNIT = 1024
KB = 1024
MAGIC = 1.5 * 2.0 ** 23
TWO_PI = (6.28125, 2029 / 2 ** 20, 2 * np.pi - 6.28125 - 2029 / 2 ** 20)
ROPE2 = 8

COL = {"mq": 0, "mk": D, "mv": 2 * D, "cq": 3 * D, "ck": 4 * D, "cv": 5 * D, "z": 6 * D,
       "ba": 7 * D, "ga": 7 * D + 16, "gb": 8 * D + 16}


def constant_tables():
    i = np.arange(P)
    row, col = i[:, None], i[None, :]
    level = [((row >> l) % 2 == 0) & ((col >> l) == (row >> l) + 1) for l in range(LEVELS)]
    masks = [row == col, row <= col] + level + [np.ones((P, P), bool)]
    square = [m.astype(np.float32) for m in masks]
    square.append(np.where(row <= col, 0, NEG).astype(np.float32))
    square.append(np.where(col <= row, 0, NEG).astype(np.float32))
    inv = (1.0 / (10000.0 ** (np.arange(0, HD, 2, dtype=np.float32) / HD))).astype(np.float32)
    angle = (np.arange(SEQ, dtype=np.float32)[:, None] * inv[None, :]).astype(np.float32)
    cos, sin = np.cos(angle), np.sin(angle)
    cos2 = np.concatenate([cos, cos], 1).reshape(NT, P, HD).transpose(1, 0, 2).reshape(P, -1)
    sin2 = np.concatenate([-sin, sin], 1).reshape(NT, P, HD).transpose(1, 0, 2).reshape(P, -1)
    inv2 = 500000.0 ** (-np.arange(0, 2 * ROPE2, 2, dtype=np.float32) / (2 * ROPE2))
    inv2 = np.broadcast_to(inv2.astype(np.float32), (P, ROPE2))
    table = np.concatenate(square + [cos2, sin2, inv2], 1).astype(np.float32)
    t = np.arange(SEQ)
    pool = []
    for w in WINDOWS:
        seen = (t[:, None] <= t[None, :]) & (t[:, None] > t[None, :] - w)
        mean = seen / np.minimum(t + 1, w)[None, :] - np.eye(SEQ)
        pool.append(mean.reshape(NT, P, SEQ).transpose(1, 0, 2))
    pool = np.stack(pool, 1).reshape(P, -1).astype(np.float32)
    return np.ascontiguousarray(table), np.ascontiguousarray(pool)


class Done:

    def __init__(self, sem, known):
        self.sem, self.known, self.n, self.names = sem, known, 0, {}

    def mark(self, *name):
        self.n += 1
        if name:
            self.names[name] = self.n
        return self.sem, 1

    def __call__(self, *name):
        return self.sem, (self.known[name] if self.known else 1)


def schedule():
    s = [("u",)]
    for gr in range(2):
        s += [("conv", gr, 0)] + ([("ba",)] if gr == 0 else []) + [("conv", gr, 1)] + ([("rates",)] if gr == 0 else [])
        s += [("tri", gr), ("conv", gr, 2), ("decay", gr), ("moba", gr, 0), ("tok", gr), ("moba", gr, 1), ("feat", gr),
              ("moba", gr, 2), ("att", gr)]
        s += [("z", 0), ("inv", 0), ("z", 1), ("ga", 0), ("scan", 0)] if gr == 0 else [("ga", 1), ("inv", 1), ("proj_a",), ("scan", 1)]
    s += [("gb", 0), ("yb",), ("gb", 1), ("p",), ("mem",), ("proj_b",), ("xkv", 0), ("merge",), ("w_out",)]
    s += [("norm", "mix"), ("ple",), ("next", "mix"), ("e",)]
    s += [("ffn", 1, c) for c in range(6)] + [("down", 1), ("norm", "ffn1"), ("xkv", 1), ("next", "ffn1")]
    s += [("ple_gate",), ("norm", "ple"), ("xkv", 2), ("next", "ple")]
    s += [("angles",)] + [("in2", c) for c in range(2)] + [("rope2",), ("in2", 2), ("heads2",), ("in2", 3)]
    s += [("diff",), ("pool",), ("probs",), ("dnorm",), ("out2",), ("norm", "mix2"), ("xkv", 3), ("next", "mix2")]
    s += [("xq",), ("cross",), ("xo",), ("norm", "x"), ("next", "x")]
    s += [("ffn", 2, c) for c in range(6)] + [("down", 2), ("norm", "ffn2")]
    return s


FILLING = {("tok", 0): [("moba", 0, 1)], ("tok", 1): [("moba", 1, 1)], ("feat", 0): [("moba", 0, 2)], ("feat", 1): [("moba", 1, 2)],
           ("att", 0): [("z", 0)], ("inv", 0): [("z", 1), ("ga", 0)],
           ("att", 1): [("ga", 1)], ("inv", 1): [("proj_a",)]}
INSIDE = {f for fs in FILLING.values() for f in fs}

LATE = ("mix", "x")

ROW_ORDER = {("out2",): (4, 5, 6, 7, 0, 1, 2, 3)}

INPUT = {("w_out",): ("merge",), ("ffn", 1, 0): ("next", "mix"), ("ple_gate",): ("next", "ffn1"), ("in2", 0): ("next", "ple"),
         ("xq",): ("next", "mix2"), ("ffn", 2, 0): ("next", "x")}


SCHEDULE = schedule()


def weight_units(w):
    units = []

    def columns(step, m, c0, n=512):
        per = UNIT // n
        for j in range(m.shape[0] // P // per):
            units.append((step, m[j * per * P:(j + 1) * per * P, c0:c0 + n].rearrange("(k p) n -> p k n", p=P)))

    def rows(step, m):
        for k in ROW_ORDER.get(step, range(m.shape[0] // P)):
            units.append((step, m[k * P:(k + 1) * P, :].rearrange("(k p) n -> p k n", p=P)))

    wide = {"proj_a": w["w_proj_a"], "proj_b": w["w_proj_b"], "w_out": w["w_out"], "ple_gate": w["w_ple_gate"],
            "ple": w["w_ple"], "out2": w["w_out_2"], "xq": w["w_xq_2"], "xo": w["w_xo_2"]}
    order = []
    for step in SCHEDULE:
        order += FILLING.get(step, [] if step in INSIDE else [step])
    for step in order:
        kind = step[0]
        if kind == "conv":
            columns(step, w["w_in"], COL["cq"] + step[2] * D + step[1] * 512)
        elif kind == "moba":
            columns(step, w["w_in"], COL["mq"] + step[2] * D + step[1] * 512)
        elif kind in ("z", "ga", "gb"):
            columns(step, w["w_in"], COL[kind] + step[1] * 512)
        elif kind == "xkv":
            columns(step, w["w_xkv_2"], step[1] * 512)
        elif kind == "in2":
            columns(step, w["w_in_2"], step[1] * 512)
        elif kind == "ffn":
            n = 512 if step[2] < FF // 512 else FF % 512
            for m in (("w_ffn_gate", "w_ffn_up") if step[1] == 1 else ("w_gate_2", "w_up_2")):
                columns(step, w[m], step[2] * 512, n)
        elif kind == "down":
            rows(step, w["w_ffn_down"] if step[1] == 1 else w["w_down_2"])
        elif kind in wide:
            rows(step, wide[kind])
    return units


def build(nc, a, out, known):
    w = {n: (a[n][0] if len(a[n].shape) == 3 else a[n]) for n in
         ("w_in", "w_proj_a", "w_proj_b", "w_out", "w_ffn_gate", "w_ffn_up", "w_ffn_down", "w_ple", "w_ple_gate",
          "w_in_2", "w_out_2", "w_xq_2", "w_xkv_2", "w_xo_2", "w_gate_2", "w_up_2", "w_down_2")}
    UNITS = weight_units(w)
    FIRST, LAST = {}, {}
    for n, (step, _) in enumerate(UNITS):
        FIRST.setdefault(step, n)
        LAST[step] = n
    ctx = ExitStack()
    with ctx:
        def sem(name):
            return ctx.enter_context(nc.semaphore(name))

        base = -(-nc.sbuf_base // 32) * 32
        at = [base]

        def place(name, shape, dt=F32, offset=None):
            size = 4 * int(np.prod(shape[1:]))
            if offset is None:
                offset = at[0]
                at[0] += -(-size // 32) * 32
            return nc.alloc_sbuf_tensor_at(name, list(shape), dt, offset=offset)

        raw = place("raw", [P, RAW, UNIT])
        w_hi = place("w_hi", [P, SPLIT, UNIT], F32R)
        w_lo = place("w_lo", [P, SPLIT, UNIT], F32R)
        uH = place("uH", [P, KD, SEQ], F32R)
        uL = place("uL", [P, KD, SEQ], F32R)
        table = place("table", [P, 12 * P + 2 * NT * HD + ROPE2])
        small = place("small", [P, 960])
        Y = at[0]
        yH = place("yH", [P, KD, SEQ], F32R)
        yL = place("yL", [P, KD, SEQ], F32R)
        B = at[0]
        hH = place("hH", [P, KF, SEQ], F32R, Y)
        hL = place("hL", [P, KF, SEQ], F32R, Y + KF * SEQ * 4)

        def big(name, kb, shape, dt=F32):
            return place(name, shape, dt, B + int(kb * KB))

        HALF = [P, NT, GH, HD]
        x0 = big("x0", 0, [P, NT, D])
        z = big("z", 0, [P, NT, D])
        gs = big("gs", 8, [P, NT, D])
        o = big("o", 16, [P, NT, D])
        ln0 = big("ln0", 24, [P, D])
        C = big("C", 24, [P, 3 * GH, SEQ])
        kT = big("kT", 24, HALF)
        kbqT = big("kbqT", 28, [P, NT, GH, 2, HD])
        gsb = big("gsb", 24, [P, NT, D])
        tok = big("tok", 36, [P, NT, 3, GH, HD])
        mtok = big("mtok", 48, [P, 3, NT, GH, HD])
        T = big("T", 60, HALF)
        TT = big("TT", 64, HALF)
        X = big("X", 68, HALF)
        M = big("M", 72, HALF)
        kb = big("kb", 72, HALF)
        vn = big("vn", 76, HALF)
        xn0 = big("xn0", 60, [P, NT, D])
        qTa = big("qTa", 60, [P, GH, SEQ])
        kTa = big("kTa", 64, [P, GH, SEQ])
        pr = big("pr", 68, [P, GH, 3 * P])
        prT = big("prT", 74, [P, GH, 3 * P])
        qeT = big("qeT", 80, [P, GH, HD])
        Dm = big("Dm", 82, HALF)
        AT = big("AT", 86, HALF)
        aT = big("aT", 90, HALF)
        kbe = big("kbe", 94, [P, GH, HD])
        kdec = big("kdec", 96, [P, GH, HD])
        qe = big("qe", 98, [P, GH, HD])
        S = big("S", 72, [P, GH, HD])
        wT = big("wT", 74, [P, GH, HD])
        sq = big("sq", 98, [P, GH, HD])
        sqr = big("sqr", 98, [P, GH, HD])
        h = big("h", 28, [P, NT, D])
        tmp = big("tmp", 36, [P, NT, D])
        sil = big("sil", 36, [P, NT, 512])
        hm = big("hm", 40, [P, NT, 512])
        gA = big("gA", 44, [P, D])
        gB = big("gB", 48, [P, D])
        hg = big("hg", 52, [P, NT, D])
        e = big("e", 60, [P, NT, D])
        mem = big("mem", 60, [P, NT, D])
        xkT = big("xkT", 68, [P, KD, SEQ])
        lnm = big("lnm", 68, [P, D])
        xv = big("xv", 76, [P, NT, D])
        mH = big("mH", 84, [P, KD, SEQ], F32R)
        mL = big("mL", 92, [P, KD, SEQ], F32R)
        pt = big("pt", 16, [P, NT, PLE])
        lnp = big("lnp", 20, [P, D])
        pH = big("pH", 0, [P, PLE // P, SEQ], F32R)
        pL = big("pL", 2, [P, PLE // P, SEQ], F32R)
        xk = [big("xk0", 52, [P, NT, 512]), big("xk1", 20, [P, NT, 512])]
        poolm = big("poolm", 0, [P, 4, NT, SEQ])
        qk2 = big("qk2", 8, [P, NT, 2, 2 * GH, 64])
        v2 = big("v2", 16, [P, NT, GH, HD])
        u2 = big("u2", 20, [P, NT, 512])
        da = big("da", 24, [P, NT, GH, HD])
        dqT = big("dqT", 36, [P, GH, SEQ])
        dkT = big("dkT", 40, [P, GH, SEQ])
        pd = [big("pd0", 52, [P, GH, 3 * P]), big("pd1", 60, [P, GH, 3 * P])]
        pdT = big("pdT", 36, [P, GH, 3 * P])
        poolT = place("poolT", [P, 4, SEQ], F32, Y)
        wpool = place("wpool", [P, 4, P], F32, Y + 4 * KB)
        dsq = place("dsq", [P, GH, HD], F32, Y + 6 * KB)
        gsub = place("gsub", [P, HD], F32, Y + 8 * KB)
        lamv = place("lamv", [P, 4, 64], F32, Y + 9 * KB)
        cq = big("cq", 0, [P, NT, D])
        cqT = big("cqT", 8, [P, KD, SEQ])
        cp = big("cp", 16, [P, NT, GH, SEQ])
        cpT = place("cpT", [P, NT, GH, SEQ], F32, Y)
        used = B + 100 * KB
        assert used <= nc.sbuf_usable_end, (used, nc.sbuf_usable_end)

        def square(n):
            return table[:, n * P:(n + 1) * P]

        ident, tri, ones = square(0), square(1), square(2 + LEVELS)
        neg_kq, neg_qk = square(3 + LEVELS), square(4 + LEVELS)
        base_t = (5 + LEVELS) * P
        cos1 = table[:, base_t:base_t + NT * HD].rearrange("p (t d) -> p t d", t=NT)
        sin1 = table[:, base_t + NT * HD:base_t + 2 * NT * HD].rearrange("p (t d) -> p t d", t=NT)
        inv2 = table[:, base_t + 2 * NT * HD:base_t + 2 * NT * HD + ROPE2]

        free = [0]

        def tiny(n):
            free[0] += n
            assert free[0] <= 960
            return small[:, free[0] - n:free[0]]

        def over(ap, n):
            return ap.unsqueeze(2).to_broadcast([P, ap.shape[1], n])

        def each(ap, n):
            return ap.unsqueeze(1).to_broadcast([P, n, ap.shape[1]])

        ss = tiny(8)
        rv = tiny(16)
        rt = tiny(16)
        rstd0 = tiny(2)
        rstd_m = tiny(2)
        rstd_p = tiny(2)
        rstd_h = tiny(2)
        rstd_o = tiny(2)
        cw = tiny(CONV * 24)
        cwr = tiny(P)
        gnorm = tiny(HD)
        ba_raw = tiny(KD * 16)
        ba = tiny(32)
        dtb, alog = tiny(8), tiny(8)
        beta, g = tiny(16), tiny(16)
        tA, tB = tiny(16), tiny(16)
        ss_p = tA[:, 0:2]
        gc, eg = tiny(8), tiny(8)
        glast, edec = tiny(4), tiny(4)
        s2 = tiny(16)
        rq = tiny(16)
        mx, nm, rs, ri = tiny(16), tiny(16), tiny(16), tiny(16)
        lam = tiny(4)
        posf = tiny(2)
        ang, kk, sn, cs = tiny(16), tiny(16), tiny(16), tiny(16)
        psc = tiny(4)
        r1, so = tiny(8), tiny(16)
        baH = big("baH", 36, [P, KD, 16], F32R)
        baL = big("baL", 37, [P, KD, 16], F32R)
        baT = big("baT", 64, [P, SEQ])
        trg = big("trg", 68, HALF)
        pos_i = place("pos_i", [P, NT], I32, Y + 12 * KB)
        psr = place("psr", [4, P], F32, Y + 12 * KB + 512)
        r2t = [place(f"r2t{n}", [P, 4 * GH * ROPE2], F32, Y + 10 * KB + 512 * n) for n in range(4)]

        L = [ctx.enter_context(nc.psum_tensor(f"L{n}", [P, 512], F32)) for n in range(4)]
        Q = [ctx.enter_context(nc.psum_tensor(f"Q{n}", [P, 512], F32)) for n in range(4)]

        tensor_done, scalar_done, vector_done = sem("tensor_done"), sem("scalar_done"), sem("vector_done")
        w_landed = [sem(f"w_landed{n}") for n in range(RAW)]
        w_hi_there, w_lo_there, w_used = sem("w_hi_there"), sem("w_lo_there"), sem("w_used")
        loads = {}

        def load_sem(name):
            if name not in loads:
                loads[name] = sem(f"{name}_landed")
            return loads[name]

        PE = Done(tensor_done, known.get("pe"))
        AC = Done(scalar_done, known.get("act"))
        VE = Done(vector_done, known.get("dve"))
        load_names = ["x0", "x1", "table", "ln0", "cwr", "ba", "dtb", "alog", "gnorm", "mem", "lnm", "p", "lnp", "xres",
                      "gA_mix", "gA_ffn1", "gA_mix2", "gA_x", "gA_ffn2", "gB_mix", "gB_ple", "gB_mix2", "gB_x",
                      "poolm", "wpool", "gsub", "lamv", "pos", "psc"]
        landed = {n: sem(f"{n}_landed") for n in load_names}
        stored = sem("stored")

        def fed(step, units=None):
            return w_used, (LAST[step] + 1 if units is None else FIRST[step] + units)

        block = ctx.enter_context(nc.Block())

        def tokens(ap):
            return ap.rearrange("(t p) d -> p t d", p=P)

        def row(ap, n):
            return ap.rearrange("(o d) -> o d", o=1).to_broadcast([P, n])

        RES = {"mix": ("ln_post_mix", "ln_pre_ffn"), "ffn1": ("ln_post_ffn", None), "ple": (None, "g_mix_pre_2"),
               "mix2": ("g_mix_post_2", "g_x_pre_2"), "x": ("g_x_post_2", "g_ffn_pre_2"), "ffn2": ("g_ffn_post_2", None)}

        @block.sync
        def _(sp):
            for t in range(NT):
                sp.dma_start(x0[:, t, :], a["x"][0][t * P:(t + 1) * P, :]).then_inc(landed[f"x{t}"], 16)
            sp.dma_start(ln0[:], row(a["ln_pre_mix"][0], D)).then_inc(landed["ln0"], 16)
            for n, (step, src) in enumerate(UNITS):
                if n >= RAW:
                    sp.wait_ge(w_lo_there, n - RAW + 1)
                dst = raw[:, n % RAW, :].rearrange("p (k n) -> p k n", k=src.shape[1])
                sp.dma_start(dst, src).then_inc(w_landed[n % RAW], 16)
            for c in range(2):
                cc = slice(c * 512, (c + 1) * 512)
                sp.wait_ge(*VE("out", 2 * c + 3))
                sp.dma_start(tokens(out[0])[:, :, cc], h[:, :, cc]).then_inc(stored, 16)
            sp.wait_ge(stored, 32)

        @block.gpsimd
        def _(pool):
            for n in range(len(UNITS)):
                pool.wait_ge(w_hi_there, n + 1)
                nc.gpsimd.tensor_tensor(w_lo[:, n % SPLIT, :], raw[:, n % RAW, :], w_hi[:, n % SPLIT, :].bitcast(F32),
                                        ALU.subtract).then_inc(w_lo_there, 1)

        @block.tensor
        def _(pe):
            mm, turn = nc.tensor.matmul, nc.tensor.transpose

            def split_mm(dst, sH, sL, wH, wL, start, stop):
                mm(dst, sH, wH, start=start, stop=False)
                mm(dst, sH, wL, start=False, stop=False)
                return mm(dst, sL, wH, start=False, stop=stop)

            def unit(n, k):
                slot = n % SPLIT
                return (w_hi[:, slot, :].rearrange("p (k n) -> p k n", k=k),
                        w_lo[:, slot, :].rearrange("p (k n) -> p k n", k=k))

            def column_unit(step, j, banks, n0=None, n=512, sH=uH, sL=uL):
                n0 = FIRST[step] if n0 is None else n0
                per = UNIT // n
                pe.wait_ge(w_lo_there, n0 + j + 1)
                wH, wL = unit(n0 + j, per)
                for i in range(per):
                    k = j * per + i
                    if n0 == FIRST[step]:
                        turned(step, k)
                    for t in range(NT):
                        last = split_mm(banks[t][:, 0:n], sH[:, k, t * P:(t + 1) * P], sL[:, k, t * P:(t + 1) * P],
                                        wH[:, i, :], wL[:, i, :], k == 0, k == KD - 1)
                last.then_inc(w_used, 1)

            def columns(step, banks, n0=None, n=512, sH=uH, sL=uL):
                for j in range(KD * n // UNIT):
                    column_unit(step, j, banks, n0, n, sH, sL)

            def row_unit(step, k, sH, sL, k_tiles):
                n0 = FIRST[step]
                turned(step, k)
                pe.wait_ge(w_lo_there, n0 + k + 1)
                wH, wL = unit(n0 + k, 2)
                tile = ROW_ORDER[step][k] if step in ROW_ORDER else k
                for t in range(NT):
                    s_h, s_l = sH[:, tile, t * P:(t + 1) * P], sL[:, tile, t * P:(t + 1) * P]
                    for c in range(2):
                        last = split_mm(L[2 * t + c][:], s_h, s_l, wH[:, c, :], wL[:, c, :], k == 0, k == k_tiles - 1)
                        if k == k_tiles - 1 and 2 * t + c < 3:
                            last.then_inc(*PE.mark(step, "bank", 2 * t + c))
                last.then_inc(w_used, 1)

            def rows(step, sH, sL, k_tiles):
                for k in range(k_tiles):
                    row_unit(step, k, sH, sL, k_tiles)

            inside = {("moba", 0, 1): ([L[0], L[1]], [VE(("conv", 0, 2), "taps done")]),
                      ("moba", 1, 1): ([L[0], L[1]], [VE(("conv", 1, 2), "taps done")]),
                      ("moba", 0, 2): ([L[2], L[3]], [VE(("moba", 0, 0), "rope", 1)]),
                      ("moba", 1, 2): ([L[2], L[3]], [VE(("moba", 1, 0), "rope", 1)]),
                      ("z", 0): ([L[0], L[1]], [VE(("moba", 0, 1), "rope", 1)]),
                      ("z", 1): ([L[2], L[3]], [AC(("moba", 0, 2), "v", 1)]),
                      ("ga", 0): ([L[0], L[1]], [AC(("z", 0))]),
                      ("ga", 1): ([L[0], L[1]], [VE(("moba", 1, 1), "rope", 1)]),
                      ("proj_a",): (L, [AC(("moba", 1, 2), "v", 1), AC(("ga", 1)), VE(("att", 1), "lo", 1)])}

            def fill(step, i):
                n = FIRST[FILLING[step][0]] + i
                f, j = next((f, n - FIRST[f]) for f in FILLING[step] if FIRST[f] <= n <= LAST[f])
                banks, free_ = inside[f]
                if j == 0:
                    for wt in free_:
                        pe.wait_ge(*wt)
                if f == ("proj_a",):
                    row_unit(f, j, yH, yL, KD)
                else:
                    column_unit(f, j, banks)

            def turn_tiles(step, src, tiles, ready):
                for j in tiles:
                    for t in range(NT):
                        pe.wait_ge(*ready(j, t))
                        for i in range(2):
                            last = turn(Q[j][:, i * SEQ + t * P:i * SEQ + (t + 1) * P],
                                        src[:, t, (2 * j + i) * P:(2 * j + i + 1) * P], ident)
                    last.then_inc(*PE.mark(step, "turned", j))

            def turned(step, k):
                if step in INPUT:
                    source = INPUT[step]
                    if k % 2:
                        if k < KD - 1:
                            turn_next(source, k // 2 + 1)
                    else:
                        pe.wait_ge(*VE(source, "lo", k // 2))

            def turn_next(source, j):
                if source == ("merge",):
                    turn_tiles(source, gs, (j,), lambda j, t: VE(("proj_b",), "sum", t, j // 2))
                else:
                    turn_tiles(source, h if source[1] == "ffn1" else hg, (j,),
                               lambda j, t: VE(("norm", source[1]), "next", t, min(j, 2)))

            for step in SCHEDULE:
                kind = step[0]
                if kind == "u":
                    pe.wait_ge(landed["table"], 16)
                    pe.wait_ge(landed["cwr"], 16)
                    turn(L[3][:, 0:CONV * 24], cwr[0:CONV * 24, :], ident[0:CONV * 24, 0:CONV * 24]).then_inc(*PE.mark(step, "taps"))
                    turn_tiles(step, xn0, range(4), lambda j, t: VE(("u",), "scaled", t))
                elif step in INSIDE:
                    continue
                elif kind == "ba":
                    pe.wait_ge(*VE(("u",), "split"))
                    for k in range(KD):
                        mm(Q[0][0:16, 0:SEQ], baH[:, k, :], uH[:, k, :], start=k == 0, stop=False)
                        mm(Q[0][0:16, 0:SEQ], baH[:, k, :], uL[:, k, :], start=False, stop=False)
                        last = mm(Q[0][0:16, 0:SEQ], baL[:, k, :], uH[:, k, :], start=False, stop=k == KD - 1)
                    last.then_inc(*PE.mark(step))
                elif kind == "rates":
                    pe.wait_ge(*VE(("ba",), "turned"))
                    for t in range(NT):
                        last = turn(Q[1][:, t * 16:t * 16 + 16], baT[0:16, t * P:(t + 1) * P], ident[0:16, 0:16])
                    last.then_inc(*PE.mark(step))
                elif kind == "conv":
                    _, gr, part = step
                    n0 = FIRST[step]
                    b0 = 2 * (part % 2)
                    if part == 2:
                        pe.wait_ge(*VE(("conv", gr, 0), "taps done"))
                    elif gr == 1:
                        pe.wait_ge(*AC(("ga", 0) if part == 0 else ("z", 1)))
                    for ct in range(4):
                        for k in range(KD):
                            if gr == 0 and part == 0 and ct == 0 and k % 2 == 0:
                                pe.wait_ge(*VE(("u",), "lo", k // 2))
                            if ct == 0 and k % 2 == 0:
                                pe.wait_ge(w_lo_there, n0 + k // 2 + 1)
                            wH, wL = unit(n0 + k // 2, 2)
                            bank = L[b0 + ct // 2][:, (ct % 2) * SEQ:(ct % 2 + 1) * SEQ]
                            sH, sL = wH[:, k % 2, ct * P:(ct + 1) * P], wL[:, k % 2, ct * P:(ct + 1) * P]
                            mm(bank, sH, uH[:, k, :], start=k == 0, stop=False)
                            mm(bank, sH, uL[:, k, :], start=False, stop=False)
                            last = mm(bank, sL, uH[:, k, :], start=False, stop=k == KD - 1)
                            if ct == 3 and k % 2 == 1:
                                last.then_inc(w_used, 1)
                        if ct == 1:
                            last.then_inc(*PE.mark(step, "half"))
                elif kind == "tok":
                    gr = step[1]
                    for part in range(3):
                        for t in range(NT):
                            b = part * NT + t
                            pe.wait_ge(*AC(("conv", gr, part), "silu"))
                            if b == 4:
                                fill(step, 0)
                            if b >= 4:
                                pe.wait_ge(*AC(step, "out", (b - 4) // NT, (b - 4) % NT))
                            elif b == 0:
                                pe.wait_ge(*VE(("decay", gr), "decay log", 1))
                            for i in range(GH):
                                last = turn(Q[b % 4][:, i * P:(i + 1) * P], C[:, part * GH + i, t * P:(t + 1) * P], ident)
                            last.then_inc(*PE.mark(step, "turned", part, t))
                    for i in range(1, 4):
                        fill(step, i)
                elif kind == "moba":
                    _, gr, part = step
                    pe.wait_ge(*VE(("conv", gr, 1 + part), "taps done"))
                    columns(step, [L[2 - 2 * part], L[3 - 2 * part]])
                elif kind == "decay":
                    gr = step[1]
                    pe.wait_ge(*(VE(("rates",), "g") if gr == 0 else AC(("scan", 0), "o", 1)))
                    for t in range(NT):
                        last = mm(Q[3][:, t * 8:t * 8 + GH], tri, g[:, t * 8 + gr * GH:t * 8 + gr * GH + GH], start=True, stop=True)
                    last.then_inc(*PE.mark(step, "gc"))
                    for t in range(NT):
                        pe.wait_ge(*VE(("tri", gr), t))
                        mm(Q[t][:], ones, trg[:, t, :, :].rearrange("p h d -> p (h d)"), start=True, stop=True).then_inc(*PE.mark(step, "rows", t))
                elif kind == "feat":
                    gr = step[1]
                    fill(step, 0)
                    pe.wait_ge(*AC(("tok", gr), "out", 2, 1))
                    lots = [("kn", 0), ("kb", 0), ("qn", 0), ("kn", 1), ("kb", 1), ("qn", 1), ("qe", 1)]
                    src = {"kn": lambda t, i: tok[:, t, 1, i, :], "kb": lambda t, i: kb[:, t, i, :],
                           "qn": lambda t, i: tok[:, t, 0, i, :], "qe": lambda t, i: qe[:, i, :]}
                    for b, (what, t) in enumerate(lots):
                        if b == 4:
                            fill(step, 1)
                        pe.wait_ge(*VE(step, what, t))
                        if b >= 4:
                            pe.wait_ge(*AC(step, "out", b - 4))
                        for i in range(GH):
                            last = turn(Q[b % 4][:, i * P:(i + 1) * P], src[what](t, i), ident)
                        last.then_inc(*PE.mark(step, "turned", b))
                    fill(step, 2)
                    pe.wait_ge(*AC(step, "out", 6))
                    for t in range(NT):
                        for i in range(GH):
                            last = mm(Q[2 * t + i // 2][:, (i % 2) * 256:(i % 2 + 1) * 256], kT[:, t, i, :],
                                      kbqT[:, t, i, :, :].rearrange("p a b -> p (a b)"), start=True, stop=True)
                            if i % 2:
                                last.then_inc(*PE.mark(step, "kk", t, i // 2))
                    fill(step, 3)
                elif kind == "att":
                    gr = step[1]
                    for b in range(4):
                        part, pair = b // 2, b % 2
                        pe.wait_ge(*VE(("moba", gr, part), "rope", 1))
                        pe.wait_ge(*VE(("feat", gr), "attn", 1, 1))
                        for i in range(2):
                            for t in range(NT):
                                last = turn(Q[b][:, i * SEQ + t * P:i * SEQ + (t + 1) * P], mtok[:, part, t, 2 * pair + i, :], ident)
                        last.then_inc(*PE.mark(step, "turned", b))
                    fill(step, 0)
                    pe.wait_ge(*AC(step, "heads", 3))
                    for i in range(GH):
                        last = mm(Q[0][:, i * P:(i + 1) * P], qTa[:, i, 0:P], kTa[:, i, 0:P], start=True, stop=True)
                    last.then_inc(*PE.mark(step, "scores", 0))
                    for i in range(GH):
                        last = mm(Q[1 + i // 2][:, (i % 2) * SEQ:(i % 2 + 1) * SEQ], qTa[:, i, P:SEQ], kTa[:, i, :], start=True, stop=True)
                        if i % 2:
                            last.then_inc(*PE.mark(step, "scores", 1 + i // 2))
                    fill(step, 1)
                    fill(step, 2)
                    for b, j in enumerate((0, 1, 2)):
                        pe.wait_ge(*VE(step, "probs"))
                        for i in range(GH):
                            last = turn(Q[b][:, i * P:(i + 1) * P], pr[:, i, j * P:(j + 1) * P], ident)
                        last.then_inc(*PE.mark(step, "probs turned", b))
                    fill(step, 3)
                    pe.wait_ge(*AC(("moba", gr, 2), "v", 1))
                    pe.wait_ge(*AC(step, "probs", 2))
                    for i in range(GH):
                        bank = Q[3 if i < 2 else 0]
                        c0 = (i % 2) * SEQ
                        mm(bank[:, c0:c0 + SEQ], mtok[:, 2, 0, i, :], prT[:, i, 0:SEQ], start=True, stop=False)
                        last = mm(bank[:, c0 + P:c0 + SEQ], mtok[:, 2, 1, i, :], prT[:, i, SEQ:3 * P], start=False, stop=True)
                        if i % 2:
                            last.then_inc(*PE.mark(step, "out", i // 2))
                elif kind == "gb":
                    c = step[1]
                    pe.wait_ge(*VE(("proj_a",), "mul", 2 + c))
                    columns(step, [L[c], L[2 + c]])
                elif kind == "proj_b":
                    pe.wait_ge(*AC(("gb", 1)))
                    pe.wait_ge(*VE(("yb",), "lo", 3))
                    rows(step, yH, yL, KD)
                elif kind == "inv":
                    gr = step[1]
                    fill(step, 0)
                    pe.wait_ge(*VE(step, "mask", 0))
                    pe.wait_ge(*VE(("att", gr), "lo", 1))
                    for t in range(NT):
                        for i in range(GH):
                            last = turn(Q[t][:, i * P:(i + 1) * P], M[:, t, i, :], ident)
                        last.then_inc(*PE.mark(step, "M0", t))
                    fill(step, 1)
                    for l in range(1, LEVELS):
                        pe.wait_ge(*VE(step, "mask", l))
                        A = [Q[2], Q[3], Q[0], Q[1]] if l % 2 else Q
                        for t in range(NT):
                            pe.wait_ge(*VE(step, "T", l - 1, t))
                            for i in range(GH):
                                last = mm(A[t][:, i * P:(i + 1) * P], M[:, t, i, :], T[:, t, i, :], start=True, stop=True)
                            last.then_inc(*PE.mark(step, "X", l, t))
                        if l > 1:
                            for t in range(NT):
                                for i in range(GH):
                                    last = turn(A[2 + t][:, i * P:(i + 1) * P], T[:, t, i, :], ident)
                                last.then_inc(*PE.mark(step, "turned", l, t))
                        fill(step, l + 1)
                        for t in range(NT):
                            pe.wait_ge(*AC(step, "X", l, t))
                            if l > 1:
                                pe.wait_ge(*AC(step, "TT", l, t))
                            for i in range(GH):
                                one, other = (TT, X) if l < LEVELS - 1 else (X, TT)
                                last = mm(A[t][:, i * P:(i + 1) * P], one[:, t, i, :], other[:, t, i, :], start=True, stop=True)
                            last.then_inc(*PE.mark(step, "Y", l, t))
                elif kind == "scan":
                    gr = step[1]
                    iv = ("inv", gr)
                    pe.wait_ge(*VE(iv, "TT", LEVELS - 1, 1))
                    for t in range(NT):
                        for i in range(GH):
                            last = mm(Q[t][:, i * P:(i + 1) * P], TT[:, t, i, :], tok[:, t, 2, i, :], start=True, stop=True)
                        last.then_inc(*PE.mark(step, "u", t))
                    for i in range(GH):
                        last = mm(Q[2][:, i * P:(i + 1) * P], kbe[:, i, :], TT[:, 1, i, :], start=True, stop=True)
                    last.then_inc(*PE.mark(step, "wT"))
                    pe.wait_ge(*AC(step, "u", 0))
                    for i in range(GH):
                        last = mm(Q[3][:, i * P:(i + 1) * P], kdec[:, i, :], vn[:, 0, i, :], start=True, stop=True)
                    last.then_inc(*PE.mark(step, "S"))
                    for i in range(GH):
                        last = mm(Q[0][:, i * P:(i + 1) * P], aT[:, 0, i, :], vn[:, 0, i, :], start=True, stop=True)
                    last.then_inc(*PE.mark(step, "o", 0))
                    pe.wait_ge(*AC(step, "S"))
                    for i in range(GH):
                        last = mm(Q[2][:, i * P:(i + 1) * P], wT[:, i, :], S[:, i, :], start=True, stop=True)
                    last.then_inc(*PE.mark(step, "wS"))
                    pe.wait_ge(*VE(step, "vn"))
                    for i in range(GH):
                        mm(Q[1][:, i * P:(i + 1) * P], qeT[:, i, :], S[:, i, :], start=True, stop=False)
                        last = mm(Q[1][:, i * P:(i + 1) * P], aT[:, 1, i, :], vn[:, 1, i, :], start=False, stop=True)
                    last.then_inc(*PE.mark(step, "o", 1))
                elif kind == "mem":
                    pe.wait_ge(*VE(("yb",), "lo", 3))
                    turn_tiles(step, mem, range(4), lambda j, t: VE(("mem",), "scaled") if j < 3 else VE(("p",), "lo"))
                elif kind == "yb":
                    pe.wait_ge(*AC(("scan", 1), "o", 1))
                    turn_tiles(step, o, range(4), lambda j, t: VE(("yb",), "y", t))
                elif kind == "p":
                    pe.wait_ge(landed["p"], 16)
                    for i in range(2):
                        for t in range(NT):
                            pe.wait_ge(*VE(("yb",), "lo", 3))
                            last = turn(Q[3][:, i * SEQ + t * P:i * SEQ + (t + 1) * P], pt[:, t, i * P:(i + 1) * P], ident)
                    last.then_inc(*PE.mark(step, "turned"))
                elif kind == "merge":
                    pe.wait_ge(*AC(("xkv", 0), 1))
                    turn_next(step, 0)
                    pe.wait_ge(*AC(("xkv", 0), "turned", 1))
                elif kind == "w_out":
                    rows(step, uH, uL, KD)
                elif kind == "ple":
                    pe.wait_ge(*VE(("merge",), "lo", 3))
                    for k in range(2):
                        n = FIRST[step] + k
                        pe.wait_ge(w_lo_there, n + 1)
                        wH, wL = unit(n, 2)
                        for t in range(NT):
                            for c in range(2):
                                last = split_mm(Q[2 * t + c][:], pH[:, k, t * P:(t + 1) * P], pL[:, k, t * P:(t + 1) * P],
                                                wH[:, c, :], wL[:, c, :], k == 0, k == 1)
                        last.then_inc(w_used, 1)
                elif kind == "xkv":
                    c = step[1]
                    before = {0: VE(("mem",), "lo", 3), 1: VE(("ffn", 1, 5), "lo", 0), 2: VE(("next", "ffn1"), "lo", 3),
                              3: VE(("dnorm",), "lo", 1)}
                    pe.wait_ge(*before[c])
                    columns(step, [Q[0], Q[1]], sH=mH, sL=mL)
                    if c < 2:
                        pe.wait_ge(*AC(step, 1))
                        for j in range(2):
                            for i in range(2):
                                for t in range(NT):
                                    last = turn(Q[2 + j][:, i * SEQ + t * P:i * SEQ + (t + 1) * P],
                                                xk[c][:, t, (2 * j + i) * P:(2 * j + i + 1) * P], ident)
                            last.then_inc(*PE.mark(step, "turned", j))
                elif kind == "next":
                    what = step[1]
                    through = {"mix": AC(("ple",), "out", 3), "ffn1": AC(("xkv", 1), "turned", 1), "ple": AC(("xkv", 2), 1),
                               "mix2": AC(("xkv", 3), 1)}
                    if what in through:
                        pe.wait_ge(*through[what])
                    turn_next(step, 0)
                elif kind == "ffn":
                    _, blk, c = step
                    n = 512 if c < 5 else 256
                    half = (LAST[step] + 1 - FIRST[step]) // 2
                    if c > 0:
                        pe.wait_ge(*AC(("ffn", blk, c - 1), "silu", 1))
                    columns(step, [L[0], L[2]], n=n)
                    if c > 0:
                        prev = ("ffn", blk, c - 1)
                        pe.wait_ge(*VE(prev, "hidden", 1))
                        for j in range(2):
                            for i in range(2):
                                for t in range(NT):
                                    last = turn(Q[2 * (c % 2) + j][:, i * SEQ + t * P:i * SEQ + (t + 1) * P],
                                                hm[:, t, (2 * j + i) * P:(2 * j + i + 1) * P], ident)
                            last.then_inc(*PE.mark(prev, "turned", j))
                    if c == 0:
                        pe.wait_ge(*VE(("norm", "mix" if blk == 1 else "x"), "next", 1, 2))
                    columns(step, [L[1], L[3]], FIRST[step] + half, n)
                elif kind == "down":
                    blk = step[1]
                    prev = ("ffn", blk, 5)
                    pe.wait_ge(*VE(prev, "hidden", 1))
                    for k in range(KF):
                        if k == 1:
                            for i in range(2):
                                for t in range(NT):
                                    last = turn(Q[0][:, i * SEQ + t * P:i * SEQ + (t + 1) * P], hm[:, t, i * P:(i + 1) * P], ident)
                            last.then_inc(*PE.mark(prev, "turned", 0))
                        elif k == KF - 2:
                            pe.wait_ge(*VE(prev, "lo", 0))
                        row_unit(step, k, hH, hL, KF)
                elif kind == "ple_gate":
                    rows(step, uH, uL, KD)
                elif kind == "in2":
                    c = step[1]
                    if c >= 2:
                        pe.wait_ge(*AC(("in2", c - 2), 1))
                    b0 = 2 * (c % 2)
                    columns(step, [L[b0], L[b0 + 1]])
                elif kind == "heads2":
                    pe.wait_ge(*VE(("rope2",), "rope"))
                    pe.wait_ge(*VE(("next", "ple"), "lo", 3))
                    for b in range(4):
                        part, pair = b // 2, b % 2
                        for i in range(2):
                            for t in range(NT):
                                hh = 2 * pair + i
                                last = turn(Q[b][:, i * SEQ + t * P:i * SEQ + (t + 1) * P],
                                            qk2[:, t, part, 2 * hh:2 * hh + 2, :].rearrange("p m d -> p (m d)"), ident)
                        last.then_inc(*PE.mark(step, "turned", b))
                elif kind == "diff":
                    pe.wait_ge(*AC(("heads2",), "heads", 3))
                    pe.wait_ge(*AC(("in2", 3), 1))
                    banks = [[Q[0], Q[1], Q[2]], [Q[3], L[0], L[1]]]
                    for m in range(2):
                        lo, hi = 64 * m, 64 * m + 64
                        for i in range(GH):
                            last = mm(banks[m][0][:, i * P:(i + 1) * P], dqT[lo:hi, i, 0:P], dkT[lo:hi, i, 0:P], start=True, stop=True)
                        last.then_inc(*PE.mark(step, "scores", m, 0))
                        for i in range(GH):
                            last = mm(banks[m][1 + i // 2][:, (i % 2) * SEQ:(i % 2 + 1) * SEQ], dqT[lo:hi, i, P:SEQ], dkT[lo:hi, i, :],
                                      start=True, stop=True)
                            if i % 2:
                                last.then_inc(*PE.mark(step, "scores", m, 1 + i // 2))
                    pe.wait_ge(landed["poolm"], 16)
                    for b in range(2):
                        for i in range(2):
                            gi = 2 * b + i
                            mm(L[2 + b][:, i * SEQ:(i + 1) * SEQ], u2[:, 0, gi * P:(gi + 1) * P], poolm[:, gi, 0, :], start=True, stop=False)
                            last = mm(L[2 + b][:, i * SEQ + P:(i + 1) * SEQ], u2[:, 1, gi * P:(gi + 1) * P], poolm[:, gi, 1, P:SEQ],
                                      start=False, stop=True)
                        last.then_inc(*PE.mark(("pool",), "pooled", b))
                elif kind == "pool":
                    pe.wait_ge(landed["wpool"], 16)
                    pe.wait_ge(landed["psc"], 16)
                    pe.wait_ge(*VE(("diff",), "max", 0))
                    turn(Q[2][:, 0:4], psr[:, :], ident[0:4, 0:4]).then_inc(*PE.mark(step, "scale"))
                    for b in range(2):
                        pe.wait_ge(*AC(step, "pooled", b))
                        for i in range(2):
                            gi = 2 * b + i
                            last = mm(Q[b][:, i * SEQ:(i + 1) * SEQ], wpool[:, gi, :], poolT[:, gi, :], start=True, stop=True)
                        last.then_inc(*PE.mark(step, "out", b))
                    pe.wait_ge(*VE(("diff",), "max", 1))
                    for k in range(2):
                        pe.wait_ge(*VE(step, "lo", k))
                        row_unit(("out2",), k, uH, uL, KD)
                elif kind == "probs":
                    pe.wait_ge(*VE(step, "probs"))
                    for j in range(3):
                        for i in range(GH):
                            last = turn(Q[j][:, i * P:(i + 1) * P], pd[0][:, i, j * P:(j + 1) * P], ident)
                        last.then_inc(*PE.mark(step, "probs turned", j))
                    pe.wait_ge(*VE(("pool",), "lo", 2))
                    row_unit(("out2",), 2, uH, uL, KD)
                    pe.wait_ge(*AC(step, "probs", 2))
                    for t in range(NT):
                        bank = Q[3] if t == 0 else Q[0]
                        for i in range(GH):
                            o_ = bank[:, i * P:(i + 1) * P]
                            last = mm(o_, pdT[:, i, t * P:(t + 1) * P], v2[:, 0, i, :], start=True, stop=t == 0)
                            if t == 1:
                                last = mm(o_, pdT[:, i, 2 * P:3 * P], v2[:, 1, i, :], start=False, stop=True)
                        last.then_inc(*PE.mark(step, "out", t))
                elif kind == "dnorm":
                    pe.wait_ge(*VE(("pool",), "lo", 3))
                    row_unit(("out2",), 3, uH, uL, KD)
                    for j in range(2):
                        pe.wait_ge(*VE(step, "da"))
                        for i in range(2):
                            for t in range(NT):
                                last = turn(Q[2 + j][:, i * SEQ + t * P:i * SEQ + (t + 1) * P], da[:, t, 2 * j + i, :], ident)
                        last.then_inc(*PE.mark(step, "turned", j))
                elif kind == "out2":
                    for k in range(4, KD):
                        if k % 2 == 0:
                            pe.wait_ge(*VE(("dnorm",), "lo", k // 2 - 2))
                        row_unit(step, k, uH, uL, KD)
                elif kind == "xq":
                    rows(step, uH, uL, KD)
                elif kind == "cross":
                    for j in range(4):
                        for t in range(NT):
                            pe.wait_ge(*AC(("xq",), t, j // 2))
                            for i in range(2):
                                last = turn(Q[j][:, i * SEQ + t * P:i * SEQ + (t + 1) * P],
                                            cq[:, t, (2 * j + i) * P:(2 * j + i + 1) * P], ident)
                        last.then_inc(*PE.mark(step, "turned", j))
                    pe.wait_ge(*AC(step, "heads", 3))
                    pe.wait_ge(*VE(step, "heads", 2))
                    for t in range(NT):
                        for i in range(GH):
                            bank = L[2 * t + i // 2][:, (i % 2) * SEQ:(i % 2 + 1) * SEQ]
                            for k in range(2):
                                last = mm(bank, cqT[:, 2 * i + k, t * P:(t + 1) * P], xkT[:, 2 * i + k, :], start=k == 0, stop=k == 1)
                            if i % 2:
                                last.then_inc(*PE.mark(step, "scores", t, i // 2))
                    for t in range(NT):
                        pe.wait_ge(*VE(step, "probs", t))
                        for j in range(2):
                            for i in range(GH):
                                last = turn(Q[2 * t + j][:, i * P:(i + 1) * P], cp[:, t, i, j * P:(j + 1) * P], ident)
                            last.then_inc(*PE.mark(step, "probs turned", t, j))
                    pe.wait_ge(*AC(step, "probs", 1, 1))
                    for j in range(4):
                        for i in range(2):
                            for k in range(NT):
                                last = mm(L[j][:, i * SEQ:(i + 1) * SEQ], xv[:, k, (2 * j + i) * P:(2 * j + i + 1) * P], cpT[:, k, j, :],
                                          start=k == 0, stop=k == 1)
                        last.then_inc(*PE.mark(step, "out", j))
                elif kind == "xo":
                    pe.wait_ge(*VE(("cross",), "lo", 3))
                    rows(step, uH, uL, KD)

        @block.scalar
        def _(act):
            made = [0]
            copy, actf = nc.scalar.copy, nc.scalar.activation

            def split_up_to(n):
                while made[0] < min(n, len(UNITS)):
                    u = made[0]
                    act.wait_ge(w_landed[u % RAW], 16 * (u // RAW + 1))
                    if u >= SPLIT:
                        act.wait_ge(w_used, u - SPLIT + 1)
                    copy(w_hi[:, u % SPLIT, :], raw[:, u % RAW, :]).then_inc(w_hi_there, 1)
                    made[0] += 1

            def hi_wide(step, dst, tiles=range(4)):
                for j in tiles:
                    act.wait_ge(*PE(step, "turned", j))
                    copy(dst[:, 2 * j:2 * j + 2, :], Q[j][:].rearrange("p (k n) -> p k n", k=2)).then_inc(*AC.mark(step, "hi", j))

            def hi_next(step, then):
                n = UNIT // UNITS[FIRST[then]][1].shape[2]
                for j in range(4):
                    if j > 0:
                        split_up_to(FIRST[then] + (2 * j - 1) // n + SPLIT - 1)
                    hi_wide(step, uH, (j,))

            def load(name, dst, src, *waits, **how):
                for wt in waits:
                    act.wait_ge(*wt)
                act.dma_start(dst, src, **how).then_inc(landed[name], 16)

            def fill(step, i):
                split_up_to(FIRST[FILLING[step][0]] + i + SPLIT)

            load("table", table[:], a["table"])
            load("cwr", cwr[0:CONV * 24, :], a["conv_w"][0].rearrange("j (t c) -> (j t) c", c=P))
            load("ba", ba_raw.rearrange("p (k n) -> p k n", k=KD),
                 w["w_in"][:, COL["ba"]:COL["ba"] + 16].rearrange("(k p) n -> p k n", p=P))
            load("dtb", dtb, row(a["dt_bias"][0], 8))
            load("alog", alog, row(a["a_log"][0], 8))
            load("gnorm", gnorm, row(a["gdn_norm"][0], HD))
            consumed = 0
            for step in SCHEDULE:
                kind = step[0]
                if step in LAST:
                    consumed = max(consumed, LAST[step] + 1)
                if kind != "u" and kind != "ffn":
                    split_up_to(consumed + SPLIT - 1)
                if kind == "u":
                    for t in range(NT):
                        act.wait_ge(landed[f"x{t}"], 16)
                        actf(xn0[:, t, :], x0[:, t, :], ACT.Square, accum_out=ss[:, t:t + 1]).then_inc(*AC.mark(step, "ss", t))
                    for j in range(4):
                        split_up_to(j + 2)
                        hi_wide(step, uH, (j,))
                elif kind == "rates":
                    act.wait_ge(*VE(step, "ba"))
                    bav = ba.rearrange("p (t n) -> p t n", t=NT)
                    actf(beta.rearrange("p (t n) -> p t n", t=NT), bav[:, :, 0:8], ACT.Sigmoid).then_inc(*AC.mark(step, "beta"))
                    act.wait_ge(landed["alog"], 16)
                    actf(alog, alog, ACT.Exp).then_inc(*AC.mark(step, "alog"))
                    act.wait_ge(*VE(step, "abs"))
                    actf(tB, tB, ACT.Exp, scale=-1.0).then_inc(*AC.mark(step, "exp"))
                    act.wait_ge(*VE(step, "1+exp"))
                    actf(tB, tB, ACT.Ln).then_inc(*AC.mark(step, "ln"))
                elif kind == "conv":
                    _, gr, part = step
                    act.wait_ge(*VE(step, "taps done"))
                    cv = C[:, part * GH:(part + 1) * GH, :]
                    actf(cv, cv, ACT.Silu).then_inc(*AC.mark(step, "silu"))
                elif kind == "decay":
                    act.wait_ge(*VE(step, "gc"))
                    actf(eg, gc, ACT.Exp).then_inc(*AC.mark(step, "eg"))
                    act.wait_ge(*VE(step, "glast"))
                    actf(edec, edec, ACT.Exp).then_inc(*AC.mark(step, "edec"))
                    for t in range(NT):
                        act.wait_ge(*VE(step, "decay log", t))
                        actf(Dm[:, t], Dm[:, t], ACT.Exp).then_inc(*AC.mark(step, "decay", t))
                elif kind == "tok":
                    for part in range(3):
                        for t in range(NT):
                            if part == 2 and t == 0:
                                fill(step, 0)
                            act.wait_ge(*PE(step, "turned", part, t))
                            if part == 0 and t == 0 and step[1] == 1:
                                act.wait_ge(*PE(("scan", 0), "o", 1))
                            copy(tok[:, t, part, :, :], Q[(part * NT + t) % 4][:].rearrange("p (h d) -> p h d", h=GH)).then_inc(*AC.mark(step, "out", part, t))
                            if part < 2:
                                act.wait_ge(*AC(step, "out", part, t))
                                if part + t == 0:
                                    act.wait_ge(*VE(("moba", step[1], 0), "rope", 1))
                                if part + t > 0:
                                    pt_, pp_ = (0, part) if t == 1 else (1, part - 1)
                                    act.wait_ge(*VE(step, "sum", pp_, pt_))
                                elif step[1] == 1:
                                    act.wait_ge(*VE(("scan", 0), "sum", 1))
                                actf(sq[:], tok[:, t, part, :, :], ACT.Square).then_inc(*AC.mark(step, "sq", part, t))
                    for i in range(1, 4):
                        fill(step, i)
                elif kind == "moba":
                    _, gr, part = step
                    if part == 2:
                        act.wait_ge(*fed(step))
                        if gr == 1:
                            act.wait_ge(*PE(("att", 0), "out", 1))
                        for t in range(NT):
                            copy(mtok[:, 2, t, :, :], L[2 + t][:].rearrange("p (h d) -> p h d", h=GH)).then_inc(*AC.mark(step, "v", t))
                elif kind == "feat":
                    gr = step[1]
                    outs = [kT[:, 0], kbqT[:, 0, :, 0, :], kbqT[:, 0, :, 1, :], kT[:, 1], kbqT[:, 1, :, 0, :], kbqT[:, 1, :, 1, :], qeT[:]]
                    fill(step, 0)
                    for b in range(7):
                        if b == 4:
                            fill(step, 1)
                        act.wait_ge(*PE(step, "turned", b))
                        copy(outs[b], Q[b % 4][:].rearrange("p (h d) -> p h d", h=GH)).then_inc(*AC.mark(step, "out", b))
                    fill(step, 2)
                    fill(step, 3)
                elif kind == "att":
                    gr = step[1]
                    outs = [qTa[:, 0:2, :], qTa[:, 2:4, :], kTa[:, 0:2, :], kTa[:, 2:4, :]]
                    for b in range(4):
                        act.wait_ge(*PE(step, "turned", b))
                        copy(outs[b], Q[b][:].rearrange("p (h d) -> p h d", h=2)).then_inc(*AC.mark(step, "heads", b))
                    fill(step, 0)
                    act.wait_ge(*VE(step, "max"))
                    for t in range(NT):
                        for i in range(GH):
                            p_ = pr[:, i, 0:P] if t == 0 else pr[:, i, P:3 * P]
                            n_ = t * GH + i
                            actf(p_, p_, ACT.Exp, bias=nm[:, n_:n_ + 1], accum_out=rs[:, n_:n_ + 1]).then_inc(*AC.mark(step, "exp", t, i))
                    fill(step, 1)
                    fill(step, 2)
                    for b in range(3):
                        act.wait_ge(*PE(step, "probs turned", b))
                        copy(prT[:, :, b * P:(b + 1) * P], Q[b][:].rearrange("p (h d) -> p h d", h=GH)).then_inc(*AC.mark(step, "probs", b))
                    fill(step, 3)
                    for b in range(2):
                        act.wait_ge(*PE(step, "out", b))
                        copy(yH[:, gr * GH + 2 * b:gr * GH + 2 * b + 2, :], Q[3 if b == 0 else 0][:].rearrange("p (h d) -> p h d", h=2)).then_inc(*AC.mark(step, "hi", b))
                elif kind in ("z", "ga", "gb"):
                    c = step[1]
                    act.wait_ge(*fed(step))
                    dst = {"z": z, "ga": gs, "gb": gsb}[kind]
                    fn = ACT.Silu if kind == "z" else ACT.Sigmoid
                    banks = {"z": ((0, 1), (2, 3)), "ga": ((0, 1), (0, 1)), "gb": ((0, 2), (1, 3))}[kind][c]
                    for t in range(NT):
                        last = actf(dst[:, t, c * 512:(c + 1) * 512], L[banks[t]][:], fn)
                    last.then_inc(*AC.mark(step))
                elif kind == "inv":
                    fill(step, 0)
                    for l in range(1, LEVELS):
                        fill(step, l)
                        for t in range(NT):
                            act.wait_ge(*PE(step, "X", l, t))
                            copy(X[:, t], (Q[(t + 2) % 4] if l % 2 else Q[t])[:].rearrange("p (h d) -> p h d", h=GH)).then_inc(*AC.mark(step, "X", l, t))
                        if l > 1:
                            for t in range(NT):
                                act.wait_ge(*PE(step, "turned", l, t))
                                copy(TT[:, t], (Q[t] if l % 2 else Q[2 + t])[:].rearrange("p (h d) -> p h d", h=GH)).then_inc(*AC.mark(step, "TT", l, t))
                    fill(step, LEVELS)
                elif kind == "scan":
                    for t in range(NT):
                        act.wait_ge(*PE(step, "u", t))
                        copy(vn[:, t], Q[t][:].rearrange("p (h d) -> p h d", h=GH)).then_inc(*AC.mark(step, "u", t))
                    act.wait_ge(*PE(step, "wT"))
                    copy(wT[:], Q[2][:].rearrange("p (h d) -> p h d", h=GH)).then_inc(*AC.mark(step, "wT"))
                    act.wait_ge(*PE(step, "S"))
                    copy(S[:], Q[3][:].rearrange("p (h d) -> p h d", h=GH)).then_inc(*AC.mark(step, "S"))
                    gr = step[1]
                    for t in range(NT):
                        act.wait_ge(*PE(step, "o", t))
                        ot = o[:, t, gr * 512:(gr + 1) * 512].rearrange("p (h d) -> p h d", h=GH)
                        copy(ot, Q[t][:].rearrange("p (h d) -> p h d", h=GH)).then_inc(*AC.mark(step, "o", t))
                        act.wait_ge(*AC(step, "o", t))
                        if t == 1:
                            act.wait_ge(*VE(step, "sum", 0))
                        actf(sq[:], ot, ACT.Square).then_inc(*AC.mark(step, "sq", t))
                    if gr == 1:
                        load("mem", mem[:], tokens(a["mem_2"][0]), PE(("scan", 1), "o", 1), AC(("scan", 1), "u", 1))
                        load("lnm", lnm[:], row(a["g_mem_2"], D), VE(("inv", 1), "TT", LEVELS - 1, 1))
                elif kind == "mem":
                    hi_wide(step, mH)
                elif kind == "yb":
                    hi_wide(step, yH)
                    act.wait_ge(landed["mem"], 16)
                    act.wait_ge(*PE(("scan", 1), "u", 1))
                    for t in range(NT):
                        actf(xv[:, t, :], mem[:, t, :], ACT.Square, accum_out=ss[:, 4 + t:5 + t]).then_inc(*AC.mark(("mem",), "ss", t))
                    load("p", pt[:], tokens(a["p"][0, 0]), VE(("yb",), "lo", 3))
                    load("lnp", lnp[:], row(a["ln_ple"][0], D))
                    load("gA_mix", gA[:], row(a["ln_post_mix"][0], D))
                    load("gB_mix", gB[:], row(a["ln_pre_ffn"][0], D), PE(("att", 1), "out", 1))
                elif kind == "p":
                    act.wait_ge(*PE(step, "turned"))
                    copy(pH[:], Q[3][:].rearrange("p (k n) -> p k n", k=2)).then_inc(*AC.mark(step, "hi"))
                elif kind == "merge":
                    load("xres", h[:], tokens(a["x"][0]), VE(("proj_b",), "sum", 1, 1))
                    hi_next(step, ("w_out",))
                elif kind == "ple":
                    act.wait_ge(*fed(step))
                    for t in range(NT):
                        for c in range(2):
                            b = 2 * t + c
                            copy(e[:, t, c * 512:(c + 1) * 512], Q[b][:]).then_inc(*AC.mark(step, "out", b))
                elif kind == "e":
                    for t in range(NT):
                        act.wait_ge(*AC(("ple",), "out", 2 * t + 1))
                        actf(xv[:, t, :], e[:, t, :], ACT.Square, accum_out=ss_p[:, t:t + 1]).then_inc(*AC.mark(step, "ss", t))
                elif kind == "xkv":
                    c = step[1]
                    act.wait_ge(*fed(step))
                    for t in range(NT):
                        dst = xk[c][:, t, :] if c < 2 else xv[:, t, (c - 2) * 512:(c - 1) * 512]
                        actf(dst, Q[t][:], ACT.Copy, scale=rstd_m[:, t:t + 1]).then_inc(*AC.mark(step, t))
                    if c < 2:
                        for j in range(2):
                            act.wait_ge(*PE(step, "turned", j))
                            copy(xkT[:, 4 * c + 2 * j:4 * c + 2 * j + 2, :], Q[2 + j][:].rearrange("p (k n) -> p k n", k=2)).then_inc(*AC.mark(step, "turned", j))
                elif kind == "norm":
                    what = step[1]
                    src_step = {"mix": ("w_out",), "ffn1": ("down", 1), "ple": ("ple_gate",), "mix2": ("out2",), "x": ("xo",),
                                "ffn2": ("down", 2)}[what]
                    if what in ("ffn1", "ffn2"):
                        act.wait_ge(*PE(("ffn", 1 if what == "ffn1" else 2, 5), "turned", 0))
                    for t in range(NT):
                        for c in range(2):
                            b = 2 * t + c
                            act.wait_ge(*(PE(src_step, "bank", b) if b < 3 else fed(src_step)))
                            out_ = tmp[:, t, c * 512:(c + 1) * 512]
                            if what == "ple":
                                actf(out_, L[b][:], ACT.Sigmoid).then_inc(*AC.mark(step, "gate", t, c))
                            else:
                                actf(out_, L[b][:], ACT.Square, accum_out=ss[:, b:b + 1]).then_inc(*AC.mark(step, "ss", t, c))
                    if what == "ffn1":
                        load("pos", pos_i[:], a["positions_2"][0].rearrange("(t p) -> p t", p=P), allow_slow_non_contiguous=True)
                        load("wpool", wpool[:], a["w_pool_2"].rearrange("g c d -> c g d"))
                        load("gsub", gsub[:], row(a["g_subln_2"], HD))
                        for n, v_ in enumerate(("lambda_q1_2", "lambda_k1_2", "lambda_q2_2", "lambda_k2_2")):
                            act.dma_start(lamv[:, n, :], row(a[v_], 64)).then_inc(landed["lamv"], 16)
                        load("psc", psr[:], a["pool_scale_2"].rearrange("(g c) -> g c", c=P))
                        load("poolm", poolm[:].rearrange("p a b c -> p (a b c)"), a["pool_table"], fed(("down", 1)))
                elif kind == "next":
                    what = step[1]
                    hi_next(step, next(s_ for s_, i_ in INPUT.items() if i_ == step))
                    if what != "ffn1":
                        for t in range(NT):
                            act.wait_ge(*VE(("norm", what), "next", t, 2))
                            actf(tmp[:, t, :], h[:, t, :], ACT.Square, accum_out=ss[:, 4 + t:5 + t]).then_inc(*AC.mark(step, "hss", t))
                    if what == "mix":
                        load("gA_ffn1", gA[:], row(a["ln_post_ffn"][0], D), VE(("norm", what), "next", 1, 2))
                    if what == "ffn1":
                        load("gB_ple", gB[:], row(a["g_mix_pre_2"], D), VE(("norm", what), "next", 1, 2))
                        load("gA_mix2", gA[:], row(a["g_mix_post_2"], D))
                    if what == "ple":
                        load("gB_mix2", gB[:], row(a["g_x_pre_2"], D), VE(("norm", what), "next", 1, 2))
                    if what == "mix2":
                        load("gA_x", gA[:], row(a["g_x_post_2"], D), VE(("norm", what), "next", 1, 2))
                        load("gB_x", gB[:], row(a["g_ffn_pre_2"], D))
                    if what == "x":
                        load("gA_ffn2", gA[:], row(a["g_ffn_post_2"], D), VE(("norm", what), "next", 1, 2))
                elif kind == "ffn":
                    _, blk, c = step
                    n = 512 if c < 5 else 256
                    half = (LAST[step] + 1 - FIRST[step]) // 2
                    split_up_to(FIRST[step] + half + SPLIT - 1)
                    act.wait_ge(*fed(step, half))
                    if c > 0:
                        act.wait_ge(*VE(("ffn", blk, c - 1), "hidden", 1))
                    else:
                        act.wait_ge(*VE(("next", "mix" if blk == 1 else "x"), "rstd"))
                    for t in range(NT):
                        actf(sil[:, t, 0:n], L[2 * t][:, 0:n], ACT.Silu, scale=rstd_h[:, t:t + 1]).then_inc(*AC.mark(step, "silu", t))
                    todo = ([c - 1] if c > 0 else []) + ([5] if c == 5 else [])
                    for c_ in todo:
                        prev = ("ffn", blk, c_)
                        if c_ == 5:
                            split_up_to(FIRST[("down", blk)] + SPLIT)
                        for j in range(2 if c_ < 5 else 1):
                            act.wait_ge(*PE(prev, "turned", j))
                            bank = Q[2 * ((c_ + 1) % 2) + j]
                            copy(hH[:, 4 * c_ + 2 * j:4 * c_ + 2 * j + 2, :], bank[:].rearrange("p (k n) -> p k n", k=2)).then_inc(*AC.mark(prev, "hi", j))
                    split_up_to(consumed + SPLIT - 1)
                elif kind == "in2":
                    c = step[1]
                    act.wait_ge(*fed(step))
                    if c == 0:
                        act.wait_ge(*VE(("next", "ple"), "rstd"))
                    for t in range(NT):
                        src = L[2 * (c % 2) + t][:]
                        if c < 2:
                            dst, src = qk2[:, t, c, :, :], src.rearrange("p (h d) -> p h d", h=2 * GH)
                        elif c == 2:
                            dst, src = v2[:, t, :, :], src.rearrange("p (h d) -> p h d", h=GH)
                        else:
                            dst = u2[:, t, :]
                        actf(dst, src, ACT.Copy, scale=rstd_h[:, t:t + 1]).then_inc(*AC.mark(step, t))
                elif kind == "angles":
                    act.wait_ge(*VE(step, "angles"))
                    actf(sn, sn, ACT.Sin).then_inc(*AC.mark(step, "sin"))
                    actf(cs, cs, ACT.Sin).then_inc(*AC.mark(step, "cos"))
                    act.wait_ge(*VE(step, "lam sums"))
                    actf(lam[:, 0:2], lam[:, 0:2], ACT.Exp).then_inc(*AC.mark(step, "lam"))
                elif kind == "heads2":
                    outs = [dqT[:, 0:2, :], dqT[:, 2:4, :], dkT[:, 0:2, :], dkT[:, 2:4, :]]
                    for b in range(4):
                        act.wait_ge(*PE(step, "turned", b))
                        copy(outs[b], Q[b][:].rearrange("p (h d) -> p h d", h=2)).then_inc(*AC.mark(step, "heads", b))
                elif kind == "pool":
                    for m in range(2):
                        act.wait_ge(*VE(("diff",), "max", m))
                        for t in range(NT):
                            for i in range(GH):
                                p_ = pd[m][:, i, 0:P] if t == 0 else pd[m][:, i, P:3 * P]
                                n_ = m * 8 + t * GH + i
                                actf(p_, p_, ACT.Exp, bias=nm[:, n_:n_ + 1], accum_out=rs[:, n_:n_ + 1]).then_inc(*AC.mark(("probs",), "exp", m, t, i))
                        if m == 0:
                            for b in range(2):
                                act.wait_ge(*PE(step, "pooled", b))
                                copy(poolT[:, 2 * b:2 * b + 2, :], L[2 + b][:].rearrange("p (k n) -> p k n", k=2)).then_inc(*AC.mark(step, "pooled", b))
                            act.wait_ge(*VE(step, "scale"))
                            for b in range(2):
                                act.wait_ge(*PE(step, "out", b))
                                for i in range(2):
                                    gi = 2 * b + i
                                    actf(uH[:, 4 + gi, :], Q[b][:, i * SEQ:(i + 1) * SEQ], ACT.Copy, scale=psc[:, gi:gi + 1]).then_inc(*AC.mark(step, "hi", gi))
                    split_up_to(FIRST[("out2",)] + 2 + SPLIT - 1)
                elif kind == "probs":
                    for b in range(3):
                        act.wait_ge(*PE(step, "probs turned", b))
                        copy(pdT[:, :, b * P:(b + 1) * P], Q[b][:].rearrange("p (h d) -> p h d", h=GH)).then_inc(*AC.mark(step, "probs", b))
                    split_up_to(FIRST[("out2",)] + 3 + SPLIT - 1)
                    for t in range(NT):
                        act.wait_ge(*PE(step, "out", t))
                        bank = Q[3] if t == 0 else Q[0]
                        copy(da[:, t], bank[:].rearrange("p (h d) -> p h d", h=GH)).then_inc(*AC.mark(step, "out", t))
                        act.wait_ge(*AC(step, "out", t))
                        if t == 1:
                            act.wait_ge(*VE(step, "sum", 0))
                        actf(dsq[:], da[:, t], ACT.Square).then_inc(*AC.mark(step, "sq", t))
                elif kind == "dnorm":
                    split_up_to(FIRST[("out2",)] + 4 + SPLIT - 1)
                    for j in range(2):
                        act.wait_ge(*PE(step, "turned", j))
                        copy(uH[:, 2 * j:2 * j + 2, :], Q[2 + j][:].rearrange("p (k n) -> p k n", k=2)).then_inc(*AC.mark(step, "hi", j))
                elif kind == "xq":
                    act.wait_ge(*fed(step))
                    act.wait_ge(*VE(("next", "mix2"), "rstd"))
                    for t in range(NT):
                        for c in range(2):
                            actf(cq[:, t, c * 512:(c + 1) * 512], L[2 * t + c][:], ACT.Copy, scale=rstd_h[:, t:t + 1]).then_inc(*AC.mark(step, t, c))
                elif kind == "cross":
                    for j in (1, 3):
                        act.wait_ge(*PE(step, "turned", j))
                        copy(cqT[:, 2 * j:2 * j + 2, :], Q[j][:].rearrange("p (k n) -> p k n", k=2)).then_inc(*AC.mark(step, "heads", j))
                    for t in range(NT):
                        act.wait_ge(*VE(step, "max", t))
                        for i in range(GH):
                            n_ = t * GH + i
                            actf(cp[:, t, i, :], L[2 * t + i // 2][:, (i % 2) * SEQ:(i % 2 + 1) * SEQ], ACT.Exp, scale=1.0 / 16,
                                 bias=nm[:, n_:n_ + 1], accum_out=rs[:, n_:n_ + 1]).then_inc(*AC.mark(step, "exp", t, i))
                    for t in range(NT):
                        for j in range(2):
                            act.wait_ge(*PE(step, "probs turned", t, j))
                            copy(cpT[:, j, :, t * P:(t + 1) * P], Q[2 * t + j][:].rearrange("p (h d) -> p h d", h=GH)).then_inc(*AC.mark(step, "probs", t, j))
                    for j in range(4):
                        act.wait_ge(*PE(step, "out", j))
                        copy(uH[:, 2 * j:2 * j + 2, :], L[j][:].rearrange("p (k n) -> p k n", k=2)).then_inc(*AC.mark(step, "hi", j))

        @block.vector
        def _(dve):
            V = nc.vector

            def v(ins, *name):
                ins.then_inc(*VE.mark(*name))
                dve.wait_ge(vector_done, VE.n)

            def tt(out_, x_, y_, op, *name):
                v(V.tensor_tensor(out_, x_, y_, op), *name)

            def ts(out_, x_, s1, s2_, op0, op1, *name):
                if op1 is None:
                    v(V.tensor_scalar(out_, x_, s1, None, op0), *name)
                else:
                    v(V.tensor_scalar(out_, x_, s1, s2_, op0, op1), *name)

            def stt(out_, x_, s_, y_, op0, op1, *name):
                v(V.scalar_tensor_tensor(out=out_, in0=x_, scalar=s_, in1=y_, op0=op0, op1=op1), *name)

            def rsqrt(dst, src, *name):
                n = src.shape[1]
                t_ = rt[:, 0:n]
                ts(dst.bitcast(I32), src.bitcast(I32), -0.5, 1597463007.0, ALU.mult, ALU.add)
                for i in range(3):
                    stt(t_, src, -0.5, dst, ALU.mult, ALU.mult)
                    tt(t_, t_, dst, ALU.mult)
                    stt(dst, t_, 1.5, dst, ALU.add, ALU.mult, *(name if i == 2 else ()))

            def lo_wide(step, dH, dL, tiles=range(4)):
                for j in tiles:
                    dve.wait_ge(*AC(step, "hi", j))
                    tt(dL[:, 2 * j:2 * j + 2, :], Q[j][:].rearrange("p (k n) -> p k n", k=2), dH[:, 2 * j:2 * j + 2, :].bitcast(F32),
                       ALU.subtract, step, "lo", j)

            def heads(bank, n=GH):
                return bank[:].rearrange("p (h d) -> p h d", h=n)

            def norm_part(what, part):
                post, pre = RES[what]
                step = ("norm", what)
                c0, c1 = ((0, 256), (256, 512), (512, D))[part]
                for t in range(NT):
                    cc, b = slice(c0, c1), 2 * t + c0 // 512
                    if post:
                        stt(tmp[:, t, cc], L[b][:, c0 % 512:(c1 - 1) % 512 + 1], rstd_o[:, t:t + 1], gA[:, cc], ALU.mult, ALU.mult)
                    else:
                        dve.wait_ge(*AC(step, "gate", t, c0 // 512))
                        tt(tmp[:, t, cc], tmp[:, t, cc], e[:, t, cc], ALU.mult)
                    name = {"ffn1": (step, "next", t, part), "ffn2": ("out", 2 * part + t)}.get(what, ())
                    tt(h[:, t, cc], h[:, t, cc], tmp[:, t, cc], ALU.add, *name)
                    if pre:
                        tt(hg[:, t, cc], h[:, t, cc], gB[:, cc], ALU.mult, step, "next", t, part)

            for step in SCHEDULE:
                kind = step[0]
                if kind == "u":
                    for t in range(NT):
                        one = slice(t, t + 1)
                        dve.wait_ge(*AC(step, "ss", t))
                        ts(rv[:, one], ss[:, one], 1.0 / D, EPS, ALU.mult, ALU.add)
                        rsqrt(rstd0[:, one], rv[:, one])
                        if t == 0:
                            dve.wait_ge(landed["ln0"], 16)
                        stt(xn0[:, t, :], x0[:, t, :], rstd0[:, one], ln0[:], ALU.mult, ALU.mult, step, "scaled", t)
                    dve.wait_ge(*PE(step, "taps"))
                    v(V.tensor_copy(cw, L[3][:, 0:CONV * 24]))
                    lo_wide(step, uH, uL)
                    dve.wait_ge(landed["ba"], 16)
                    bv = ba_raw.rearrange("p (k n) -> p k n", k=KD)
                    v(V.tensor_copy(baH[:], bv))
                    tt(baL[:], bv, baH[:].bitcast(F32), ALU.subtract, step, "split")
                elif kind == "ba":
                    dve.wait_ge(*PE(step))
                    v(V.tensor_copy(baT[0:16, :], Q[0][0:16, 0:SEQ]), step, "turned")
                elif kind == "rates":
                    dve.wait_ge(*PE(step))
                    v(V.tensor_copy(ba, Q[1][:, 0:32]), step, "ba")
                    bav = ba.rearrange("p (t n) -> p t n", t=NT)
                    tAv = tA.rearrange("p (t n) -> p t n", t=NT)
                    dve.wait_ge(landed["dtb"], 16)
                    tt(tAv, bav[:, :, 8:16], each(dtb, NT), ALU.add)
                    ts(tB, tA, -1.0, None, ALU.mult, None)
                    tt(tB, tB, tA, ALU.max, step, "abs")
                    dve.wait_ge(*AC(step, "exp"))
                    ts(tB, tB, 1.0, None, ALU.add, None, step, "1+exp")
                    ts(tA, tA, 0.0, None, ALU.max, None)
                    dve.wait_ge(*AC(step, "ln"))
                    tt(tA, tA, tB, ALU.add)
                    gv = g.rearrange("p (t n) -> p t n", t=NT)
                    ts(tA, tA, -1.0, None, ALU.mult, None)
                    tt(gv, tAv, each(alog, NT), ALU.mult, step, "g")
                elif kind == "conv":
                    _, gr, part = step
                    cwv = cw.rearrange("p (j t) -> p j t", j=CONV)
                    if part == 0 and gr == 1:
                        dve.wait_ge(*PE(("feat", 0), "kk", 1, 1))
                    for ct in range(4):
                        if ct % 2 == 0:
                            dve.wait_ge(*(PE(step, "half") if ct == 0 else fed(step)))
                        tile = part * 8 + gr * GH + ct
                        src = L[2 * (part % 2) + ct // 2][:, (ct % 2) * SEQ:(ct % 2 + 1) * SEQ]
                        dst = C[:, part * GH + ct, :]
                        ts(dst, src, cwv[:, 3, tile:tile + 1], None, ALU.mult, None)
                        for back in range(1, CONV):
                            j = CONV - 1 - back
                            name = (step, "taps done") if back == CONV - 1 and ct == 3 else ()
                            stt(dst[:, back:SEQ], src[:, 0:SEQ - back], cwv[:, j, tile:tile + 1], dst[:, back:SEQ], ALU.mult, ALU.add, *name)
                elif kind == "tok":
                    s2v = s2.rearrange("p (t a h) -> p t a h", t=NT, a=2)
                    for part in range(2):
                        for t in range(NT):
                            dve.wait_ge(*AC(step, "sq", part, t))
                            v(V.tensor_reduce(s2v[:, t, part, :], sq[:], AX.X, ALU.add), step, "sum", part, t)
                    ts(s2, s2, EPS, None, ALU.add, None)
                    rsqrt(rq, s2)
                    rqv = rq.rearrange("p (t a h) -> p t a h", t=NT, a=2)
                    ts(rqv[:, :, 0, :], rqv[:, :, 0, :], float(HD) ** -0.5, None, ALU.mult, None, step, "rq")
                elif kind == "moba":
                    _, gr, part = step
                    if part == 2:
                        continue
                    dve.wait_ge(*fed(step))
                    if gr == 1 and part == 0:
                        dve.wait_ge(*PE(("att", 0), "turned", 3))
                    for t in range(NT):
                        src = heads(L[2 - 2 * part + t])
                        dst = mtok[:, part, t]
                        r_ = sqr[:]
                        tt(dst, src, each(cos1[:, t, :], GH), ALU.mult)
                        tt(r_[:, :, 0:64], src[:, :, 64:128], each(sin1[:, t, 0:64], GH), ALU.mult)
                        tt(r_[:, :, 64:128], src[:, :, 0:64], each(sin1[:, t, 64:128], GH), ALU.mult)
                        tt(dst, dst, r_, ALU.add, step, "rope", t)
                elif kind == "tri":
                    gr = step[1]
                    gv = g.rearrange("p (t n) -> p t n", t=NT)[:, :, gr * GH:(gr + 1) * GH]
                    if gr == 1:
                        dve.wait_ge(*PE(("scan", 0), "o", 1))
                    for t in range(NT):
                        tt(trg[:, t], each(tri, GH), over(gv[:, t, :], P), ALU.mult, step, t)
                elif kind == "decay":
                    gcv = gc.rearrange("p (t h) -> p t h", t=NT)
                    dve.wait_ge(*PE(step, "gc"))
                    v(V.tensor_copy(gcv, Q[3][:, 0:16].rearrange("p (t h) -> p t h", t=NT)[:, :, 0:GH]), step, "gc")
                    for t in range(NT):
                        dve.wait_ge(*PE(step, "rows", t))
                        if t == 0:
                            tt(edec, heads(Q[0])[:, :, P - 1], gcv[:, 0, :], ALU.subtract, step, "glast")
                        tt(Dm[:, t], heads(Q[t]), over(gcv[:, t, :], P), ALU.subtract)
                        tt(Dm[:, t], Dm[:, t], each(neg_kq, GH), ALU.add, step, "decay log", t)
                elif kind == "feat":
                    gr = step[1]
                    rqv = rq.rearrange("p (t a h) -> p t a h", t=NT, a=2)
                    bet = beta.rearrange("p (t n) -> p t n", t=NT)[:, :, gr * GH:(gr + 1) * GH]
                    egv = eg.rearrange("p (t h) -> p t h", t=NT)
                    dve.wait_ge(*AC(("tok", gr), "out", 2, 1))
                    dve.wait_ge(*AC(("rates",), "beta"))
                    for t in range(NT):
                        tt(tok[:, t, 1], tok[:, t, 1], over(rqv[:, t, 1, :], HD), ALU.mult, step, "kn", t)
                        tt(kb[:, t], tok[:, t, 1], over(bet[:, t, :], HD), ALU.mult, step, "kb", t)
                        tt(tok[:, t, 0], tok[:, t, 0], over(rqv[:, t, 0, :], HD), ALU.mult, step, "qn", t)
                    dve.wait_ge(*AC(("decay", gr), "edec"))
                    tt(qe[:], tok[:, 1, 0], over(egv[:, 1, :], HD), ALU.mult, step, "qe", 1)
                    for t in range(NT):
                        dve.wait_ge(*AC(("decay", gr), "decay", t))
                        for pair in range(2):
                            dve.wait_ge(*PE(step, "kk", t, pair))
                            kk_ = Q[2 * t + pair][:].rearrange("p (i a d) -> p i a d", i=2, a=2)
                            hs = slice(2 * pair, 2 * pair + 2)
                            tt(AT[:, t, hs], kk_[:, :, 0, :], Dm[:, t, hs], ALU.mult)
                            tt(aT[:, t, hs], kk_[:, :, 1, :], Dm[:, t, hs], ALU.mult, step, "attn", t, pair)
                    tt(kbe[:], kb[:, 1], over(egv[:, 1, :], HD), ALU.mult)
                    tt(kdec[:], tok[:, 0, 1], over(edec, HD), ALU.mult)
                    for t in range(NT):
                        tt(tok[:, t, 2], tok[:, t, 2], over(bet[:, t, :], HD), ALU.mult)
                elif kind == "att":
                    gr = step[1]
                    scale = float(HD) ** -0.5
                    dve.wait_ge(*PE(step, "scores", 0))
                    stt(pr[:, :, 0:P], heads(Q[0]), scale, each(neg_qk, GH), ALU.mult, ALU.add)
                    v(V.tensor_reduce(mx[:, 0:GH], pr[:, :, 0:P], AX.X, ALU.max))
                    for pair in range(2):
                        dve.wait_ge(*PE(step, "scores", 1 + pair))
                        src, hs = heads(Q[1 + pair], 2), slice(2 * pair, 2 * pair + 2)
                        ts(pr[:, hs, P:2 * P], src[:, :, 0:P], scale, None, ALU.mult, None)
                        stt(pr[:, hs, 2 * P:3 * P], src[:, :, P:SEQ], scale, each(neg_qk, 2), ALU.mult, ALU.add)
                    v(V.tensor_reduce(mx[:, GH:2 * GH], pr[:, :, P:3 * P], AX.X, ALU.max))
                    ts(nm[:, 0:8], mx[:, 0:8], -1.0, None, ALU.mult, None, step, "max")
                    dve.wait_ge(*AC(step, "exp", 1, 3))
                    v(V.reciprocal(ri[:, 0:8], rs[:, 0:8]))
                    tt(pr[:, :, 0:P], pr[:, :, 0:P], over(ri[:, 0:GH], P), ALU.mult)
                    tt(pr[:, :, P:3 * P], pr[:, :, P:3 * P], over(ri[:, GH:2 * GH], 2 * P), ALU.mult, step, "probs")
                    for b in range(2):
                        dve.wait_ge(*AC(step, "hi", b))
                        k0 = gr * GH + 2 * b
                        tt(yL[:, k0:k0 + 2, :], heads(Q[3 if b == 0 else 0], 2), yH[:, k0:k0 + 2, :].bitcast(F32), ALU.subtract, step, "lo", b)
                elif kind == "inv":
                    gr = step[1]

                    def mask(l):
                        tt(M[:].rearrange("p t h d -> p (t h) d"), AT[:].rearrange("p t h d -> p (t h) d"), each(square(2 + l), NT * GH),
                           ALU.mult, step, "mask", l)

                    dve.wait_ge(*PE(("att", gr), "out", 1))
                    mask(0)
                    for t in range(NT):
                        dve.wait_ge(*PE(step, "M0", t))
                        tt(T[:, t], each(ident, GH), heads(Q[t]), ALU.subtract, step, "T", 0, t)
                        tt(TT[:, t], each(ident, GH), M[:, t], ALU.subtract)
                    mask(1)
                    for l in range(1, LEVELS):
                        if l < LEVELS - 1:
                            dve.wait_ge(*PE(step, "X", l, 1))
                            mask(l + 1)
                        for t in range(NT):
                            dve.wait_ge(*PE(step, "Y", l, t))
                            to, name = (T, "T") if l < LEVELS - 1 else (TT, "TT")
                            tt(to[:, t], to[:, t], heads(Q[t + 2] if l % 2 else Q[t]), ALU.subtract, step, name, l, t)
                elif kind == "scan":
                    gr = step[1]
                    dve.wait_ge(*AC(step, "u", 1))
                    dve.wait_ge(*PE(step, "wS"))
                    tt(vn[:, 1], vn[:, 1], heads(Q[2]), ALU.subtract, step, "vn")
                    for t in range(NT):
                        dve.wait_ge(*AC(step, "sq", t))
                        v(V.tensor_reduce(so[:, t * 8 + gr * GH:t * 8 + (gr + 1) * GH], sq[:], AX.X, ALU.add), step, "sum", t)
                elif kind == "proj_a":
                    dve.wait_ge(*fed(step))
                    dve.wait_ge(*AC(("ga", 1)))
                    for t in range(NT):
                        for c in range(2):
                            gt = gs[:, t, c * 512:(c + 1) * 512]
                            tt(gt, gt, L[2 * t + c][:], ALU.mult, step, "mul", 2 * t + c)
                elif kind == "proj_b":
                    dve.wait_ge(*fed(step))
                    dve.wait_ge(*AC(("gb", 1)))
                    for c in range(2):
                        for t in range(NT):
                            gt, bt = gs[:, t, c * 512:(c + 1) * 512], gsb[:, t, c * 512:(c + 1) * 512]
                            tt(bt, bt, L[2 * t + c][:], ALU.mult)
                            tt(gt, gt, bt, ALU.add, step, "sum", t, c)
                elif kind == "mem":
                    lo_wide(step, mH, mL)
                elif kind == "yb":
                    ts(so, so, 1.0 / HD, EPS, ALU.mult, ALU.add)
                    rsqrt(rq, so)
                    dve.wait_ge(landed["gnorm"], 16)
                    dve.wait_ge(*AC(("z", 1)))
                    for t in range(NT):
                        ot = o[:, t, :].rearrange("p (h d) -> p h d", h=8)
                        tt(ot, ot, over(rq[:, t * 8:(t + 1) * 8], HD), ALU.mult)
                        tt(ot, ot, each(gnorm, 8), ALU.mult)
                        tt(o[:, t, :], o[:, t, :], z[:, t, :], ALU.mult, step, "y", t)
                    lo_wide(step, yH, yL)
                elif kind == "p":
                    dve.wait_ge(landed["mem"], 16)
                    dve.wait_ge(landed["lnm"], 16)
                    dve.wait_ge(*AC(("mem",), "ss", 1))
                    ts(rv[:, 0:2], ss[:, 4:6], 1.0 / D, EPS, ALU.mult, ALU.add)
                    rsqrt(rstd_m, rv[:, 0:2], ("mem",), "rstd")
                    tt(mem[:], mem[:], each(lnm[:], NT), ALU.mult, ("mem",), "scaled")
                    dve.wait_ge(*AC(step, "hi"))
                    tt(pL[:], heads(Q[3], 2), pH[:].bitcast(F32), ALU.subtract, step, "lo")
                elif kind == "merge":
                    lo_wide(step, uH, uL)
                elif kind == "e":
                    dve.wait_ge(*AC(step, "ss", 1))
                    ts(rv[:, 0:2], ss_p[:, 0:2], 1.0 / D, EPS, ALU.mult, ALU.add)
                    rsqrt(rstd_p, rv[:, 0:2])
                    dve.wait_ge(landed["lnp"], 16)
                    for t in range(NT):
                        for c in range(2):
                            cc = slice(c * 512, (c + 1) * 512)
                            stt(e[:, t, cc], e[:, t, cc], rstd_p[:, t:t + 1], lnp[:, cc], ALU.mult, ALU.mult, step, "e", 2 * t + c)
                elif kind == "norm":
                    what = step[1]
                    post, pre = RES[what]
                    if post:
                        dve.wait_ge(*AC(step, "ss", 1, 1))
                        tt(rv[:, 0:2], ss[:, 0:4:2], ss[:, 1:4:2], ALU.add)
                        ts(rv[:, 0:2], rv[:, 0:2], 1.0 / D, EPS, ALU.mult, ALU.add)
                        rsqrt(rstd_o, rv[:, 0:2])
                        dve.wait_ge(landed["gA_" + what], 16)
                    if what == "mix":
                        dve.wait_ge(landed["xres"], 16)
                    if pre:
                        dve.wait_ge(landed["gB_" + what], 16)
                    for part in range(2 if what in LATE else 3):
                        norm_part(what, part)
                elif kind == "next":
                    lo_wide(step, uH, uL, (0,))
                    if step[1] in LATE:
                        norm_part(step[1], 2)
                    lo_wide(step, uH, uL, (1, 2, 3))
                    if step[1] != "ffn1":
                        dve.wait_ge(*AC(step, "hss", 1))
                        ts(rv[:, 0:2], ss[:, 4:6], 1.0 / D, EPS, ALU.mult, ALU.add)
                        rsqrt(rstd_h, rv[:, 0:2], step, "rstd")
                elif kind == "ffn":
                    _, blk, c = step
                    n = 512 if c < 5 else 256

                    def low(c_, j):
                        prev = ("ffn", blk, c_)
                        dve.wait_ge(*AC(prev, "hi", j))
                        k0 = 4 * c_ + 2 * j
                        tt(hL[:, k0:k0 + 2, :], heads(Q[2 * ((c_ + 1) % 2) + j], 2), hH[:, k0:k0 + 2, :].bitcast(F32), ALU.subtract, prev, "lo", j)

                    if c > 0:
                        low(c - 1, 0)
                        low(c - 1, 1)
                    dve.wait_ge(*fed(step))
                    for t in range(NT):
                        dve.wait_ge(*AC(step, "silu", t))
                        stt(hm[:, t, 0:n], L[2 * t + 1][:, 0:n], rstd_h[:, t:t + 1], sil[:, t, 0:n], ALU.mult, ALU.mult, step, "hidden", t)
                    if c == 5:
                        low(5, 0)
                elif kind == "angles":
                    dve.wait_ge(landed["pos"], 16)
                    ang3, kk3 = (q_.rearrange("p (t n) -> p t n", t=NT) for q_ in (ang, kk))
                    v(V.tensor_copy(posf, pos_i[:]))
                    tt(ang3, over(posf, ROPE2), each(inv2, NT), ALU.mult)
                    ts(kk, ang, 1.0 / (2 * np.pi), MAGIC, ALU.mult, ALU.add)
                    ts(kk, kk, MAGIC, None, ALU.subtract, None)
                    stt(sn, kk, -TWO_PI[0], ang, ALU.mult, ALU.add)
                    stt(sn, kk, -TWO_PI[1], sn, ALU.mult, ALU.add)
                    stt(sn, kk, -TWO_PI[2], sn, ALU.mult, ALU.add)
                    ts(cs, sn, float(np.pi / 2), None, ALU.add, None)
                    ts(kk, cs, float(np.pi), -2 * float(np.pi), ALU.is_gt, ALU.mult)
                    tt(cs, cs, kk, ALU.add)
                    ts(sn, sn, 3.1415925, -3.1415925, ALU.min, ALU.max)
                    ts(cs, cs, 3.1415925, -3.1415925, ALU.min, ALU.max, step, "angles")
                    dve.wait_ge(landed["lamv"], 64)
                    for n in range(2):
                        tt(lamv[:, 2 * n, :], lamv[:, 2 * n, :], lamv[:, 2 * n + 1, :], ALU.mult)
                        v(V.tensor_reduce(lam[:, n:n + 1], lamv[:, 2 * n, :], AX.X, ALU.add), *((step, "lam sums") if n else ()))
                elif kind == "rope2":
                    dve.wait_ge(*AC(("in2", 1), 1))
                    dve.wait_ge(*AC(("angles",), "cos"))
                    sn3, cs3 = (q_.rearrange("p (t n) -> p t n", t=NT) for q_ in (sn, cs))
                    for t in range(NT):
                        x_ = qk2[:, t].rearrange("p a h d -> p (a h) d")
                        x1, x2 = x_[:, :, 0:ROPE2], x_[:, :, ROPE2:2 * ROPE2]
                        c_, s_ = each(cs3[:, t, :], 4 * GH), each(sn3[:, t, :], 4 * GH)
                        q4 = [r2t[n][:].rearrange("p (h d) -> p h d", d=ROPE2) for n in range(4)]
                        tt(q4[0], x1, c_, ALU.mult)
                        tt(q4[1], x2, s_, ALU.mult)
                        tt(q4[2], x2, c_, ALU.mult)
                        tt(q4[3], x1, s_, ALU.mult)
                        tt(x1, q4[0], q4[1], ALU.subtract)
                        tt(x2, q4[2], q4[3], ALU.add, *((step, "rope") if t else ()))
                elif kind == "diff":
                    banks = [[Q[0], Q[1], Q[2]], [Q[3], L[0], L[1]]]
                    for m in range(2):
                        p_ = pd[m]
                        dve.wait_ge(*PE(step, "scores", m, 0))
                        stt(p_[:, :, 0:P], heads(banks[m][0]), 0.125, each(neg_qk, GH), ALU.mult, ALU.add)
                        v(V.tensor_reduce(mx[:, 8 * m:8 * m + GH], p_[:, :, 0:P], AX.X, ALU.max))
                        for pair in range(2):
                            dve.wait_ge(*PE(step, "scores", m, 1 + pair))
                            src, hs = heads(banks[m][1 + pair], 2), slice(2 * pair, 2 * pair + 2)
                            ts(p_[:, hs, P:2 * P], src[:, :, 0:P], 0.125, None, ALU.mult, None)
                            stt(p_[:, hs, 2 * P:3 * P], src[:, :, P:SEQ], 0.125, each(neg_qk, 2), ALU.mult, ALU.add)
                        v(V.tensor_reduce(mx[:, 8 * m + GH:8 * m + 8], p_[:, :, P:3 * P], AX.X, ALU.max))
                        ts(nm[:, 8 * m:8 * m + 8], mx[:, 8 * m:8 * m + 8], -1.0, None, ALU.mult, None, step, "max", m)
                    dve.wait_ge(*AC(("angles",), "lam"))
                    tt(lam[:, 2:3], lam[:, 0:1], lam[:, 1:2], ALU.subtract)
                    ts(lam[:, 2:3], lam[:, 2:3], LAM_INIT, None, ALU.add, None)
                elif kind == "pool":
                    dve.wait_ge(*PE(step, "scale"))
                    v(V.tensor_copy(psc, Q[2][:, 0:4]), step, "scale")
                    for gi in range(4):
                        dve.wait_ge(*AC(step, "hi", gi | 1))
                        stt(uL[:, 4 + gi, :], Q[gi // 2][:, (gi % 2) * SEQ:(gi % 2 + 1) * SEQ], psc[:, gi:gi + 1], uH[:, 4 + gi, :].bitcast(F32),
                            ALU.mult, ALU.subtract, step, "lo", gi)
                elif kind == "probs":
                    for m in range(2):
                        dve.wait_ge(*AC(step, "exp", m, 1, 3))
                        v(V.reciprocal(ri[:, 8 * m:8 * m + 8], rs[:, 8 * m:8 * m + 8]))
                        if m == 1:
                            ts(ri[:, 8:16], ri[:, 8:16], lam[:, 2:3], None, ALU.mult, None)
                        tt(pd[m][:, :, 0:P], pd[m][:, :, 0:P], over(ri[:, 8 * m:8 * m + GH], P), ALU.mult)
                        tt(pd[m][:, :, P:3 * P], pd[m][:, :, P:3 * P], over(ri[:, 8 * m + GH:8 * m + 8], 2 * P), ALU.mult)
                    tt(pd[0][:], pd[0][:], pd[1][:], ALU.subtract, step, "probs")
                    for t in range(NT):
                        dve.wait_ge(*AC(step, "sq", t))
                        v(V.tensor_reduce(mx[:, t * GH:(t + 1) * GH], dsq[:], AX.X, ALU.add), step, "sum", t)
                elif kind == "dnorm":
                    ts(rv[:, 0:8], mx[:, 0:8], 1.0 / HD, EPS, ALU.mult, ALU.add)
                    rsqrt(r1, rv[:, 0:8])
                    dve.wait_ge(landed["gsub"], 16)
                    ts(gsub[:], gsub[:], 1.0 - LAM_INIT, None, ALU.mult, None)
                    dav = da[:].rearrange("p t h d -> p (t h) d")
                    tt(dav, dav, over(r1, HD), ALU.mult)
                    tt(dav, dav, each(gsub[:], NT * GH), ALU.mult, step, "da")
                    for j in range(2):
                        dve.wait_ge(*AC(step, "hi", j))
                        tt(uL[:, 2 * j:2 * j + 2, :], heads(Q[2 + j], 2), uH[:, 2 * j:2 * j + 2, :].bitcast(F32), ALU.subtract, step, "lo", j)
                elif kind == "cross":
                    for j in (0, 2):
                        dve.wait_ge(*PE(step, "turned", j))
                        v(V.tensor_copy(cqT[:, 2 * j:2 * j + 2, :], heads(Q[j], 2)), step, "heads", j)
                    for t in range(NT):
                        for pair in range(2):
                            dve.wait_ge(*PE(step, "scores", t, pair))
                            n_ = t * GH + 2 * pair
                            v(V.tensor_reduce(mx[:, n_:n_ + 2], heads(L[2 * t + pair], 2), AX.X, ALU.max))
                        ts(nm[:, t * GH:(t + 1) * GH], mx[:, t * GH:(t + 1) * GH], -1.0 / 16, None, ALU.mult, None, step, "max", t)
                    for t in range(NT):
                        dve.wait_ge(*AC(step, "exp", t, 3))
                        v(V.reciprocal(ri[:, t * GH:(t + 1) * GH], rs[:, t * GH:(t + 1) * GH]))
                        tt(cp[:, t], cp[:, t], over(ri[:, t * GH:(t + 1) * GH], SEQ), ALU.mult, step, "probs", t)
                    for j in range(4):
                        dve.wait_ge(*AC(step, "hi", j))
                        tt(uL[:, 2 * j:2 * j + 2, :], heads(L[j], 2), uH[:, 2 * j:2 * j + 2, :].bitcast(F32), ALU.subtract, step, "lo", j)

    return {"pe": PE.names, "act": AC.names, "dve": VE.names}


_INS = ["x", "p", "ln_pre_mix", "w_in", "conv_w", "a_log", "dt_bias", "gdn_norm", "w_proj_a", "w_proj_b", "w_out",
        "ln_post_mix", "ln_pre_ffn", "w_ffn_gate", "w_ffn_up", "w_ffn_down", "ln_post_ffn", "w_ple", "ln_ple", "w_ple_gate",
        "mem_2", "positions_2", "g_mix_pre_2", "w_in_2", "lambda_q1_2", "lambda_k1_2", "lambda_q2_2", "lambda_k2_2",
        "g_subln_2", "w_pool_2", "pool_scale_2", "w_out_2", "g_mix_post_2", "g_x_pre_2", "g_mem_2", "w_xq_2", "w_xkv_2",
        "w_xo_2", "g_x_post_2", "g_ffn_pre_2", "w_gate_2", "w_up_2", "w_down_2", "g_ffn_post_2"]


def kernel(**inputs):
    import concourse.bacc as bacc
    from concourse.bass_utils import run_bass_kernel_spmd

    arrays = {f"in_{n}": np.ascontiguousarray(inputs[n]) for n in _INS}
    arrays["in_table"], arrays["in_pool_table"] = constant_tables()

    def program(known):
        nc = bacc.Bacc("TRN2", target_bir_lowering=False, num_devices=1)
        a = {k[3:]: nc.dram_tensor(k, v.shape, mybir.dt.from_np(v.dtype), kind="ExternalInput").ap() for k, v in arrays.items()}
        out = nc.dram_tensor("out", (1, SEQ, D), F32, kind="ExternalOutput").ap()
        return nc, build(nc, a, out, known)

    _, known = program({})
    nc, _ = program(known)
    r = run_bass_kernel_spmd(nc, [arrays], core_ids=[0])
    return r.results[0]["out"]
```

```python
from contextlib import ExitStack

import numpy as np

import concourse.bass as bass
from concourse import mybir

F32 = mybir.dt.float32
F32R = mybir.dt.float32r
I32 = mybir.dt.int32
ALU = mybir.AluOpType
ACT = mybir.ActivationFunctionType
AX = mybir.AxisListType

P = 128
SEQ = 256
NT = SEQ // P
D = 1024
KD = D // P
HD = 128
GH = 4
FF = 2816
KF = FF // P
CONV = 4
PLE = 256
EPS = 1e-6
NEG = -3.0e38
LEVELS = 7
LAM_INIT = 0.2
WINDOWS = (2, 4, 8, 16)
RAW, SPLIT = 4, 6
UNIT = 1024
KB = 1024
MAGIC = 1.5 * 2.0 ** 23
TWO_PI = (6.28125, 2029 / 2 ** 20, 2 * np.pi - 6.28125 - 2029 / 2 ** 20)
ROPE2 = 8

COL = {"mq": 0, "mk": D, "mv": 2 * D, "cq": 3 * D, "ck": 4 * D, "cv": 5 * D, "z": 6 * D,
       "ba": 7 * D, "ga": 7 * D + 16, "gb": 8 * D + 16}


def constant_tables():
    i = np.arange(P)
    row, col = i[:, None], i[None, :]
    level = [((row >> l) % 2 == 0) & ((col >> l) == (row >> l) + 1) for l in range(LEVELS)]
    masks = [row == col, row <= col] + level + [np.ones((P, P), bool)]
    square = [m.astype(np.float32) for m in masks]
    square.append(np.where(row <= col, 0, NEG).astype(np.float32))
    square.append(np.where(col <= row, 0, NEG).astype(np.float32))
    inv = (1.0 / (10000.0 ** (np.arange(0, HD, 2, dtype=np.float32) / HD))).astype(np.float32)
    angle = (np.arange(SEQ, dtype=np.float32)[:, None] * inv[None, :]).astype(np.float32)
    cos, sin = np.cos(angle), np.sin(angle)
    cos2 = np.concatenate([cos, cos], 1).reshape(NT, P, HD).transpose(1, 0, 2).reshape(P, -1)
    sin2 = np.concatenate([-sin, sin], 1).reshape(NT, P, HD).transpose(1, 0, 2).reshape(P, -1)
    inv2 = 500000.0 ** (-np.arange(0, 2 * ROPE2, 2, dtype=np.float32) / (2 * ROPE2))
    inv2 = np.broadcast_to(inv2.astype(np.float32), (P, ROPE2))
    table = np.concatenate(square + [cos2, sin2, inv2], 1).astype(np.float32)
    t = np.arange(SEQ)
    pool = []
    for w in WINDOWS:
        seen = (t[:, None] <= t[None, :]) & (t[:, None] > t[None, :] - w)
        mean = seen / np.minimum(t + 1, w)[None, :] - np.eye(SEQ)
        pool.append(mean.reshape(NT, P, SEQ).transpose(1, 0, 2))
    pool = np.stack(pool, 1).reshape(P, -1).astype(np.float32)
    return np.ascontiguousarray(table), np.ascontiguousarray(pool)


class Done:

    def __init__(self, sem, known):
        self.sem, self.known, self.n, self.names = sem, known, 0, {}

    def mark(self, *name):
        self.n += 1
        if name:
            self.names[name] = self.n
        return self.sem, 1

    def __call__(self, *name):
        return self.sem, (self.known[name] if self.known else 1)


def schedule():
    s = [("u",)]
    for gr in range(2):
        s += [("conv", gr, 0)] + ([("ba",)] if gr == 0 else [])
        s += [("conv", gr, 1)] + ([("rates",)] if gr == 0 else [])
        s += [("tri", gr), ("conv", gr, 2), ("decay", gr)]
        s += [("moba", gr, 0), ("tok", gr), ("feat", gr), ("moba", gr, 1), ("within", gr), ("moba", gr, 2)]
        s += [("att", gr)]
        s += [("z", 0), ("inv", 0), ("z", 1), ("ga", 0)] if gr == 0 else [("ga", 1), ("inv", 1), ("gb", 0), ("gb", 1)]
        s += [("scan", gr)]
    s += [("yb",), ("p",), ("proj_a",), ("mem",), ("proj_b",), ("xkv", 0), ("merge",), ("w_out",)]
    s += [("norm", "mix"), ("ple",), ("next", "mix"), ("e",)]
    s += [("ffn", 1, c) for c in range(6)] + [("down", 1), ("norm", "ffn1"), ("xkv", 1), ("next", "ffn1")]
    s += [("ple_gate",), ("norm", "ple"), ("xkv", 2), ("next", "ple")]
    s += [("angles",), ("in2", 0), ("in2", 1), ("rope2",), ("in2", 2), ("heads2",), ("in2", 3)]
    s += [("diff",), ("pool",), ("probs",), ("dnorm",), ("out2",), ("norm", "mix2"), ("xkv", 3), ("next", "mix2")]
    s += [("xq",), ("cross",), ("xo",), ("norm", "x"), ("next", "x")]
    s += [("ffn", 2, c) for c in range(6)] + [("down", 2), ("norm", "ffn2")]
    return s


FILLING = {("decay", 0): [("moba", 0, 0)], ("tok", 0): [("moba", 0, 1)], ("feat", 0): [("moba", 0, 2)],
           ("att", 0): [("z", 0)], ("inv", 0): [("z", 1), ("ga", 0)],
           ("decay", 1): [("moba", 1, 0)], ("tok", 1): [("moba", 1, 1)], ("feat", 1): [("moba", 1, 2)],
           ("att", 1): [("ga", 1)], ("inv", 1): [("gb", 0), ("gb", 1)],
           ("yb",): [("proj_a",)]}
INSIDE = {f for fs in FILLING.values() for f in fs}

BETWEEN = {("merge",): 0, ("next", "ffn1"): 1, ("next", "ple"): 2, ("next", "mix2"): 3}

LATE = ("mix", "x")
PARTS = {what: ((0, 256), (256, 512), (512, 768), (768, D)) if what in LATE else ((0, 256), (256, 512), (512, D))
         for what in ("mix", "ffn1", "ple", "mix2", "x")}
PARTS["ffn2"] = ((0, 512), (512, D))

ROW_ORDER = {("out2",): (4, 5, 6, 7, 0, 1, 2, 3)}

INPUT = {("w_out",): ("merge",), ("ffn", 1, 0): ("next", "mix"), ("ple_gate",): ("next", "ffn1"), ("in2", 0): ("next", "ple"),
         ("xq",): ("next", "mix2"), ("ffn", 2, 0): ("next", "x")}


SCHEDULE = schedule()


def weight_units(w):
    units = []

    def columns(step, m, c0, n=512):
        per = UNIT // n
        for j in range(m.shape[0] // P // per):
            units.append((step, m[j * per * P:(j + 1) * per * P, c0:c0 + n].rearrange("(k p) n -> p k n", p=P)))

    def rows(step, m):
        for k in ROW_ORDER.get(step, range(m.shape[0] // P)):
            units.append((step, m[k * P:(k + 1) * P, :].rearrange("(k p) n -> p k n", p=P)))

    wide = {"proj_a": w["w_proj_a"], "proj_b": w["w_proj_b"], "w_out": w["w_out"], "ple_gate": w["w_ple_gate"],
            "ple": w["w_ple"], "out2": w["w_out_2"], "xq": w["w_xq_2"], "xo": w["w_xo_2"]}
    order = []
    for step in SCHEDULE:
        order += FILLING.get(step, [] if step in INSIDE else [step])
    for step in order:
        kind = step[0]
        if kind == "conv":
            columns(step, w["w_in"], COL["cq"] + step[2] * D + step[1] * 512)
        elif kind == "moba":
            columns(step, w["w_in"], COL["mq"] + step[2] * D + step[1] * 512)
        elif kind in ("z", "ga", "gb"):
            columns(step, w["w_in"], COL[kind] + step[1] * 512)
        elif kind == "xkv":
            columns(step, w["w_xkv_2"], step[1] * 512)
        elif kind == "in2":
            columns(step, w["w_in_2"], step[1] * 512)
        elif kind == "ffn":
            n = 512 if step[2] < FF // 512 else FF % 512
            for m in (("w_ffn_gate", "w_ffn_up") if step[1] == 1 else ("w_gate_2", "w_up_2")):
                columns(step, w[m], step[2] * 512, n)
        elif kind == "down":
            rows(step, w["w_ffn_down"] if step[1] == 1 else w["w_down_2"])
        elif kind in wide:
            rows(step, wide[kind])
    return units


def build(nc, a, out, known):
    w = {n: (a[n][0] if len(a[n].shape) == 3 else a[n]) for n in
         ("w_in", "w_proj_a", "w_proj_b", "w_out", "w_ffn_gate", "w_ffn_up", "w_ffn_down", "w_ple", "w_ple_gate",
          "w_in_2", "w_out_2", "w_xq_2", "w_xkv_2", "w_xo_2", "w_gate_2", "w_up_2", "w_down_2")}
    UNITS = weight_units(w)
    FIRST, LAST = {}, {}
    for n, (step, _) in enumerate(UNITS):
        FIRST.setdefault(step, n)
        LAST[step] = n
    ctx = ExitStack()
    with ctx:
        def sem(name):
            return ctx.enter_context(nc.semaphore(name))

        base = -(-nc.sbuf_base // 32) * 32
        at = [base]

        def place(name, shape, dt=F32, offset=None):
            size = 4 * int(np.prod(shape[1:]))
            if offset is None:
                offset = at[0]
                at[0] += -(-size // 32) * 32
            return nc.alloc_sbuf_tensor_at(name, list(shape), dt, offset=offset)

        raw = place("raw", [P, RAW, UNIT])
        w_hi = place("w_hi", [P, SPLIT, UNIT], F32R)
        w_lo = place("w_lo", [P, SPLIT, UNIT], F32R)
        uH = place("uH", [P, KD, SEQ], F32R)
        uL = place("uL", [P, KD, SEQ], F32R)
        table = place("table", [P, 12 * P + 2 * NT * HD + ROPE2])
        small = place("small", [P, 960])
        Y = at[0]
        yH = place("yH", [P, KD, SEQ], F32R)
        yL = place("yL", [P, KD, SEQ], F32R)
        B = at[0]
        hH = place("hH", [P, KF, SEQ], F32R, Y)
        hL = place("hL", [P, KF, SEQ], F32R, Y + KF * SEQ * 4)

        def big(name, kb, shape, dt=F32):
            return place(name, shape, dt, B + int(kb * KB))

        HALF = [P, NT, GH, HD]
        x0 = big("x0", 0, [P, NT, D])
        z = big("z", 0, [P, NT, D])
        gs = big("gs", 8, [P, NT, D])
        o = big("o", 16, [P, NT, D])
        ln0 = big("ln0", 24, [P, D])
        C = big("C", 24, [P, 3 * GH, SEQ])
        kT = big("kT", 24, HALF)
        kbqT = big("kbqT", 28, [P, NT, GH, 2, HD])
        gsb = big("gsb", 24, [P, NT, D])
        tok = big("tok", 36, [P, NT, 3, GH, HD])
        mtok = big("mtok", 48, [P, 3, NT, GH, HD])
        T = big("T", 60, HALF)
        TT = big("TT", 64, HALF)
        X = big("X", 68, HALF)
        M = big("M", 72, HALF)
        kb = big("kb", 72, HALF)
        vn = big("vn", 76, HALF)
        xn0 = big("xn0", 60, [P, NT, D])
        qTa = big("qTa", 60, [P, GH, SEQ])
        kTa = big("kTa", 64, [P, GH, SEQ])
        pr = big("pr", 68, [P, GH, 3 * P])
        prT = big("prT", 74, [P, GH, 3 * P])
        qeT = big("qeT", 80, [P, GH, HD])
        Dm = big("Dm", 82, HALF)
        AT = big("AT", 86, HALF)
        aT = big("aT", 90, HALF)
        kbe = big("kbe", 94, [P, GH, HD])
        kdec = big("kdec", 96, [P, GH, HD])
        qe = big("qe", 98, [P, GH, HD])
        S = big("S", 72, [P, GH, HD])
        wT = big("wT", 74, [P, GH, HD])
        sq = big("sq", 98, [P, GH, HD])
        sqr = big("sqr", 94, [P, GH, HD])
        h = big("h", 28, [P, NT, D])
        tmp = big("tmp", 36, [P, NT, D])
        sil = big("sil", 36, [P, NT, 512])
        hm = big("hm", 40, [P, NT, 512])
        gA = big("gA", 44, [P, D])
        gB = big("gB", 48, [P, D])
        hg = big("hg", 52, [P, NT, D])
        e = big("e", 60, [P, NT, D])
        mem = big("mem", 60, [P, NT, D])
        xkT = big("xkT", 68, [P, KD, SEQ])
        lnm = big("lnm", 68, [P, D])
        xv = big("xv", 76, [P, NT, D])
        mH = big("mH", 84, [P, KD, SEQ], F32R)
        mL = big("mL", 92, [P, KD, SEQ], F32R)
        pt = big("pt", 16, [P, NT, PLE])
        lnp = big("lnp", 20, [P, D])
        pH = big("pH", 0, [P, PLE // P, SEQ], F32R)
        pL = big("pL", 2, [P, PLE // P, SEQ], F32R)
        xk = [big("xk0", 52, [P, NT, 512]), big("xk1", 20, [P, NT, 512])]
        poolm = big("poolm", 0, [P, 4, NT, SEQ])
        qk2 = big("qk2", 8, [P, NT, 2, 2 * GH, 64])
        v2 = big("v2", 16, [P, NT, GH, HD])
        u2 = big("u2", 20, [P, NT, 512])
        da = big("da", 24, [P, NT, GH, HD])
        dqT = big("dqT", 36, [P, GH, SEQ])
        dkT = big("dkT", 40, [P, GH, SEQ])
        pd = [big("pd0", 52, [P, GH, 3 * P]), big("pd1", 60, [P, GH, 3 * P])]
        pdT = big("pdT", 36, [P, GH, 3 * P])
        poolT = place("poolT", [P, 4, SEQ], F32, Y)
        wpool = place("wpool", [P, 4, P], F32, Y + 4 * KB)
        dsq = place("dsq", [P, GH, HD], F32, Y + 6 * KB)
        gsub = place("gsub", [P, HD], F32, Y + 8 * KB)
        lamv = place("lamv", [P, 4, 64], F32, Y + 9 * KB)
        cq = big("cq", 0, [P, NT, D])
        cqT = big("cqT", 8, [P, KD, SEQ])
        cp = big("cp", 16, [P, NT, GH, SEQ])
        cpT = place("cpT", [P, NT, GH, SEQ], F32, Y)
        used = B + 100 * KB
        assert used <= nc.sbuf_usable_end, (used, nc.sbuf_usable_end)

        def square(n):
            return table[:, n * P:(n + 1) * P]

        ident, tri, ones = square(0), square(1), square(2 + LEVELS)
        neg_kq, neg_qk = square(3 + LEVELS), square(4 + LEVELS)
        base_t = (5 + LEVELS) * P
        cos1 = table[:, base_t:base_t + NT * HD].rearrange("p (t d) -> p t d", t=NT)
        sin1 = table[:, base_t + NT * HD:base_t + 2 * NT * HD].rearrange("p (t d) -> p t d", t=NT)
        inv2 = table[:, base_t + 2 * NT * HD:base_t + 2 * NT * HD + ROPE2]

        free = [0]

        def tiny(n):
            free[0] += n
            assert free[0] <= 960
            return small[:, free[0] - n:free[0]]

        def over(ap, n):
            return ap.unsqueeze(2).to_broadcast([P, ap.shape[1], n])

        def each(ap, n):
            return ap.unsqueeze(1).to_broadcast([P, n, ap.shape[1]])

        ss = tiny(8)
        rv = tiny(16)
        rt = tiny(16)
        rstd0 = tiny(2)
        rstd_m = tiny(2)
        rstd_p = tiny(2)
        rstd_h = tiny(2)
        rstd_o = tiny(2)
        cw = tiny(CONV * 24)
        cwr = tiny(P)
        gnorm = tiny(HD)
        ba_raw = tiny(KD * 16)
        ba = tiny(32)
        dtb, alog = tiny(8), tiny(8)
        beta, g = tiny(16), tiny(16)
        tA, tB = tiny(16), tiny(16)
        ss_p = tA[:, 0:2]
        gc, eg = tiny(8), tiny(8)
        edec = tiny(4)
        s2 = tiny(16)
        rq = tiny(16)
        mx, nm, rs, ri = tiny(16), tiny(16), tiny(16), tiny(16)
        lam = tiny(4)
        posf = tiny(2)
        ang, kk, sn, cs = tiny(16), tiny(16), tiny(16), tiny(16)
        psc = tiny(4)
        r1, so = tiny(8), tiny(16)
        baH = big("baH", 36, [P, KD, 16], F32R)
        baL = big("baL", 37, [P, KD, 16], F32R)
        baT = big("baT", 64, [P, SEQ])
        trg = big("trg", 68, HALF)
        pos_i = place("pos_i", [P, NT], I32, Y + 12 * KB)
        psr = place("psr", [4, P], F32, Y + 12 * KB + 512)
        r2t = [place(f"r2t{n}", [P, 4 * GH * ROPE2], F32, Y + 10 * KB + 512 * n) for n in range(4)]

        L = [ctx.enter_context(nc.psum_tensor(f"L{n}", [P, 512], F32)) for n in range(4)]
        Q = [ctx.enter_context(nc.psum_tensor(f"Q{n}", [P, 512], F32)) for n in range(4)]

        tensor_done, scalar_done, vector_done = sem("tensor_done"), sem("scalar_done"), sem("vector_done")
        w_landed = [sem(f"w_landed{n}") for n in range(RAW)]
        w_hi_there, w_lo_there, w_used = sem("w_hi_there"), sem("w_lo_there"), sem("w_used")
        PE = Done(tensor_done, known.get("pe"))
        AC = Done(scalar_done, known.get("act"))
        VE = Done(vector_done, known.get("dve"))
        load_names = ["x0", "x1", "table", "ln0", "cwr", "ba", "dtb", "alog", "gnorm", "mem", "lnm", "p", "lnp", "xres",
                      "gA_mix", "gA_ffn1", "gA_mix2", "gA_x", "gA_ffn2", "gB_mix", "gB_ple", "gB_mix2", "gB_x",
                      "poolm", "wpool", "gsub", "lamv", "pos", "psc"]
        landed = {n: sem(f"{n}_landed") for n in load_names}
        stored = sem("stored")

        def fed(step, units=None):
            return w_used, (LAST[step] + 1 if units is None else FIRST[step] + units)

        block = ctx.enter_context(nc.Block())

        def tokens(ap):
            return ap.rearrange("(t p) d -> p t d", p=P)

        def row(ap, n):
            return ap.rearrange("(o d) -> o d", o=1).to_broadcast([P, n])

        RES = {"mix": ("ln_post_mix", "ln_pre_ffn"), "ffn1": ("ln_post_ffn", None), "ple": (None, "g_mix_pre_2"),
               "mix2": ("g_mix_post_2", "g_x_pre_2"), "x": ("g_x_post_2", "g_ffn_pre_2"), "ffn2": ("g_ffn_post_2", None)}

        @block.sync
        def _(sp):
            for t in range(NT):
                sp.dma_start(x0[:, t, :], a["x"][0][t * P:(t + 1) * P, :]).then_inc(landed[f"x{t}"], 16)
            sp.dma_start(ln0[:], row(a["ln_pre_mix"][0], D)).then_inc(landed["ln0"], 16)
            for n, (step, src) in enumerate(UNITS):
                if n >= RAW:
                    sp.wait_ge(w_lo_there, n - RAW + 1)
                dst = raw[:, n % RAW, :].rearrange("p (k n) -> p k n", k=src.shape[1])
                sp.dma_start(dst, src).then_inc(w_landed[n % RAW], 16)
            for n in range(2 * NT):
                c, t = n // NT, n % NT
                cc = slice(c * 512, (c + 1) * 512)
                sp.wait_ge(*VE("out", n))
                sp.dma_start(out[0, t * P:(t + 1) * P, cc], h[:, t, cc]).then_inc(stored, 16)
            sp.wait_ge(stored, 2 * NT * 16)

        @block.gpsimd
        def _(pool):
            for n in range(len(UNITS)):
                pool.wait_ge(w_hi_there, n + 1)
                nc.gpsimd.tensor_tensor(w_lo[:, n % SPLIT, :], raw[:, n % RAW, :], w_hi[:, n % SPLIT, :].bitcast(F32),
                                        ALU.subtract).then_inc(w_lo_there, 1)

        @block.tensor
        def _(pe):
            mm, turn = nc.tensor.matmul, nc.tensor.transpose

            def split_mm(dst, sH, sL, wH, wL, start, stop):
                mm(dst, sH, wH, start=start, stop=False)
                mm(dst, sH, wL, start=False, stop=False)
                return mm(dst, sL, wH, start=False, stop=stop)

            def unit(n, k):
                slot = n % SPLIT
                return (w_hi[:, slot, :].rearrange("p (k n) -> p k n", k=k),
                        w_lo[:, slot, :].rearrange("p (k n) -> p k n", k=k))

            def column_unit(step, j, banks, n0=None, n=512, sH=uH, sL=uL):
                n0 = FIRST[step] if n0 is None else n0
                per = UNIT // n
                pe.wait_ge(w_lo_there, n0 + j + 1)
                wH, wL = unit(n0 + j, per)
                for i in range(per):
                    k = j * per + i
                    if n0 == FIRST[step]:
                        turned(step, k)
                    for t in range(NT):
                        last = split_mm(banks[t][:, 0:n], sH[:, k, t * P:(t + 1) * P], sL[:, k, t * P:(t + 1) * P],
                                        wH[:, i, :], wL[:, i, :], k == 0, k == KD - 1)
                last.then_inc(w_used, 1)

            def columns(step, banks, n0=None, n=512, sH=uH, sL=uL):
                for j in range(KD * n // UNIT):
                    column_unit(step, j, banks, n0, n, sH, sL)

            def row_unit(step, k, sH, sL, k_tiles, free_=None):
                n0 = FIRST[step]
                turned(step, k)
                pe.wait_ge(w_lo_there, n0 + k + 1)
                wH, wL = unit(n0 + k, 2)
                tile = ROW_ORDER[step][k] if step in ROW_ORDER else k
                for t in range(NT):
                    s_h, s_l = sH[:, tile, t * P:(t + 1) * P], sL[:, tile, t * P:(t + 1) * P]
                    for c in range(2):
                        if free_:
                            pe.wait_ge(*free_[2 * t + c])
                        last = split_mm(L[2 * t + c][:], s_h, s_l, wH[:, c, :], wL[:, c, :], k == 0, k == k_tiles - 1)
                        if k == k_tiles - 1 and 2 * t + c < 3:
                            last.then_inc(*PE.mark(step, "bank", 2 * t + c))
                last.then_inc(w_used, 1)

            def rows(step, sH, sL, k_tiles):
                for k in range(k_tiles):
                    row_unit(step, k, sH, sL, k_tiles)

            inside = {("moba", 0, 0): ([L[2], L[3]], [VE(("conv", 0, 1), "taps done")]),
                      ("moba", 1, 0): ([L[2], L[3]], [VE(("conv", 1, 1), "taps done")]),
                      ("moba", 0, 1): ([L[0], L[1]], [VE(("conv", 0, 2), "taps done")]),
                      ("moba", 1, 1): ([L[0], L[1]], [VE(("conv", 1, 2), "taps done")]),
                      ("moba", 0, 2): ([L[2], L[3]], [VE(("moba", 0, 0), "rope", 1)]),
                      ("moba", 1, 2): ([L[2], L[3]], [VE(("moba", 1, 0), "rope", 1)]),
                      ("z", 0): ([L[0], L[1]], [VE(("moba", 0, 1), "rope", 1)]),
                      ("z", 1): ([L[2], L[3]], [AC(("moba", 0, 2), "v", 1)]),
                      ("ga", 0): ([L[0], L[1]], [AC(("z", 0))]),
                      ("ga", 1): ([L[0], L[1]], [VE(("moba", 1, 1), "rope", 1)]),
                      ("gb", 0): ([L[2], L[3]], [AC(("moba", 1, 2), "v", 1)]),
                      ("gb", 1): ([L[0], L[1]], [AC(("ga", 1))]),
                      ("proj_a",): (L, [AC(("gb", 1)), VE(("att", 1), "lo", 1)])}

            def fill(step, i):
                n = FIRST[FILLING[step][0]] + i
                f, j = next((f, n - FIRST[f]) for f in FILLING[step] if FIRST[f] <= n <= LAST[f])
                banks, free_ = inside[f]
                if j == 0:
                    for wt in free_:
                        pe.wait_ge(*wt)
                if f == ("proj_a",):
                    row_unit(f, j, yH, yL, KD)
                else:
                    column_unit(f, j, banks)

            def turn_tiles(step, src, tiles, ready):
                for j in tiles:
                    for t in range(NT):
                        pe.wait_ge(*ready(j, t))
                        for i in range(2):
                            last = turn(Q[j][:, i * SEQ + t * P:i * SEQ + (t + 1) * P],
                                        src[:, t, (2 * j + i) * P:(2 * j + i + 1) * P], ident)
                    last.then_inc(*PE.mark(step, "turned", j))

            def turned(step, k):
                if step in INPUT:
                    source = INPUT[step]
                    if k % 2 == 0:
                        if k < KD - 2:
                            turn_next(source, k // 2 + 1)
                        pe.wait_ge(*VE(source, "lo", k // 2))
                    elif k == 1 and BETWEEN.get(source, 2) < 2:
                        turn_keys(BETWEEN[source])

            def turn_next(source, j):
                if source == ("next", "mix"):
                    pe.wait_ge(*AC(("ple",), "out", j))
                elif source in BETWEEN and j >= 2:
                    c = BETWEEN[source]
                    pe.wait_ge(*(AC(("xkv", c), "turned", j - 2) if c < 2 else AC(("xkv", c), j - 2)))
                if source == ("merge",):
                    turn_tiles(source, gs, (j,), lambda j, t: VE(("proj_b",), "sum", t, j // 2))
                else:
                    turn_tiles(source, h if source[1] == "ffn1" else hg, (j,),
                               lambda j, t: VE(("norm", source[1]), "next", t, min(j, len(PARTS[source[1]]) - 1)))

            def turn_keys(c):
                step = ("xkv", c)
                pe.wait_ge(*AC(step, 1))
                for j in range(2):
                    for i in range(2):
                        for t in range(NT):
                            last = turn(Q[2 + j][:, i * SEQ + t * P:i * SEQ + (t + 1) * P],
                                        xk[c][:, t, (2 * j + i) * P:(2 * j + i + 1) * P], ident)
                    last.then_inc(*PE.mark(step, "turned", j))

            for step in SCHEDULE:
                kind = step[0]
                if kind == "u":
                    pe.wait_ge(landed["table"], 16)
                    pe.wait_ge(landed["cwr"], 16)
                    turn(L[3][:, 0:CONV * 24], cwr[0:CONV * 24, :], ident[0:CONV * 24, 0:CONV * 24]).then_inc(*PE.mark(step, "taps"))
                    turn_tiles(step, xn0, range(4), lambda j, t: VE(("u",), "scaled", t))
                elif step in INSIDE:
                    continue
                elif kind == "ba":
                    pe.wait_ge(*VE(("u",), "split"))
                    for k in range(KD):
                        mm(Q[0][0:16, 0:SEQ], baH[:, k, :], uH[:, k, :], start=k == 0, stop=False)
                        mm(Q[0][0:16, 0:SEQ], baH[:, k, :], uL[:, k, :], start=False, stop=False)
                        last = mm(Q[0][0:16, 0:SEQ], baL[:, k, :], uH[:, k, :], start=False, stop=k == KD - 1)
                    last.then_inc(*PE.mark(step))
                elif kind == "rates":
                    pe.wait_ge(*VE(("ba",), "turned"))
                    for t in range(NT):
                        last = turn(Q[1][:, t * 16:t * 16 + 16], baT[0:16, t * P:(t + 1) * P], ident[0:16, 0:16])
                    last.then_inc(*PE.mark(step))
                elif kind == "conv":
                    _, gr, part = step
                    n0 = FIRST[step]
                    b0 = 2 * (part % 2)
                    if part == 2:
                        pe.wait_ge(*VE(("conv", gr, 0), "taps done"))
                    elif gr == 1:
                        pe.wait_ge(*AC(("ga", 0) if part == 0 else ("z", 1)))
                    for pair in range(2):
                        for k in range(KD):
                            if pair == 0 and k % 2 == 0:
                                if gr == 0 and part == 0:
                                    pe.wait_ge(*VE(("u",), "lo", k // 2))
                                pe.wait_ge(w_lo_there, n0 + k // 2 + 1)
                            wH, wL = unit(n0 + k // 2, 2)
                            for ct in (pair, pair + 2):
                                bank = L[b0 + ct // 2][:, (ct % 2) * SEQ:(ct % 2 + 1) * SEQ]
                                sH, sL = wH[:, k % 2, ct * P:(ct + 1) * P], wL[:, k % 2, ct * P:(ct + 1) * P]
                                mm(bank, sH, uH[:, k, :], start=k == 0, stop=False)
                                mm(bank, sH, uL[:, k, :], start=False, stop=False)
                                last = mm(bank, sL, uH[:, k, :], start=False, stop=k == KD - 1)
                            if pair == 1 and k % 2 == 1:
                                last.then_inc(w_used, 1)
                elif kind == "tok":
                    gr = step[1]
                    for part in range(3):
                        for t in range(NT):
                            b = part * NT + t
                            pe.wait_ge(*AC(("conv", gr, part), "silu"))
                            if b in (0, 4):
                                fill(step, b // 4)
                            if b >= 4:
                                pe.wait_ge(*AC(step, "out", (b - 4) // NT, (b - 4) % NT))
                            elif b == 0:
                                pe.wait_ge(*VE(("decay", gr), "decay log", 1))
                            for i in range(GH):
                                last = turn(Q[b % 4][:, i * P:(i + 1) * P], C[:, part * GH + i, t * P:(t + 1) * P], ident)
                            last.then_inc(*PE.mark(step, "turned", part, t))
                    fill(step, 2)
                    fill(step, 3)
                elif kind == "decay":
                    gr = step[1]
                    fill(step, 0)
                    fill(step, 1)
                    pe.wait_ge(*(VE(("rates",), "g") if gr == 0 else AC(("scan", 0), "o", 1)))
                    for t in range(NT):
                        last = mm(Q[3][:, t * 8:t * 8 + GH], tri, g[:, t * 8 + gr * GH:t * 8 + gr * GH + GH], start=True, stop=True)
                    last.then_inc(*PE.mark(step, "gc"))
                    for t in range(NT):
                        pe.wait_ge(*VE(("tri", gr), t))
                        mm(Q[t][:], ones, trg[:, t, :, :].rearrange("p h d -> p (h d)"), start=True, stop=True).then_inc(*PE.mark(step, "rows", t))
                    fill(step, 2)
                    fill(step, 3)
                elif kind == "feat":
                    gr = step[1]
                    fill(step, 0)
                    pe.wait_ge(*AC(("tok", gr), "out", 2, 1))
                    lots = [("kn", 0), ("qn", 0), ("kb", 0), ("kn", 1), ("qn", 1), ("kb", 1), ("qe", 1)]
                    src = {"kn": lambda t, i: tok[:, t, 1, i, :], "kb": lambda t, i: kb[:, t, i, :],
                           "qn": lambda t, i: tok[:, t, 0, i, :], "qe": lambda t, i: qe[:, i, :]}
                    for b, (what, t) in enumerate(lots):
                        if b == 4:
                            fill(step, 1)
                        pe.wait_ge(*VE(step, what, t))
                        if b >= 4:
                            pe.wait_ge(*AC(step, "out", b - 4))
                        for i in range(GH):
                            last = turn(Q[b % 4][:, i * P:(i + 1) * P], src[what](t, i), ident)
                        last.then_inc(*PE.mark(step, "turned", b))
                    fill(step, 2)
                    pe.wait_ge(*AC(step, "out", 6))
                    for t in range(NT):
                        for i in range(GH):
                            last = mm(Q[2 * t + i // 2][:, (i % 2) * 256:(i % 2 + 1) * 256], kT[:, t, i, :],
                                      kbqT[:, t, i, :, :].rearrange("p a b -> p (a b)"), start=True, stop=True)
                            if i % 2:
                                last.then_inc(*PE.mark(step, "kk", t, i // 2))
                    fill(step, 3)
                elif kind == "att":
                    gr = step[1]
                    for b in range(4):
                        part, pair = b // 2, b % 2
                        pe.wait_ge(*VE(("moba", gr, part), "rope", 1))
                        pe.wait_ge(*VE(("feat", gr), "attn", 1, 1))
                        for i in range(2):
                            for t in range(NT):
                                last = turn(Q[b][:, i * SEQ + t * P:i * SEQ + (t + 1) * P], mtok[:, part, t, 2 * pair + i, :], ident)
                        last.then_inc(*PE.mark(step, "turned", b))
                    fill(step, 0)
                    pe.wait_ge(*AC(step, "heads", 3))
                    for i in range(GH):
                        last = mm(Q[0][:, i * P:(i + 1) * P], qTa[:, i, 0:P], kTa[:, i, 0:P], start=True, stop=True)
                    last.then_inc(*PE.mark(step, "scores", 0))
                    for i in range(GH):
                        last = mm(Q[1 + i // 2][:, (i % 2) * SEQ:(i % 2 + 1) * SEQ], qTa[:, i, P:SEQ], kTa[:, i, :], start=True, stop=True)
                        if i % 2:
                            last.then_inc(*PE.mark(step, "scores", 1 + i // 2))
                    for i in range(1, 4):
                        fill(step, i)
                    for b, j in enumerate((0, 1, 2)):
                        pe.wait_ge(*VE(step, "probs", min(b, 1)))
                        for i in range(GH):
                            last = turn(Q[b][:, i * P:(i + 1) * P], pr[:, i, j * P:(j + 1) * P], ident)
                        last.then_inc(*PE.mark(step, "probs turned", b))
                    pe.wait_ge(*AC(("moba", gr, 2), "v", 1))
                    pe.wait_ge(*AC(step, "probs", 2))
                    for i in range(GH):
                        bank = Q[3 if i < 2 else 0]
                        c0 = (i % 2) * SEQ
                        mm(bank[:, c0:c0 + SEQ], mtok[:, 2, 0, i, :], prT[:, i, 0:SEQ], start=True, stop=False)
                        last = mm(bank[:, c0 + P:c0 + SEQ], mtok[:, 2, 1, i, :], prT[:, i, SEQ:3 * P], start=False, stop=True)
                        if i % 2:
                            last.then_inc(*PE.mark(step, "out", i // 2))
                elif kind == "proj_b":
                    pe.wait_ge(*VE(("yb",), "lo", 3))
                    for k in range(KD):
                        row_unit(step, k, uH, uL, KD, [VE(("proj_a",), "mul", b) for b in range(4)] if k == 0 else None)
                elif kind == "inv":
                    gr = step[1]
                    fill(step, 0)
                    pe.wait_ge(*VE(step, "mask", 0))
                    pe.wait_ge(*VE(("att", gr), "lo", 1))
                    for t in range(NT):
                        for i in range(GH):
                            last = turn(Q[t][:, i * P:(i + 1) * P], M[:, t, i, :], ident)
                        last.then_inc(*PE.mark(step, "M0", t))
                    fill(step, 1)
                    for l in range(1, LEVELS):
                        pe.wait_ge(*VE(step, "mask", l))
                        A = [Q[2], Q[3], Q[0], Q[1]] if l % 2 else Q
                        for t in range(NT):
                            pe.wait_ge(*VE(step, "T", l - 1, t))
                            for i in range(GH):
                                last = mm(A[t][:, i * P:(i + 1) * P], M[:, t, i, :], T[:, t, i, :], start=True, stop=True)
                            last.then_inc(*PE.mark(step, "X", l, t))
                        if l > 1:
                            for t in range(NT):
                                for i in range(GH):
                                    last = turn(A[2 + t][:, i * P:(i + 1) * P], T[:, t, i, :], ident)
                                last.then_inc(*PE.mark(step, "turned", l, t))
                        fill(step, l + 1)
                        for t in range(NT):
                            pe.wait_ge(*AC(step, "X", l, t))
                            if l > 1:
                                pe.wait_ge(*AC(step, "TT", l, t))
                            for i in range(GH):
                                one, other = (TT, X) if l < LEVELS - 1 else (X, TT)
                                last = mm(A[t][:, i * P:(i + 1) * P], one[:, t, i, :], other[:, t, i, :], start=True, stop=True)
                            last.then_inc(*PE.mark(step, "Y", l, t))
                elif kind == "scan":
                    gr = step[1]
                    iv = ("inv", gr)
                    pe.wait_ge(*VE(iv, "TT", LEVELS - 1, 1))
                    for t in range(NT):
                        for i in range(GH):
                            last = mm(Q[t][:, i * P:(i + 1) * P], TT[:, t, i, :], tok[:, t, 2, i, :], start=True, stop=True)
                        last.then_inc(*PE.mark(step, "u", t))
                    for i in range(GH):
                        last = mm(Q[2][:, i * P:(i + 1) * P], kbe[:, i, :], TT[:, 1, i, :], start=True, stop=True)
                    last.then_inc(*PE.mark(step, "wT"))
                    pe.wait_ge(*AC(step, "u", 0))
                    for i in range(GH):
                        last = mm(Q[3][:, i * P:(i + 1) * P], kdec[:, i, :], vn[:, 0, i, :], start=True, stop=True)
                    last.then_inc(*PE.mark(step, "S"))
                    for i in range(GH):
                        last = mm(Q[0][:, i * P:(i + 1) * P], aT[:, 0, i, :], vn[:, 0, i, :], start=True, stop=True)
                    last.then_inc(*PE.mark(step, "o", 0))
                    pe.wait_ge(*AC(step, "S"))
                    for i in range(GH):
                        last = mm(Q[2][:, i * P:(i + 1) * P], wT[:, i, :], S[:, i, :], start=True, stop=True)
                    last.then_inc(*PE.mark(step, "wS"))
                    pe.wait_ge(*VE(step, "vn"))
                    for i in range(GH):
                        mm(Q[1][:, i * P:(i + 1) * P], qeT[:, i, :], S[:, i, :], start=True, stop=False)
                        last = mm(Q[1][:, i * P:(i + 1) * P], aT[:, 1, i, :], vn[:, 1, i, :], start=False, stop=True)
                    last.then_inc(*PE.mark(step, "o", 1))
                elif kind == "mem":
                    pe.wait_ge(*VE(("yb",), "lo", 3))
                    turn_tiles(step, mem, range(4), lambda j, t: VE(("mem",), "scaled") if j < 3 else VE(("p",), "lo"))
                elif kind == "yb":
                    pe.wait_ge(*AC(("scan", 1), "o", 1))
                    for i in range(4):
                        fill(step, i)
                    turn_tiles(step, o, range(4), lambda j, t: VE(("yb",), "y", t))
                    for i in range(4, KD):
                        fill(step, i)
                elif kind == "p":
                    pe.wait_ge(landed["p"], 16)
                    for i in range(2):
                        for t in range(NT):
                            pe.wait_ge(*VE(("yb",), "lo", 3))
                            last = turn(Q[3][:, i * SEQ + t * P:i * SEQ + (t + 1) * P], pt[:, t, i * P:(i + 1) * P], ident)
                    last.then_inc(*PE.mark(step, "turned"))
                elif kind == "w_out":
                    rows(step, uH, uL, KD)
                elif kind == "ple":
                    pe.wait_ge(*VE(("merge",), "lo", 3))
                    for k in range(2):
                        n = FIRST[step] + k
                        pe.wait_ge(w_lo_there, n + 1)
                        wH, wL = unit(n, 2)
                        for t in range(NT):
                            for c in range(2):
                                last = split_mm(Q[2 * t + c][:], pH[:, k, t * P:(t + 1) * P], pL[:, k, t * P:(t + 1) * P],
                                                wH[:, c, :], wL[:, c, :], k == 0, k == 1)
                        last.then_inc(w_used, 1)
                elif kind == "xkv":
                    c = step[1]
                    before = {0: VE(("mem",), "lo", 3), 1: VE(("ffn", 1, 5), "lo", 0), 2: VE(("next", "ffn1"), "lo", 3),
                              3: VE(("dnorm",), "lo", 1)}
                    pe.wait_ge(*before[c])
                    for j in range(KD // 2):
                        if j == KD // 2 - 1:
                            turn_next(next(s_ for s_, c_ in BETWEEN.items() if c_ == c), 0)
                        column_unit(step, j, [Q[2], Q[3]], sH=mH, sL=mL)
                elif kind == "next":
                    if step not in BETWEEN:
                        turn_next(step, 0)
                elif kind == "ffn":
                    _, blk, c = step
                    n = 512 if c < 5 else 256
                    half = (LAST[step] + 1 - FIRST[step]) // 2
                    if c > 0:
                        pe.wait_ge(*AC(("ffn", blk, c - 1), "silu", 1))
                    columns(step, [L[0], L[2]], n=n)
                    if c > 0:
                        prev = ("ffn", blk, c - 1)
                        pe.wait_ge(*VE(prev, "hidden", 1))
                        for j in range(2):
                            for i in range(2):
                                for t in range(NT):
                                    last = turn(Q[2 * (c % 2) + j][:, i * SEQ + t * P:i * SEQ + (t + 1) * P],
                                                hm[:, t, (2 * j + i) * P:(2 * j + i + 1) * P], ident)
                            last.then_inc(*PE.mark(prev, "turned", j))
                    if c == 0:
                        pe.wait_ge(*VE(("norm", "mix" if blk == 1 else "x"), "next", 1, 3))
                    columns(step, [L[1], L[3]], FIRST[step] + half, n)
                elif kind == "down":
                    blk = step[1]
                    prev = ("ffn", blk, 5)
                    pe.wait_ge(*AC(prev, "silu", 1))
                    free_ = [VE(prev, "hidden", t) for t in range(NT) for _ in range(2)]
                    for k in range(KF):
                        if k == 1:
                            for i in range(2):
                                for t in range(NT):
                                    last = turn(Q[0][:, i * SEQ + t * P:i * SEQ + (t + 1) * P], hm[:, t, i * P:(i + 1) * P], ident)
                            last.then_inc(*PE.mark(prev, "turned", 0))
                        elif k == KF - 2:
                            pe.wait_ge(*VE(prev, "lo", 0))
                        row_unit(step, k, hH, hL, KF, free_ if k == 0 else None)
                elif kind == "ple_gate":
                    rows(step, uH, uL, KD)
                elif kind == "in2":
                    c = step[1]
                    if c >= 2:
                        pe.wait_ge(*AC(("in2", c - 2), 1))
                    b0 = 2 * (c % 2)
                    columns(step, [L[b0], L[b0 + 1]])
                elif kind == "heads2":
                    pe.wait_ge(*VE(("rope2",), "rope"))
                    pe.wait_ge(*VE(("next", "ple"), "lo", 3))
                    for b in range(4):
                        part, pair = b // 2, b % 2
                        for i in range(2):
                            for t in range(NT):
                                hh = 2 * pair + i
                                last = turn(Q[b][:, i * SEQ + t * P:i * SEQ + (t + 1) * P],
                                            qk2[:, t, part, 2 * hh:2 * hh + 2, :].rearrange("p m d -> p (m d)"), ident)
                        last.then_inc(*PE.mark(step, "turned", b))
                elif kind == "diff":
                    pe.wait_ge(*AC(("heads2",), "heads", 3))
                    pe.wait_ge(*AC(("in2", 2), 1))
                    banks = [[Q[0], Q[1], Q[2]], [Q[3], L[0], L[1]]]
                    for m in range(2):
                        lo, hi = 64 * m, 64 * m + 64
                        for i in range(GH):
                            last = mm(banks[m][0][:, i * P:(i + 1) * P], dqT[lo:hi, i, 0:P], dkT[lo:hi, i, 0:P], start=True, stop=True)
                        last.then_inc(*PE.mark(step, "scores", m, 0))
                        for i in range(GH):
                            last = mm(banks[m][1 + i // 2][:, (i % 2) * SEQ:(i % 2 + 1) * SEQ], dqT[lo:hi, i, P:SEQ], dkT[lo:hi, i, :],
                                      start=True, stop=True)
                            if i % 2:
                                last.then_inc(*PE.mark(step, "scores", m, 1 + i // 2))
                    pe.wait_ge(landed["poolm"], 16)
                    pe.wait_ge(*AC(("in2", 3), 1))
                    for b in range(2):
                        for i in range(2):
                            gi = 2 * b + i
                            mm(L[2 + b][:, i * SEQ:(i + 1) * SEQ], u2[:, 0, gi * P:(gi + 1) * P], poolm[:, gi, 0, :], start=True, stop=False)
                            last = mm(L[2 + b][:, i * SEQ + P:(i + 1) * SEQ], u2[:, 1, gi * P:(gi + 1) * P], poolm[:, gi, 1, P:SEQ],
                                      start=False, stop=True)
                        last.then_inc(*PE.mark(("pool",), "pooled", b))
                elif kind == "pool":
                    pe.wait_ge(landed["wpool"], 16)
                    pe.wait_ge(landed["psc"], 16)
                    pe.wait_ge(*VE(("diff",), "max", 0))
                    turn(Q[2][:, 0:4], psr[:, :], ident[0:4, 0:4]).then_inc(*PE.mark(step, "scale"))
                    for b in range(2):
                        pe.wait_ge(*AC(step, "pooled", b))
                        for i in range(2):
                            gi = 2 * b + i
                            last = mm(Q[b][:, i * SEQ:(i + 1) * SEQ], wpool[:, gi, :], poolT[:, gi, :], start=True, stop=True)
                        last.then_inc(*PE.mark(step, "out", b))
                    pe.wait_ge(*VE(("diff",), "max", 1))
                    for k in range(2):
                        pe.wait_ge(*VE(step, "lo", k))
                        row_unit(("out2",), k, uH, uL, KD)
                elif kind == "probs":
                    for j in range(3):
                        pe.wait_ge(*VE(step, "probs", min(j, 1), GH - 1))
                        for i in range(GH):
                            last = turn(Q[j][:, i * P:(i + 1) * P], pd[0][:, i, j * P:(j + 1) * P], ident)
                        last.then_inc(*PE.mark(step, "probs turned", j))
                    pe.wait_ge(*VE(("pool",), "lo", 2))
                    row_unit(("out2",), 2, uH, uL, KD)
                    pe.wait_ge(*AC(step, "probs", 2))
                    for t in range(NT):
                        bank = Q[3] if t == 0 else Q[0]
                        for i in range(GH):
                            o_ = bank[:, i * P:(i + 1) * P]
                            last = mm(o_, pdT[:, i, t * P:(t + 1) * P], v2[:, 0, i, :], start=True, stop=t == 0)
                            if t == 1:
                                last = mm(o_, pdT[:, i, 2 * P:3 * P], v2[:, 1, i, :], start=False, stop=True)
                        last.then_inc(*PE.mark(step, "out", t))
                elif kind == "dnorm":
                    pe.wait_ge(*VE(("pool",), "lo", 3))
                    row_unit(("out2",), 3, uH, uL, KD)
                    for j in range(2):
                        pe.wait_ge(*VE(step, "da", GH + 2 * j + 1))
                        for i in range(2):
                            for t in range(NT):
                                last = turn(Q[2 + j][:, i * SEQ + t * P:i * SEQ + (t + 1) * P], da[:, t, 2 * j + i, :], ident)
                        last.then_inc(*PE.mark(step, "turned", j))
                elif kind == "out2":
                    for k in range(4, KD):
                        if k % 2 == 0:
                            pe.wait_ge(*VE(("dnorm",), "lo", k // 2 - 2))
                        row_unit(step, k, uH, uL, KD)
                elif kind == "xq":
                    rows(step, uH, uL, KD)
                elif kind == "cross":
                    for j in range(4):
                        for t in range(NT):
                            pe.wait_ge(*AC(("xq",), t, j // 2))
                            for i in range(2):
                                last = turn(Q[j][:, i * SEQ + t * P:i * SEQ + (t + 1) * P],
                                            cq[:, t, (2 * j + i) * P:(2 * j + i + 1) * P], ident)
                        last.then_inc(*PE.mark(step, "turned", j))
                    pe.wait_ge(*AC(step, "heads", 3))
                    pe.wait_ge(*VE(step, "heads", 2))
                    for t in range(NT):
                        for i in range(GH):
                            bank = L[2 * t + i // 2][:, (i % 2) * SEQ:(i % 2 + 1) * SEQ]
                            for k in range(2):
                                last = mm(bank, cqT[:, 2 * i + k, t * P:(t + 1) * P], xkT[:, 2 * i + k, :], start=k == 0, stop=k == 1)
                            if i % 2:
                                last.then_inc(*PE.mark(step, "scores", t, i // 2))
                    for t in range(NT):
                        for j in range(2):
                            pe.wait_ge(*VE(step, "probs", t, j))
                            for i in range(GH):
                                last = turn(Q[2 * t + j][:, i * P:(i + 1) * P], cp[:, t, i, j * P:(j + 1) * P], ident)
                            last.then_inc(*PE.mark(step, "probs turned", t, j))
                        pe.wait_ge(*AC(step, "probs", t, 1))
                        for c in range(2):
                            for i in range(4):
                                f = 4 * c + i
                                for k in range(NT):
                                    last = mm(Q[2 * t + c][:, i * P:(i + 1) * P], xv[:, k, f * P:(f + 1) * P], cpT[:, k, f // 2, t * P:(t + 1) * P],
                                              start=k == 0, stop=k == 1)
                            last.then_inc(*PE.mark(step, "out", t, c))
                elif kind == "xo":
                    for k in range(KD):
                        if k % 4 == 0:
                            pe.wait_ge(*VE(("cross",), "lo", 1, k // 4))
                        row_unit(step, k, uH, uL, KD)

        @block.scalar
        def _(act):
            made = [0]
            copy, actf = nc.scalar.copy, nc.scalar.activation

            def split_up_to(n):
                while made[0] < min(n, len(UNITS)):
                    u = made[0]
                    act.wait_ge(w_landed[u % RAW], 16 * (u // RAW + 1))
                    if u >= SPLIT:
                        act.wait_ge(w_used, u - SPLIT + 1)
                    copy(w_hi[:, u % SPLIT, :], raw[:, u % RAW, :]).then_inc(w_hi_there, 1)
                    made[0] += 1

            def hi_wide(step, dst, tiles=range(4)):
                for j in tiles:
                    act.wait_ge(*PE(step, "turned", j))
                    copy(dst[:, 2 * j:2 * j + 2, :], Q[j][:].rearrange("p (k n) -> p k n", k=2)).then_inc(*AC.mark(step, "hi", j))

            def hi_next(step, then):
                n = UNIT // UNITS[FIRST[then]][1].shape[2]
                for j in range(4):
                    if j > 1:
                        split_up_to(FIRST[then] + (2 * j - 2) // n + SPLIT - 1)
                    hi_wide(step, uH, (j,))
                    if j == 0 and step in BETWEEN:
                        memory(BETWEEN[step])
                    elif j == 0 and step == ("next", "mix"):
                        embedding((2, 3))
                    elif j == 1 and BETWEEN.get(step, 2) < 2:
                        c = BETWEEN[step]
                        split_up_to(FIRST[then] + 1 + SPLIT - 1)
                        for i in range(2):
                            act.wait_ge(*PE(("xkv", c), "turned", i))
                            copy(xkT[:, 4 * c + 2 * i:4 * c + 2 * i + 2, :], Q[2 + i][:].rearrange("p (k n) -> p k n", k=2)).then_inc(*AC.mark(("xkv", c), "turned", i))

            def memory(c):
                step = ("xkv", c)
                act.wait_ge(*VE(("mem",), "rstd"))
                act.wait_ge(*fed(step))
                for t in range(NT):
                    dst = xk[c][:, t, :] if c < 2 else xv[:, t, (c - 2) * 512:(c - 1) * 512]
                    actf(dst, Q[2 + t][:], ACT.Copy, scale=rstd_m[:, t:t + 1]).then_inc(*AC.mark(step, t))

            def embedding(banks):
                act.wait_ge(*fed(("ple",)))
                for b in banks:
                    copy(e[:, b // 2, b % 2 * 512:(b % 2 + 1) * 512], Q[b][:]).then_inc(*AC.mark(("ple",), "out", b))

            def silu(gr, part):
                act.wait_ge(*VE(("conv", gr, part), "taps done"))
                cv = C[:, part * GH:(part + 1) * GH, :]
                actf(cv, cv, ACT.Silu).then_inc(*AC.mark(("conv", gr, part), "silu"))

            def load(name, dst, src, *waits, **how):
                for wt in waits:
                    act.wait_ge(*wt)
                act.dma_start(dst, src, **how).then_inc(landed[name], 16)

            def fill(step, i):
                split_up_to(FIRST[FILLING[step][0]] + i + SPLIT)

            load("table", table[:], a["table"])
            load("cwr", cwr[0:CONV * 24, :], a["conv_w"][0].rearrange("j (t c) -> (j t) c", c=P))
            load("ba", ba_raw.rearrange("p (k n) -> p k n", k=KD),
                 w["w_in"][:, COL["ba"]:COL["ba"] + 16].rearrange("(k p) n -> p k n", p=P))
            load("dtb", dtb, row(a["dt_bias"][0], 8))
            load("alog", alog, row(a["a_log"][0], 8))
            load("gnorm", gnorm, row(a["gdn_norm"][0], HD))
            consumed = 0
            for step in SCHEDULE:
                kind = step[0]
                if step in LAST:
                    consumed = max(consumed, LAST[step] + 1)
                if kind != "u" and kind != "ffn":
                    split_up_to(consumed + SPLIT - 1)
                if kind == "u":
                    act.wait_ge(*VE(step, "warm"))
                    actf(rt, rt, ACT.Square).then_inc(*AC.mark(step, "warm"))
                    for t in range(NT):
                        act.wait_ge(landed[f"x{t}"], 16)
                        actf(xn0[:, t, :], x0[:, t, :], ACT.Square, accum_out=ss[:, t:t + 1]).then_inc(*AC.mark(step, "ss", t))
                    for j in range(4):
                        split_up_to(j + 2)
                        hi_wide(step, uH, (j,))
                elif kind == "rates":
                    split_up_to(consumed + SPLIT + 1)
                    act.wait_ge(*VE(step, "ba"))
                    bav = ba.rearrange("p (t n) -> p t n", t=NT)
                    actf(beta.rearrange("p (t n) -> p t n", t=NT), bav[:, :, 0:8], ACT.Sigmoid).then_inc(*AC.mark(step, "beta"))
                    act.wait_ge(landed["alog"], 16)
                    actf(alog, alog, ACT.Exp).then_inc(*AC.mark(step, "alog"))
                    act.wait_ge(*VE(step, "abs"))
                    actf(tB, tB, ACT.Exp, scale=-1.0).then_inc(*AC.mark(step, "exp"))
                    act.wait_ge(*VE(step, "1+exp"))
                    actf(tB, tB, ACT.Ln).then_inc(*AC.mark(step, "ln"))
                elif kind == "conv":
                    if step[2] > 0:
                        silu(step[1], step[2] - 1)
                elif kind == "decay":
                    fill(step, 0)
                    silu(step[1], 2)
                    fill(step, 1)
                    act.wait_ge(*VE(step, "gc"))
                    actf(eg, gc, ACT.Exp).then_inc(*AC.mark(step, "eg"))
                    act.wait_ge(*VE(step, "glast"))
                    actf(edec, edec, ACT.Exp).then_inc(*AC.mark(step, "edec"))
                    for t in range(NT):
                        act.wait_ge(*VE(step, "decay log", t))
                        actf(Dm[:, t], Dm[:, t], ACT.Exp).then_inc(*AC.mark(step, "decay", t))
                        fill(step, 2 + t)
                elif kind == "tok":
                    for part in range(3):
                        for t in range(NT):
                            if part != 1 and t == 0:
                                fill(step, part // 2)
                            act.wait_ge(*PE(step, "turned", part, t))
                            if part == 0 and t == 0 and step[1] == 1:
                                act.wait_ge(*PE(("scan", 0), "o", 1))
                            copy(tok[:, t, part, :, :], Q[(part * NT + t) % 4][:].rearrange("p (h d) -> p h d", h=GH)).then_inc(*AC.mark(step, "out", part, t))
                            if part < 2:
                                act.wait_ge(*AC(step, "out", part, t))
                                if part + t == 0:
                                    act.wait_ge(*VE(("moba", step[1], 0), "rope", 1))
                                if part + t > 0:
                                    pt_, pp_ = (0, part) if t == 1 else (1, part - 1)
                                    act.wait_ge(*VE(step, "sum", pp_, pt_))
                                elif step[1] == 1:
                                    act.wait_ge(*VE(("scan", 0), "sum", 1))
                                actf(sq[:], tok[:, t, part, :, :], ACT.Square).then_inc(*AC.mark(step, "sq", part, t))
                    fill(step, 2)
                    fill(step, 3)
                elif kind == "moba":
                    _, gr, part = step
                    if part == 2:
                        act.wait_ge(*fed(step))
                        if gr == 1:
                            act.wait_ge(*PE(("att", 0), "out", 1))
                        for t in range(NT):
                            copy(mtok[:, 2, t, :, :], L[2 + t][:].rearrange("p (h d) -> p h d", h=GH)).then_inc(*AC.mark(step, "v", t))
                elif kind == "feat":
                    gr = step[1]
                    outs = [kT[:, 0], kbqT[:, 0, :, 1, :], kbqT[:, 0, :, 0, :], kT[:, 1], kbqT[:, 1, :, 1, :], kbqT[:, 1, :, 0, :], qeT[:]]
                    fill(step, 0)
                    for b in range(7):
                        if b == 4:
                            fill(step, 1)
                        act.wait_ge(*PE(step, "turned", b))
                        copy(outs[b], Q[b % 4][:].rearrange("p (h d) -> p h d", h=GH)).then_inc(*AC.mark(step, "out", b))
                    fill(step, 2)
                    fill(step, 3)
                elif kind == "att":
                    gr = step[1]
                    outs = [qTa[:, 0:2, :], qTa[:, 2:4, :], kTa[:, 0:2, :], kTa[:, 2:4, :]]
                    for b in range(4):
                        act.wait_ge(*PE(step, "turned", b))
                        copy(outs[b], Q[b][:].rearrange("p (h d) -> p h d", h=2)).then_inc(*AC.mark(step, "heads", b))
                    fill(step, 0)
                    for t in range(NT):
                        act.wait_ge(*VE(step, "max", t))
                        for i in range(GH):
                            p_ = pr[:, i, 0:P] if t == 0 else pr[:, i, P:3 * P]
                            n_ = t * GH + i
                            actf(p_, p_, ACT.Exp, bias=nm[:, n_:n_ + 1], accum_out=rs[:, n_:n_ + 1]).then_inc(*AC.mark(step, "exp", t, i))
                    for i in range(1, 4):
                        fill(step, i)
                    for b in range(3):
                        act.wait_ge(*PE(step, "probs turned", b))
                        copy(prT[:, :, b * P:(b + 1) * P], Q[b][:].rearrange("p (h d) -> p h d", h=GH)).then_inc(*AC.mark(step, "probs", b))
                    for b in range(2):
                        act.wait_ge(*PE(step, "out", b))
                        copy(yH[:, gr * GH + 2 * b:gr * GH + 2 * b + 2, :], Q[3 if b == 0 else 0][:].rearrange("p (h d) -> p h d", h=2)).then_inc(*AC.mark(step, "hi", b))
                elif kind in ("z", "ga", "gb"):
                    c = step[1]
                    act.wait_ge(*fed(step))
                    dst = {"z": z, "ga": gs, "gb": gsb}[kind]
                    fn = ACT.Silu if kind == "z" else ACT.Sigmoid
                    banks = {"z": ((0, 1), (2, 3)), "ga": ((0, 1), (0, 1)), "gb": ((2, 3), (0, 1))}[kind][c]
                    for t in range(NT):
                        last = actf(dst[:, t, c * 512:(c + 1) * 512], L[banks[t]][:], fn)
                    last.then_inc(*AC.mark(step))
                elif kind == "inv":
                    fill(step, 0)
                    for l in range(1, LEVELS):
                        fill(step, l)
                        for t in range(NT):
                            act.wait_ge(*PE(step, "X", l, t))
                            copy(X[:, t], (Q[(t + 2) % 4] if l % 2 else Q[t])[:].rearrange("p (h d) -> p h d", h=GH)).then_inc(*AC.mark(step, "X", l, t))
                        if l > 1:
                            for t in range(NT):
                                act.wait_ge(*PE(step, "turned", l, t))
                                copy(TT[:, t], (Q[t] if l % 2 else Q[2 + t])[:].rearrange("p (h d) -> p h d", h=GH)).then_inc(*AC.mark(step, "TT", l, t))
                    fill(step, LEVELS)
                elif kind == "scan":
                    for t in range(NT):
                        act.wait_ge(*PE(step, "u", t))
                        copy(vn[:, t], Q[t][:].rearrange("p (h d) -> p h d", h=GH)).then_inc(*AC.mark(step, "u", t))
                    act.wait_ge(*PE(step, "wT"))
                    copy(wT[:], Q[2][:].rearrange("p (h d) -> p h d", h=GH)).then_inc(*AC.mark(step, "wT"))
                    act.wait_ge(*PE(step, "S"))
                    copy(S[:], Q[3][:].rearrange("p (h d) -> p h d", h=GH)).then_inc(*AC.mark(step, "S"))
                    gr = step[1]
                    for t in range(NT):
                        act.wait_ge(*PE(step, "o", t))
                        ot = o[:, t, gr * 512:(gr + 1) * 512].rearrange("p (h d) -> p h d", h=GH)
                        copy(ot, Q[t][:].rearrange("p (h d) -> p h d", h=GH)).then_inc(*AC.mark(step, "o", t))
                        act.wait_ge(*AC(step, "o", t))
                        if t == 1:
                            act.wait_ge(*VE(step, "sum", 0))
                        actf(sq[:], ot, ACT.Square).then_inc(*AC.mark(step, "sq", t))
                    if gr == 1:
                        load("mem", mem[:], tokens(a["mem_2"][0]), PE(("scan", 1), "o", 1), AC(("scan", 1), "u", 1))
                        load("lnm", lnm[:], row(a["g_mem_2"], D), VE(("inv", 1), "TT", LEVELS - 1, 1))
                elif kind == "mem":
                    hi_wide(step, mH)
                elif kind == "yb":
                    for i in range(4):
                        fill(step, i)
                    hi_wide(step, uH)
                    act.wait_ge(landed["mem"], 16)
                    act.wait_ge(*PE(("scan", 1), "u", 1))
                    for t in range(NT):
                        actf(xv[:, t, :], mem[:, t, :], ACT.Square, accum_out=ss[:, 4 + t:5 + t]).then_inc(*AC.mark(("mem",), "ss", t))
                    load("p", pt[:], tokens(a["p"][0, 0]), VE(("yb",), "lo", 3))
                    load("lnp", lnp[:], row(a["ln_ple"][0], D))
                    load("gA_mix", gA[:], row(a["ln_post_mix"][0], D))
                    load("gB_mix", gB[:], row(a["ln_pre_ffn"][0], D), PE(("att", 1), "out", 1))
                    for i in range(4, KD):
                        fill(step, i)
                elif kind == "p":
                    act.wait_ge(*PE(step, "turned"))
                    copy(pH[:], Q[3][:].rearrange("p (k n) -> p k n", k=2)).then_inc(*AC.mark(step, "hi"))
                elif kind == "merge":
                    load("xres", h[:], tokens(a["x"][0]), VE(("proj_b",), "sum", 1, 1))
                    hi_next(step, ("w_out",))
                elif kind == "ple":
                    embedding((0, 1))
                elif kind == "e":
                    for t in range(NT):
                        act.wait_ge(*AC(("ple",), "out", 2 * t + 1))
                        actf(xv[:, t, :], e[:, t, :], ACT.Square, accum_out=ss_p[:, t:t + 1]).then_inc(*AC.mark(step, "ss", t))
                elif kind == "norm":
                    what = step[1]
                    src_step = {"mix": ("w_out",), "ffn1": ("down", 1), "ple": ("ple_gate",), "mix2": ("out2",), "x": ("xo",),
                                "ffn2": ("down", 2)}[what]
                    if what in ("ffn1", "ffn2"):
                        act.wait_ge(*PE(("ffn", 1 if what == "ffn1" else 2, 5), "turned", 0))
                    for t in range(NT):
                        for c in range(2):
                            b = 2 * t + c
                            act.wait_ge(*(PE(src_step, "bank", b) if b < 3 else fed(src_step)))
                            out_ = tmp[:, t, c * 512:(c + 1) * 512]
                            if what == "ple":
                                actf(out_, L[b][:], ACT.Sigmoid).then_inc(*AC.mark(step, "gate", t, c))
                            else:
                                actf(out_, L[b][:], ACT.Square, scale=D ** -0.5, accum_out=ss[:, b:b + 1]).then_inc(*AC.mark(step, "ss", b))
                    if what == "ffn1":
                        load("pos", pos_i[:], a["positions_2"][0].rearrange("(t p) -> p t", p=P), allow_slow_non_contiguous=True)
                        load("wpool", wpool[:], a["w_pool_2"].rearrange("g c d -> c g d"))
                        load("gsub", gsub[:], row(a["g_subln_2"], HD))
                        for n, v_ in enumerate(("lambda_q1_2", "lambda_k1_2", "lambda_q2_2", "lambda_k2_2")):
                            act.dma_start(lamv[:, n, :], row(a[v_], 64)).then_inc(landed["lamv"], 16)
                        load("psc", psr[:], a["pool_scale_2"].rearrange("(g c) -> g c", c=P))
                        load("poolm", poolm[:].rearrange("p a b c -> p (a b c)"), a["pool_table"], fed(("down", 1)))
                elif kind == "next":
                    what = step[1]
                    hi_next(step, next(s_ for s_, i_ in INPUT.items() if i_ == step))
                    if what != "ffn1":
                        for t in range(NT):
                            act.wait_ge(*VE(("norm", what), "next", t, len(PARTS[what]) - 1))
                            actf(tmp[:, t, :], h[:, t, :], ACT.Square, accum_out=ss[:, 4 + t:5 + t]).then_inc(*AC.mark(step, "hss", t))
                    if what == "mix":
                        load("gA_ffn1", gA[:], row(a["ln_post_ffn"][0], D), VE(("norm", what), "next", 1, len(PARTS[what]) - 1))
                    if what == "ffn1":
                        load("gB_ple", gB[:], row(a["g_mix_pre_2"], D), VE(("norm", what), "next", 1, len(PARTS[what]) - 1))
                        load("gA_mix2", gA[:], row(a["g_mix_post_2"], D))
                    if what == "ple":
                        load("gB_mix2", gB[:], row(a["g_x_pre_2"], D), VE(("norm", what), "next", 1, len(PARTS[what]) - 1))
                    if what == "mix2":
                        load("gA_x", gA[:], row(a["g_x_post_2"], D), VE(("norm", what), "next", 1, len(PARTS[what]) - 1))
                        load("gB_x", gB[:], row(a["g_ffn_pre_2"], D))
                    if what == "x":
                        load("gA_ffn2", gA[:], row(a["g_ffn_post_2"], D), VE(("norm", what), "next", 1, len(PARTS[what]) - 1))
                elif kind == "ffn":
                    _, blk, c = step
                    n = 512 if c < 5 else 256
                    half = (LAST[step] + 1 - FIRST[step]) // 2
                    split_up_to(FIRST[step] + half + SPLIT - 1)
                    act.wait_ge(*fed(step, half))
                    if c > 0:
                        act.wait_ge(*VE(("ffn", blk, c - 1), "hidden", 1))
                    else:
                        act.wait_ge(*VE(("next", "mix" if blk == 1 else "x"), "rstd"))
                    for t in range(NT):
                        actf(sil[:, t, 0:n], L[2 * t][:, 0:n], ACT.Silu, scale=rstd_h[:, t:t + 1]).then_inc(*AC.mark(step, "silu", t))
                    todo = ([c - 1] if c > 0 else []) + ([5] if c == 5 else [])
                    for c_ in todo:
                        prev = ("ffn", blk, c_)
                        if c_ == 5:
                            split_up_to(FIRST[("down", blk)] + SPLIT)
                        for j in range(2 if c_ < 5 else 1):
                            act.wait_ge(*PE(prev, "turned", j))
                            bank = Q[2 * ((c_ + 1) % 2) + j]
                            copy(hH[:, 4 * c_ + 2 * j:4 * c_ + 2 * j + 2, :], bank[:].rearrange("p (k n) -> p k n", k=2)).then_inc(*AC.mark(prev, "hi", j))
                    split_up_to(consumed + SPLIT - 1)
                elif kind == "in2":
                    c = step[1]
                    act.wait_ge(*fed(step))
                    if c == 0:
                        act.wait_ge(*VE(("next", "ple"), "rstd"))
                    for t in range(NT):
                        src = L[2 * (c % 2) + t][:]
                        if c < 2:
                            dst, src = qk2[:, t, c, :, :], src.rearrange("p (h d) -> p h d", h=2 * GH)
                        elif c == 2:
                            dst, src = v2[:, t, :, :], src.rearrange("p (h d) -> p h d", h=GH)
                        else:
                            dst = u2[:, t, :]
                        actf(dst, src, ACT.Copy, scale=rstd_h[:, t:t + 1]).then_inc(*AC.mark(step, t))
                elif kind == "angles":
                    act.wait_ge(*VE(step, "angles"))
                    actf(sn, sn, ACT.Sin).then_inc(*AC.mark(step, "sin"))
                    actf(cs, cs, ACT.Sin).then_inc(*AC.mark(step, "cos"))
                    act.wait_ge(*VE(step, "lam sums"))
                    actf(lam[:, 0:2], lam[:, 0:2], ACT.Exp).then_inc(*AC.mark(step, "lam"))
                elif kind == "heads2":
                    outs = [dqT[:, 0:2, :], dqT[:, 2:4, :], dkT[:, 0:2, :], dkT[:, 2:4, :]]
                    for b in range(4):
                        act.wait_ge(*PE(step, "turned", b))
                        copy(outs[b], Q[b][:].rearrange("p (h d) -> p h d", h=2)).then_inc(*AC.mark(step, "heads", b))
                elif kind == "pool":
                    for m in range(2):
                        for t in range(NT):
                            act.wait_ge(*VE(("diff",), "max" if t else "first max", m))
                            for i in range(GH):
                                p_ = pd[m][:, i, 0:P] if t == 0 else pd[m][:, i, P:3 * P]
                                n_ = m * 8 + t * GH + i
                                actf(p_, p_, ACT.Exp, bias=nm[:, n_:n_ + 1], accum_out=rs[:, n_:n_ + 1]).then_inc(*AC.mark(("probs",), "exp", m, t, i))
                            if m == 0 and t == 1:
                                for b in range(2):
                                    act.wait_ge(*PE(step, "pooled", b))
                                    copy(poolT[:, 2 * b:2 * b + 2, :], L[2 + b][:].rearrange("p (k n) -> p k n", k=2)).then_inc(*AC.mark(step, "pooled", b))
                        if m == 0:
                            act.wait_ge(*VE(step, "scale"))
                            for b in range(2):
                                act.wait_ge(*PE(step, "out", b))
                                for i in range(2):
                                    gi = 2 * b + i
                                    actf(uH[:, 4 + gi, :], Q[b][:, i * SEQ:(i + 1) * SEQ], ACT.Copy, scale=psc[:, gi:gi + 1]).then_inc(*AC.mark(step, "hi", gi))
                    split_up_to(FIRST[("out2",)] + 2 + SPLIT - 1)
                elif kind == "probs":
                    for b in range(3):
                        act.wait_ge(*PE(step, "probs turned", b))
                        copy(pdT[:, :, b * P:(b + 1) * P], Q[b][:].rearrange("p (h d) -> p h d", h=GH)).then_inc(*AC.mark(step, "probs", b))
                    split_up_to(FIRST[("out2",)] + 3 + SPLIT - 1)
                    for t in range(NT):
                        act.wait_ge(*PE(step, "out", t))
                        bank = Q[3] if t == 0 else Q[0]
                        copy(da[:, t], bank[:].rearrange("p (h d) -> p h d", h=GH)).then_inc(*AC.mark(step, "out", t))
                        act.wait_ge(*AC(step, "out", t))
                        if t == 1:
                            act.wait_ge(*VE(step, "sum", 0))
                        actf(dsq[:], da[:, t], ACT.Square).then_inc(*AC.mark(step, "sq", t))
                elif kind == "dnorm":
                    split_up_to(FIRST[("out2",)] + 4 + SPLIT - 1)
                    for j in range(2):
                        act.wait_ge(*PE(step, "turned", j))
                        copy(uH[:, 2 * j:2 * j + 2, :], Q[2 + j][:].rearrange("p (k n) -> p k n", k=2)).then_inc(*AC.mark(step, "hi", j))
                elif kind == "xq":
                    act.wait_ge(*VE(("next", "mix2"), "rstd"))
                    for t in range(NT):
                        for c in range(2):
                            act.wait_ge(*(PE(step, "bank", 2 * t + c) if 2 * t + c < 3 else fed(step)))
                            actf(cq[:, t, c * 512:(c + 1) * 512], L[2 * t + c][:], ACT.Copy, scale=rstd_h[:, t:t + 1]).then_inc(*AC.mark(step, t, c))
                elif kind == "cross":
                    for j in (1, 3):
                        act.wait_ge(*PE(step, "turned", j))
                        copy(cqT[:, 2 * j:2 * j + 2, :], Q[j][:].rearrange("p (k n) -> p k n", k=2)).then_inc(*AC.mark(step, "heads", j))
                    for t in range(NT):
                        act.wait_ge(*VE(step, "max", t))
                        for i in range(GH):
                            n_ = t * GH + i
                            actf(cp[:, t, i, :], L[2 * t + i // 2][:, (i % 2) * SEQ:(i % 2 + 1) * SEQ], ACT.Exp, scale=1.0 / 16,
                                 bias=nm[:, n_:n_ + 1], accum_out=rs[:, n_:n_ + 1]).then_inc(*AC.mark(step, "exp", t, i))
                        for j in range(2):
                            act.wait_ge(*PE(step, "probs turned", t, j))
                            copy(cpT[:, j, :, t * P:(t + 1) * P], Q[2 * t + j][:].rearrange("p (h d) -> p h d", h=GH)).then_inc(*AC.mark(step, "probs", t, j))
                    for t in range(NT):
                        for c in range(2):
                            act.wait_ge(*PE(step, "out", t, c))
                            copy(uH[:, 4 * c:4 * c + 4, t * P:(t + 1) * P], Q[2 * t + c][:].rearrange("p (h d) -> p h d", h=4)).then_inc(*AC.mark(step, "hi", t, c))

        @block.vector
        def _(dve):
            V = nc.vector

            def v(ins, *name):
                ins.then_inc(*VE.mark(*name))
                dve.wait_ge(vector_done, VE.n)

            def vector_next(ins, *name):
                ins.then_inc(*VE.mark(*name))
                dve.wait_ge(vector_done, VE.n - 1)

            def settle():
                dve.wait_ge(vector_done, VE.n)

            def tt(out_, x_, y_, op, *name):
                v(V.tensor_tensor(out_, x_, y_, op), *name)

            def ts(out_, x_, s1, s2_, op0, op1, *name):
                if op1 is None:
                    v(V.tensor_scalar(out_, x_, s1, None, op0), *name)
                else:
                    v(V.tensor_scalar(out_, x_, s1, s2_, op0, op1), *name)

            def stt(out_, x_, s_, y_, op0, op1, *name):
                v(V.scalar_tensor_tensor(out=out_, in0=x_, scalar=s_, in1=y_, op0=op0, op1=op1), *name)

            def rsqrt(dst, src, *name):
                n = src.shape[1]
                t_ = rt[:, 0:n]
                ts(dst.bitcast(I32), src.bitcast(I32), -0.5, 1597463007.0, ALU.mult, ALU.add)
                for i in range(3):
                    stt(t_, src, -0.5, dst, ALU.mult, ALU.mult)
                    tt(t_, t_, dst, ALU.mult)
                    stt(dst, t_, 1.5, dst, ALU.add, ALU.mult, *(name if i == 2 else ()))

            def lo_wide(step, dH, dL, tiles=range(4)):
                for j in tiles:
                    dve.wait_ge(*AC(step, "hi", j))
                    tt(dL[:, 2 * j:2 * j + 2, :], Q[j][:].rearrange("p (k n) -> p k n", k=2), dH[:, 2 * j:2 * j + 2, :].bitcast(F32),
                       ALU.subtract, step, "lo", j)

            def heads(bank, n=GH):
                return bank[:].rearrange("p (h d) -> p h d", h=n)

            def scaled_probs(m, t):
                hs = slice(8 * m + t * GH, 8 * m + (t + 1) * GH)
                p_ = pd[m][:, :, 0:P] if t == 0 else pd[m][:, :, P:3 * P]
                dve.wait_ge(*AC(("probs",), "exp", m, t, 3))
                v(V.reciprocal(ri[:, hs], rs[:, hs]))
                if m == 0:
                    v(V.tensor_tensor(p_, p_, over(ri[:, hs], p_.shape[2]), ALU.mult))
                    return
                ts(ri[:, hs], ri[:, hs], lam[:, 2:3], -1.0, ALU.mult, ALU.mult)
                cc = slice(0, P) if t == 0 else slice(P, 3 * P)
                for i in range(GH):
                    vector_next(V.scalar_tensor_tensor(out=pd[0][:, i, cc], in0=pd[1][:, i, cc], scalar=ri[:, hs.start + i:hs.start + i + 1],
                                                       in1=pd[0][:, i, cc], op0=ALU.mult, op1=ALU.add), ("probs",), "probs", t, i)

            def gained(b):
                t, c = b // 2, b % 2
                vector_next(V.tensor_tensor(tmp[:, t, c * 512:(c + 1) * 512], L[b][:], gA[:, c * 512:(c + 1) * 512], ALU.mult))

            def norm_part(what, part):
                post, pre = RES[what]
                step = ("norm", what)
                c0, c1 = PARTS[what][part]
                cc = slice(c0, c1)
                for t in range(NT):
                    name = {"ffn1": (step, "next", t, part), "ffn2": ("out", 2 * part + t)}.get(what, ())
                    if post:
                        vector_next(V.scalar_tensor_tensor(out=h[:, t, cc], in0=tmp[:, t, cc], scalar=rstd_o[:, t:t + 1], in1=h[:, t, cc],
                                                           op0=ALU.mult, op1=ALU.add), *name)
                    else:
                        dve.wait_ge(*AC(step, "gate", t, c0 // 512))
                        v(V.tensor_tensor(tmp[:, t, cc], tmp[:, t, cc], e[:, t, cc], ALU.mult))
                        vector_next(V.tensor_tensor(h[:, t, cc], h[:, t, cc], tmp[:, t, cc], ALU.add), *name)
                if pre:
                    for t in range(NT):
                        vector_next(V.tensor_tensor(hg[:, t, cc], h[:, t, cc], gB[:, cc], ALU.mult), step, "next", t, part)

            for step in SCHEDULE:
                kind = step[0]
                if kind == "u":
                    v(V.memset(rt, 1.0), step, "warm")
                    dve.wait_ge(*AC(step, "ss", 1))
                    ts(rv[:, 0:2], ss[:, 0:2], 1.0 / D, EPS, ALU.mult, ALU.add)
                    rsqrt(rstd0, rv[:, 0:2])
                    dve.wait_ge(landed["ln0"], 16)
                    for t in range(NT):
                        vector_next(V.scalar_tensor_tensor(out=xn0[:, t, :], in0=x0[:, t, :], scalar=rstd0[:, t:t + 1], in1=ln0[:],
                                                           op0=ALU.mult, op1=ALU.mult), step, "scaled", t)
                    dve.wait_ge(*PE(step, "taps"))
                    v(V.tensor_copy(cw, L[3][:, 0:CONV * 24]))
                    lo_wide(step, uH, uL)
                    dve.wait_ge(landed["ba"], 16)
                    bv = ba_raw.rearrange("p (k n) -> p k n", k=KD)
                    v(V.tensor_copy(baH[:], bv))
                    tt(baL[:], bv, baH[:].bitcast(F32), ALU.subtract, step, "split")
                elif kind == "ba":
                    dve.wait_ge(*PE(step))
                    v(V.tensor_copy(baT[0:16, :], Q[0][0:16, 0:SEQ]), step, "turned")
                elif kind == "rates":
                    dve.wait_ge(*PE(step))
                    v(V.tensor_copy(ba, Q[1][:, 0:32]), step, "ba")
                    bav = ba.rearrange("p (t n) -> p t n", t=NT)
                    tAv = tA.rearrange("p (t n) -> p t n", t=NT)
                    dve.wait_ge(landed["dtb"], 16)
                    tt(tAv, bav[:, :, 8:16], each(dtb, NT), ALU.add)
                    ts(tB, tA, -1.0, None, ALU.mult, None)
                    tt(tB, tB, tA, ALU.max, step, "abs")
                    dve.wait_ge(*AC(step, "exp"))
                    ts(tB, tB, 1.0, None, ALU.add, None, step, "1+exp")
                    ts(tA, tA, 0.0, None, ALU.max, None)
                    dve.wait_ge(*AC(step, "ln"))
                    tt(tA, tA, tB, ALU.add)
                    gv = g.rearrange("p (t n) -> p t n", t=NT)
                    ts(tA, tA, -1.0, None, ALU.mult, None)
                    tt(gv, tAv, each(alog, NT), ALU.mult, step, "g")
                elif kind == "conv":
                    _, gr, part = step
                    cwv = cw.rearrange("p (j t) -> p j t", j=CONV)
                    if part == 0 and gr == 1:
                        dve.wait_ge(*PE(("feat", 0), "kk", 1, 1))
                    for ct in range(4):
                        dve.wait_ge(*fed(step))
                        tile = part * 8 + gr * GH + ct
                        src = L[2 * (part % 2) + ct // 2][:, (ct % 2) * SEQ:(ct % 2 + 1) * SEQ]
                        dst = C[:, part * GH + ct, :]
                        ts(dst, src, cwv[:, 3, tile:tile + 1], None, ALU.mult, None)
                        for back in range(1, CONV):
                            j = CONV - 1 - back
                            name = (step, "taps done") if back == CONV - 1 and ct == 3 else ()
                            stt(dst[:, back:SEQ], src[:, 0:SEQ - back], cwv[:, j, tile:tile + 1], dst[:, back:SEQ], ALU.mult, ALU.add, *name)
                elif kind == "tok":
                    s2v = s2.rearrange("p (t a h) -> p t a h", t=NT, a=2)
                    for part in range(2):
                        for t in range(NT):
                            dve.wait_ge(*AC(step, "sq", part, t))
                            v(V.tensor_reduce(s2v[:, t, part, :], sq[:], AX.X, ALU.add), step, "sum", part, t)
                    ts(s2, s2, EPS, None, ALU.add, None)
                    rsqrt(rq, s2)
                    rqv = rq.rearrange("p (t a h) -> p t a h", t=NT, a=2)
                    ts(rqv[:, :, 0, :], rqv[:, :, 0, :], float(HD) ** -0.5, None, ALU.mult, None, step, "rq")
                elif kind == "moba":
                    _, gr, part = step
                    if part == 2:
                        continue
                    dve.wait_ge(*fed(step))
                    if gr == 1 and part == 0:
                        dve.wait_ge(*PE(("att", 0), "turned", 3))
                    for t in range(NT):
                        src = heads(L[2 - 2 * part + t])
                        dst = mtok[:, part, t]
                        r_ = sqr[:]
                        tt(dst, src, each(cos1[:, t, :], GH), ALU.mult)
                        tt(r_[:, :, 0:64], src[:, :, 64:128], each(sin1[:, t, 0:64], GH), ALU.mult)
                        tt(r_[:, :, 64:128], src[:, :, 0:64], each(sin1[:, t, 64:128], GH), ALU.mult)
                        tt(dst, dst, r_, ALU.add, step, "rope", t)
                elif kind == "tri":
                    gr = step[1]
                    gv = g.rearrange("p (t n) -> p t n", t=NT)[:, :, gr * GH:(gr + 1) * GH]
                    if gr == 1:
                        dve.wait_ge(*PE(("scan", 0), "o", 1))
                    for t in range(NT):
                        tt(trg[:, t], each(tri, GH), over(gv[:, t, :], P), ALU.mult, step, t)
                elif kind == "decay":
                    gcv = gc.rearrange("p (t h) -> p t h", t=NT)
                    dve.wait_ge(*PE(step, "gc"))
                    v(V.tensor_copy(gcv, Q[3][:, 0:16].rearrange("p (t h) -> p t h", t=NT)[:, :, 0:GH]), step, "gc")
                    for t in range(NT):
                        dve.wait_ge(*PE(step, "rows", t))
                        if t == 0:
                            tt(edec, heads(Q[0])[:, :, P - 1], gcv[:, 0, :], ALU.subtract, step, "glast")
                        tt(Dm[:, t], heads(Q[t]), over(gcv[:, t, :], P), ALU.subtract)
                        tt(Dm[:, t], Dm[:, t], each(neg_kq, GH), ALU.add, step, "decay log", t)
                elif kind == "feat":
                    gr = step[1]
                    rqv = rq.rearrange("p (t a h) -> p t a h", t=NT, a=2)
                    bet = beta.rearrange("p (t n) -> p t n", t=NT)[:, :, gr * GH:(gr + 1) * GH]
                    egv = eg.rearrange("p (t h) -> p t h", t=NT)
                    dve.wait_ge(*AC(("tok", gr), "out", 2, 1))
                    dve.wait_ge(*AC(("rates",), "beta"))
                    for t in range(NT):
                        vector_next(V.tensor_tensor(tok[:, t, 1], tok[:, t, 1], over(rqv[:, t, 1, :], HD), ALU.mult), step, "kn", t)
                        vector_next(V.tensor_tensor(tok[:, t, 0], tok[:, t, 0], over(rqv[:, t, 0, :], HD), ALU.mult), step, "qn", t)
                        vector_next(V.tensor_tensor(kb[:, t], tok[:, t, 1], over(bet[:, t, :], HD), ALU.mult), step, "kb", t)
                    dve.wait_ge(*AC(("decay", gr), "edec"))
                    tt(qe[:], tok[:, 1, 0], over(egv[:, 1, :], HD), ALU.mult, step, "qe", 1)
                elif kind == "within":
                    gr = step[1]
                    egv = eg.rearrange("p (t h) -> p t h", t=NT)
                    bet = beta.rearrange("p (t n) -> p t n", t=NT)[:, :, gr * GH:(gr + 1) * GH]
                    for t in range(NT):
                        dve.wait_ge(*AC(("decay", gr), "decay", t))
                        for pair in range(2):
                            dve.wait_ge(*PE(("feat", gr), "kk", t, pair))
                            kk_ = Q[2 * t + pair][:].rearrange("p (i a d) -> p i a d", i=2, a=2)
                            hs = slice(2 * pair, 2 * pair + 2)
                            vector_next(V.tensor_tensor(AT[:, t, hs], kk_[:, :, 0, :], Dm[:, t, hs], ALU.mult))
                            vector_next(V.tensor_tensor(aT[:, t, hs], kk_[:, :, 1, :], Dm[:, t, hs], ALU.mult), ("feat", gr), "attn", t, pair)
                    tt(kbe[:], kb[:, 1], over(egv[:, 1, :], HD), ALU.mult)
                    tt(kdec[:], tok[:, 0, 1], over(edec, HD), ALU.mult)
                    for t in range(NT):
                        tt(tok[:, t, 2], tok[:, t, 2], over(bet[:, t, :], HD), ALU.mult)
                elif kind == "att":
                    gr = step[1]
                    scale = float(HD) ** -0.5
                    dve.wait_ge(*PE(step, "scores", 0))
                    stt(pr[:, :, 0:P], heads(Q[0]), scale, each(neg_qk, GH), ALU.mult, ALU.add)
                    v(V.tensor_reduce(mx[:, 0:GH], pr[:, :, 0:P], AX.X, ALU.max))
                    ts(nm[:, 0:GH], mx[:, 0:GH], -1.0, None, ALU.mult, None, step, "max", 0)
                    for pair in range(2):
                        dve.wait_ge(*PE(step, "scores", 1 + pair))
                        src, hs = heads(Q[1 + pair], 2), slice(2 * pair, 2 * pair + 2)
                        vector_next(V.tensor_scalar(pr[:, hs, P:2 * P], src[:, :, 0:P], scale, None, ALU.mult))
                        vector_next(V.scalar_tensor_tensor(out=pr[:, hs, 2 * P:3 * P], in0=src[:, :, P:SEQ], scalar=scale, in1=each(neg_qk, 2),
                                                           op0=ALU.mult, op1=ALU.add))
                    settle()
                    v(V.tensor_reduce(mx[:, GH:2 * GH], pr[:, :, P:3 * P], AX.X, ALU.max))
                    ts(nm[:, GH:8], mx[:, GH:8], -1.0, None, ALU.mult, None, step, "max", 1)
                    for t, (c0, c1) in enumerate(((0, P), (P, 3 * P))):
                        dve.wait_ge(*AC(step, "exp", t, 3))
                        hs = slice(t * GH, (t + 1) * GH)
                        v(V.reciprocal(ri[:, hs], rs[:, hs]))
                        tt(pr[:, :, c0:c1], pr[:, :, c0:c1], over(ri[:, hs], c1 - c0), ALU.mult, step, "probs", t)
                    for b in range(2):
                        dve.wait_ge(*AC(step, "hi", b))
                        k0 = gr * GH + 2 * b
                        tt(yL[:, k0:k0 + 2, :], heads(Q[3 if b == 0 else 0], 2), yH[:, k0:k0 + 2, :].bitcast(F32), ALU.subtract, step, "lo", b)
                elif kind == "inv":
                    gr = step[1]

                    def mask(l):
                        tt(M[:].rearrange("p t h d -> p (t h) d"), AT[:].rearrange("p t h d -> p (t h) d"), each(square(2 + l), NT * GH),
                           ALU.mult, step, "mask", l)

                    dve.wait_ge(*PE(("att", gr), "out", 1))
                    mask(0)
                    for t in range(NT):
                        vector_next(V.tensor_tensor(TT[:, t], each(ident, GH), M[:, t], ALU.subtract))
                    for t in range(NT):
                        dve.wait_ge(*PE(step, "M0", t))
                        vector_next(V.tensor_tensor(T[:, t], each(ident, GH), heads(Q[t]), ALU.subtract), step, "T", 0, t)
                    mask(1)
                    for l in range(1, LEVELS):
                        if l < LEVELS - 1:
                            dve.wait_ge(*PE(step, "X", l, 1))
                            mask(l + 1)
                        for t in range(NT):
                            dve.wait_ge(*PE(step, "Y", l, t))
                            to, name = (T, "T") if l < LEVELS - 1 else (TT, "TT")
                            tt(to[:, t], to[:, t], heads(Q[t + 2] if l % 2 else Q[t]), ALU.subtract, step, name, l, t)
                elif kind == "scan":
                    gr = step[1]
                    dve.wait_ge(*AC(step, "u", 1))
                    dve.wait_ge(*PE(step, "wS"))
                    tt(vn[:, 1], vn[:, 1], heads(Q[2]), ALU.subtract, step, "vn")
                    for t in range(NT):
                        dve.wait_ge(*AC(step, "sq", t))
                        v(V.tensor_reduce(so[:, t * 8 + gr * GH:t * 8 + (gr + 1) * GH], sq[:], AX.X, ALU.add), step, "sum", t)
                elif kind == "proj_a":
                    dve.wait_ge(*fed(step))
                    dve.wait_ge(*AC(("ga", 1)))
                    for t in range(NT):
                        for c in range(2):
                            gt = gs[:, t, c * 512:(c + 1) * 512]
                            vector_next(V.tensor_tensor(gt, gt, L[2 * t + c][:], ALU.mult), step, "mul", 2 * t + c)
                elif kind == "proj_b":
                    dve.wait_ge(*fed(step))
                    dve.wait_ge(*AC(("gb", 1)))
                    for c in range(2):
                        for t in range(NT):
                            gt, bt = gs[:, t, c * 512:(c + 1) * 512], gsb[:, t, c * 512:(c + 1) * 512]
                            tt(bt, bt, L[2 * t + c][:], ALU.mult)
                            tt(gt, gt, bt, ALU.add, step, "sum", t, c)
                elif kind == "mem":
                    lo_wide(step, mH, mL)
                    dve.wait_ge(*AC(("mem",), "ss", 1))
                    ts(rv[:, 0:2], ss[:, 4:6], 1.0 / D, EPS, ALU.mult, ALU.add)
                    rsqrt(rstd_m, rv[:, 0:2], ("mem",), "rstd")
                elif kind == "yb":
                    ts(so, so, 1.0 / HD, EPS, ALU.mult, ALU.add)
                    rsqrt(rq, so)
                    dve.wait_ge(landed["gnorm"], 16)
                    dve.wait_ge(*AC(("z", 1)))
                    for t in range(NT):
                        ot = o[:, t, :].rearrange("p (h d) -> p h d", h=8)
                        tt(ot, ot, over(rq[:, t * 8:(t + 1) * 8], HD), ALU.mult)
                        tt(ot, ot, each(gnorm, 8), ALU.mult)
                        tt(o[:, t, :], o[:, t, :], z[:, t, :], ALU.mult, step, "y", t)
                    lo_wide(step, uH, uL)
                    dve.wait_ge(landed["mem"], 16)
                    dve.wait_ge(landed["lnm"], 16)
                    dve.wait_ge(*AC(("mem",), "ss", 1))
                    tt(mem[:], mem[:], each(lnm[:], NT), ALU.mult, ("mem",), "scaled")
                elif kind == "p":
                    dve.wait_ge(*AC(step, "hi"))
                    tt(pL[:], heads(Q[3], 2), pH[:].bitcast(F32), ALU.subtract, step, "lo")
                elif kind == "merge":
                    lo_wide(step, uH, uL)
                elif kind == "e":
                    dve.wait_ge(*AC(step, "ss", 1))
                    ts(rv[:, 0:2], ss_p[:, 0:2], 1.0 / D, EPS, ALU.mult, ALU.add)
                    rsqrt(rstd_p, rv[:, 0:2])
                    dve.wait_ge(landed["lnp"], 16)
                    for t in range(NT):
                        for c in range(2):
                            cc = slice(c * 512, (c + 1) * 512)
                            stt(e[:, t, cc], e[:, t, cc], rstd_p[:, t:t + 1], lnp[:, cc], ALU.mult, ALU.mult, step, "e", 2 * t + c)
                elif kind == "norm":
                    what = step[1]
                    post, pre = RES[what]
                    if post:
                        dve.wait_ge(landed["gA_" + what], 16)
                        for b in range(4):
                            dve.wait_ge(*AC(step, "ss", b))
                            if b < 3:
                                gained(b)
                        v(V.scalar_tensor_tensor(out=rv[:, 0:2], in0=ss[:, 0:4:2], scalar=EPS, in1=ss[:, 1:4:2], op0=ALU.add, op1=ALU.add))
                        rsqrt(rstd_o, rv[:, 0:2])
                    if what == "mix":
                        dve.wait_ge(landed["xres"], 16)
                    if pre:
                        dve.wait_ge(landed["gB_" + what], 16)
                    for part in range(2 if what in LATE else len(PARTS[what])):
                        norm_part(what, part)
                        if part == 0 and post and what not in LATE:
                            gained(3)
                elif kind == "next":
                    for j in range(4):
                        lo_wide(step, uH, uL, (j,))
                        if step[1] in LATE and j < 2:
                            if j == 0:
                                gained(3)
                            norm_part(step[1], j + 2)
                    if step[1] != "ffn1":
                        dve.wait_ge(*AC(step, "hss", 1))
                        ts(rv[:, 0:2], ss[:, 4:6], 1.0 / D, EPS, ALU.mult, ALU.add)
                        rsqrt(rstd_h, rv[:, 0:2], step, "rstd")
                elif kind == "ffn":
                    _, blk, c = step
                    n = 512 if c < 5 else 256

                    def low(c_, j):
                        prev = ("ffn", blk, c_)
                        dve.wait_ge(*AC(prev, "hi", j))
                        k0 = 4 * c_ + 2 * j
                        tt(hL[:, k0:k0 + 2, :], heads(Q[2 * ((c_ + 1) % 2) + j], 2), hH[:, k0:k0 + 2, :].bitcast(F32), ALU.subtract, prev, "lo", j)

                    if c > 0:
                        low(c - 1, 0)
                        low(c - 1, 1)
                    dve.wait_ge(*fed(step))
                    for t in range(NT):
                        dve.wait_ge(*AC(step, "silu", t))
                        stt(hm[:, t, 0:n], L[2 * t + 1][:, 0:n], rstd_h[:, t:t + 1], sil[:, t, 0:n], ALU.mult, ALU.mult, step, "hidden", t)
                    if c == 5:
                        low(5, 0)
                elif kind == "angles":
                    dve.wait_ge(landed["pos"], 16)
                    ang3 = ang.rearrange("p (t n) -> p t n", t=NT)
                    v(V.tensor_copy(posf, pos_i[:]))
                    tt(ang3, over(posf, ROPE2), each(inv2, NT), ALU.mult)
                    ts(kk, ang, 1.0 / (2 * np.pi), MAGIC, ALU.mult, ALU.add)
                    ts(kk, kk, MAGIC, None, ALU.subtract, None)
                    stt(sn, kk, -TWO_PI[0], ang, ALU.mult, ALU.add)
                    stt(sn, kk, -TWO_PI[1], sn, ALU.mult, ALU.add)
                    stt(sn, kk, -TWO_PI[2], sn, ALU.mult, ALU.add)
                    ts(cs, sn, float(np.pi / 2), None, ALU.add, None)
                    ts(kk, cs, float(np.pi), -2 * float(np.pi), ALU.is_gt, ALU.mult)
                    tt(cs, cs, kk, ALU.add)
                    ts(sn, sn, 3.1415925, -3.1415925, ALU.min, ALU.max)
                    ts(cs, cs, 3.1415925, -3.1415925, ALU.min, ALU.max, step, "angles")
                    dve.wait_ge(landed["gsub"], 16)
                    ts(gsub[:], gsub[:], 1.0 - LAM_INIT, None, ALU.mult, None)
                    dve.wait_ge(landed["lamv"], 64)
                    for n in range(2):
                        tt(lamv[:, 2 * n, :], lamv[:, 2 * n, :], lamv[:, 2 * n + 1, :], ALU.mult)
                        v(V.tensor_reduce(lam[:, n:n + 1], lamv[:, 2 * n, :], AX.X, ALU.add), *((step, "lam sums") if n else ()))
                elif kind == "rope2":
                    dve.wait_ge(*AC(("in2", 1), 1))
                    dve.wait_ge(*AC(("angles",), "cos"))
                    sn3, cs3 = (q_.rearrange("p (t n) -> p t n", t=NT) for q_ in (sn, cs))
                    for t in range(NT):
                        x_ = qk2[:, t].rearrange("p a h d -> p (a h) d")
                        x1, x2 = x_[:, :, 0:ROPE2], x_[:, :, ROPE2:2 * ROPE2]
                        c_, s_ = each(cs3[:, t, :], 4 * GH), each(sn3[:, t, :], 4 * GH)
                        q4 = [r2t[n][:].rearrange("p (h d) -> p h d", d=ROPE2) for n in range(4)]
                        tt(q4[0], x1, c_, ALU.mult)
                        tt(q4[1], x2, s_, ALU.mult)
                        tt(q4[2], x2, c_, ALU.mult)
                        tt(q4[3], x1, s_, ALU.mult)
                        tt(x1, q4[0], q4[1], ALU.subtract)
                        tt(x2, q4[2], q4[3], ALU.add, *((step, "rope") if t else ()))
                elif kind == "diff":
                    banks = [[Q[0], Q[1], Q[2]], [Q[3], L[0], L[1]]]
                    for m in range(2):
                        p_ = pd[m]
                        dve.wait_ge(*PE(step, "scores", m, 0))
                        stt(p_[:, :, 0:P], heads(banks[m][0]), 0.125, each(neg_qk, GH), ALU.mult, ALU.add)
                        v(V.tensor_reduce(mx[:, 8 * m:8 * m + GH], p_[:, :, 0:P], AX.X, ALU.max))
                        ts(nm[:, 8 * m:8 * m + GH], mx[:, 8 * m:8 * m + GH], -1.0, None, ALU.mult, None, step, "first max", m)
                        for pair in range(2):
                            dve.wait_ge(*PE(step, "scores", m, 1 + pair))
                            src, hs = heads(banks[m][1 + pair], 2), slice(2 * pair, 2 * pair + 2)
                            ts(p_[:, hs, P:2 * P], src[:, :, 0:P], 0.125, None, ALU.mult, None)
                            stt(p_[:, hs, 2 * P:3 * P], src[:, :, P:SEQ], 0.125, each(neg_qk, 2), ALU.mult, ALU.add)
                        if m == 1:
                            dve.wait_ge(*PE(("pool",), "scale"))
                            v(V.tensor_copy(psc, Q[2][:, 0:4]), ("pool",), "scale")
                        v(V.tensor_reduce(mx[:, 8 * m + GH:8 * m + 8], p_[:, :, P:3 * P], AX.X, ALU.max))
                        ts(nm[:, 8 * m + GH:8 * m + 8], mx[:, 8 * m + GH:8 * m + 8], -1.0, None, ALU.mult, None, step, "max", m)
                    dve.wait_ge(*AC(("angles",), "lam"))
                    tt(lam[:, 2:3], lam[:, 0:1], lam[:, 1:2], ALU.subtract)
                    ts(lam[:, 2:3], lam[:, 2:3], LAM_INIT, None, ALU.add, None)
                elif kind == "pool":
                    scaled_probs(0, 0)
                    for gi in range(4):
                        dve.wait_ge(*AC(step, "hi", gi | 1))
                        stt(uL[:, 4 + gi, :], Q[gi // 2][:, (gi % 2) * SEQ:(gi % 2 + 1) * SEQ], psc[:, gi:gi + 1], uH[:, 4 + gi, :].bitcast(F32),
                            ALU.mult, ALU.subtract, step, "lo", gi)
                elif kind == "probs":
                    scaled_probs(0, 1)
                    for t in range(NT):
                        scaled_probs(1, t)
                    for t in range(NT):
                        dve.wait_ge(*AC(step, "sq", t))
                        v(V.tensor_reduce(mx[:, t * GH:(t + 1) * GH], dsq[:], AX.X, ALU.add), step, "sum", t)
                elif kind == "dnorm":
                    ts(rv[:, 0:8], mx[:, 0:8], 1.0 / HD, EPS, ALU.mult, ALU.add)
                    rsqrt(r1, rv[:, 0:8])
                    for j in range(2):
                        for t in range(NT):
                            for i in (2 * j, 2 * j + 1):
                                n_ = t * GH + i
                                vector_next(V.scalar_tensor_tensor(out=da[:, t, i, :], in0=da[:, t, i, :], scalar=r1[:, n_:n_ + 1], in1=gsub[:],
                                                                   op0=ALU.mult, op1=ALU.mult), step, "da", n_)
                    for j in range(2):
                        dve.wait_ge(*AC(step, "hi", j))
                        tt(uL[:, 2 * j:2 * j + 2, :], heads(Q[2 + j], 2), uH[:, 2 * j:2 * j + 2, :].bitcast(F32), ALU.subtract, step, "lo", j)
                elif kind == "cross":
                    for j in (0, 2):
                        dve.wait_ge(*PE(step, "turned", j))
                        v(V.tensor_copy(cqT[:, 2 * j:2 * j + 2, :], heads(Q[j], 2)), step, "heads", j)
                    for t in range(NT):
                        hs = slice(t * GH, (t + 1) * GH)
                        for pair in range(2):
                            dve.wait_ge(*PE(step, "scores", t, pair))
                            n_ = t * GH + 2 * pair
                            v(V.tensor_reduce(mx[:, n_:n_ + 2], heads(L[2 * t + pair], 2), AX.X, ALU.max))
                        ts(nm[:, hs], mx[:, hs], -1.0 / 16, None, ALU.mult, None, step, "max", t)
                        dve.wait_ge(*AC(step, "exp", t, 3))
                        v(V.reciprocal(ri[:, hs], rs[:, hs]))
                        for j in range(2):
                            half = cp[:, t, :, j * P:(j + 1) * P]
                            vector_next(V.tensor_tensor(half, half, over(ri[:, hs], P), ALU.mult), step, "probs", t, j)
                    for t in range(NT):
                        for c in range(2):
                            dve.wait_ge(*AC(step, "hi", t, c))
                            vector_next(V.tensor_tensor(uL[:, 4 * c:4 * c + 4, t * P:(t + 1) * P], heads(Q[2 * t + c]),
                                                        uH[:, 4 * c:4 * c + 4, t * P:(t + 1) * P].bitcast(F32), ALU.subtract), step, "lo", t, c)

    return {"pe": PE.names, "act": AC.names, "dve": VE.names}


_INS = ["x", "p", "ln_pre_mix", "w_in", "conv_w", "a_log", "dt_bias", "gdn_norm", "w_proj_a", "w_proj_b", "w_out",
        "ln_post_mix", "ln_pre_ffn", "w_ffn_gate", "w_ffn_up", "w_ffn_down", "ln_post_ffn", "w_ple", "ln_ple", "w_ple_gate",
        "mem_2", "positions_2", "g_mix_pre_2", "w_in_2", "lambda_q1_2", "lambda_k1_2", "lambda_q2_2", "lambda_k2_2",
        "g_subln_2", "w_pool_2", "pool_scale_2", "w_out_2", "g_mix_post_2", "g_x_pre_2", "g_mem_2", "w_xq_2", "w_xkv_2",
        "w_xo_2", "g_x_post_2", "g_ffn_pre_2", "w_gate_2", "w_up_2", "w_down_2", "g_ffn_post_2"]


def kernel(**inputs):
    import concourse.bacc as bacc
    from concourse.bass_utils import run_bass_kernel_spmd

    arrays = {f"in_{n}": np.ascontiguousarray(inputs[n]) for n in _INS}
    arrays["in_table"], arrays["in_pool_table"] = constant_tables()

    def program(known):
        nc = bacc.Bacc("TRN2", target_bir_lowering=False, num_devices=1)
        a = {k[3:]: nc.dram_tensor(k, v.shape, mybir.dt.from_np(v.dtype), kind="ExternalInput").ap() for k, v in arrays.items()}
        out = nc.dram_tensor("out", (1, SEQ, D), F32, kind="ExternalOutput").ap()
        return nc, build(nc, a, out, known)

    _, known = program({})
    nc, _ = program(known)
    r = run_bass_kernel_spmd(nc, [arrays], core_ids=[0])
    return r.results[0]["out"]
```
